# Optimizing a Trainium2 kernel written in Bass

```python
import math
import jax, jax.numpy as jnp
from jax import lax
import numpy as np

D_MODEL = 1024
BATCH = 1
SEQ = 512
DEPTH = 1

D_A = D_MODEL
CONV_A_WIDTH = 3
D_R = (D_MODEL * 5) // 4
N_RG_BLOCKS = 10
RG_BLOCK = D_R // N_RG_BLOCKS
CONV_R_WIDTH = 4
RG_C = 8.0
SPLITS = (D_A, 2 * D_A, 3 * D_A, 3 * D_A + D_R, 3 * D_A + 2 * D_R, 3 * D_A + 2 * D_R + D_MODEL)
D_IN = 3 * D_A + 2 * D_R + 2 * D_MODEL
N_EXPERTS = 16
N_GROUPS = 4
EXPERTS_PER_GROUP = N_EXPERTS // N_GROUPS
TOP_K = 2
D_FF_EXPERT = D_MODEL // 2
DN_ALPHA = (2.0 * DEPTH) ** 0.25
DN_BETA = (8.0 * DEPTH) ** -0.25
LN_EPS = 1e-5

kernel_name = 'hybrid_conv_rglru_grouped_moe_deepnorm'

def layer_norm(x, g, b):
    xf = x.astype(jnp.float32)
    mu = jnp.mean(xf, axis=-1, keepdims=True)
    var = jnp.mean(jnp.square(xf - mu), axis=-1, keepdims=True)
    return ((xf - mu) * lax.rsqrt(var + LN_EPS) * g.astype(jnp.float32) + b.astype(jnp.float32)).astype(x.dtype)

def causal_dwconv(u, w):
    k_width = w.shape[0]
    s = u.shape[1]
    up = jnp.pad(u, ((0, 0), (k_width - 1, 0), (0, 0)))
    y = up[:, 0:s] * w[0]
    for k in range(1, k_width):
        y = y + up[:, k:k + s] * w[k]
    return y

def linear_recurrence(a, b):
    def combine(left, right):
        a_l, b_l = left
        a_r, b_r = right
        return a_r * a_l, a_r * b_l + b_r
    _, h = lax.associative_scan(combine, (a, b), axis=1)
    return h

def block_diag(u, w, bias):
    bsz, s, _ = u.shape
    ub = u.reshape(bsz, s, N_RG_BLOCKS, RG_BLOCK)
    return (jnp.einsum('bshi,hij->bshj', ub, w) + bias).reshape(bsz, s, D_R)

def shared_group_router(xt, w_router, b_router):
    logits = xt.astype(jnp.float32) @ w_router.astype(jnp.float32) + b_router.astype(jnp.float32)
    probs = jax.nn.softmax(logits, axis=-1)
    probs_g = probs.reshape(-1, N_GROUPS, EXPERTS_PER_GROUP)
    group_score = jnp.sum(lax.top_k(probs_g, TOP_K)[0], axis=-1)
    g_sel = jnp.argmax(group_score, axis=-1)
    in_group = jnp.take_along_axis(probs_g, g_sel[:, None, None], axis=1)[:, 0]
    vals, local = lax.top_k(in_group, TOP_K)
    vals = vals / jnp.sum(vals, axis=-1, keepdims=True)
    idx = g_sel[:, None] * EXPERTS_PER_GROUP + local
    return jnp.sum(jax.nn.one_hot(idx, N_EXPERTS, dtype=jnp.float32) * vals[..., None], axis=1)

def grouped_moe(x, w_router, b_router, w_gate, w_up, w_down):
    bsz, s, d = x.shape
    xt = x.reshape(bsz * s, d)
    gates = shared_group_router(xt, w_router, b_router).astype(x.dtype)
    out = jnp.zeros_like(xt)
    for e in range(N_EXPERTS):
        h = jax.nn.silu(xt @ w_gate[e]) * (xt @ w_up[e])
        out = out + gates[:, e:e + 1] * (h @ w_down[e])
    return out.reshape(bsz, s, d)

def setup_inputs(seed: int = 0) -> dict:
    key = jax.random.key(seed)
    ks = jax.random.split(key, 24)

    def nrm(k, shape, scale):
        return jax.random.normal(k, shape, jnp.float32) * scale

    u = jax.random.uniform(ks[10], (DEPTH, D_R), jnp.float32, minval=0.9, maxval=0.999)
    p = u ** (1.0 / RG_C)
    rg_lambda = jnp.log(p) - jnp.log1p(-p)
    return {
        'x': nrm(ks[0], (BATCH, SEQ, D_MODEL), 1.0),
        'w_in': nrm(ks[1], (DEPTH, D_MODEL, D_IN), D_MODEL ** -0.5),
        'conv_a_w': nrm(ks[2], (DEPTH, CONV_A_WIDTH, D_A), CONV_A_WIDTH ** -0.5),
        'w_branch_a': nrm(ks[3], (DEPTH, D_A, D_MODEL), DN_BETA * D_A ** -0.5),
        'conv_r_w': nrm(ks[4], (DEPTH, CONV_R_WIDTH, D_R), CONV_R_WIDTH ** -0.5),
        'conv_r_b': nrm(ks[5], (DEPTH, D_R), 0.01),
        'w_rg_a': nrm(ks[6], (DEPTH, N_RG_BLOCKS, RG_BLOCK, RG_BLOCK), RG_BLOCK ** -0.5),
        'b_rg_a': nrm(ks[7], (DEPTH, N_RG_BLOCKS, RG_BLOCK), 0.01),
        'w_rg_x': nrm(ks[8], (DEPTH, N_RG_BLOCKS, RG_BLOCK, RG_BLOCK), RG_BLOCK ** -0.5),
        'b_rg_x': nrm(ks[9], (DEPTH, N_RG_BLOCKS, RG_BLOCK), 0.01),
        'rg_lambda': rg_lambda,
        'w_branch_r': nrm(ks[11], (DEPTH, D_R, D_MODEL), DN_BETA * D_R ** -0.5),
        'w_out': nrm(ks[12], (DEPTH, D_MODEL, D_MODEL), DN_BETA * D_MODEL ** -0.5),
        'ln1_g': 1.0 + nrm(ks[13], (DEPTH, D_MODEL), 0.02),
        'ln1_b': nrm(ks[14], (DEPTH, D_MODEL), 0.02),
        'w_router': nrm(ks[15], (D_MODEL, N_EXPERTS), D_MODEL ** -0.5),
        'b_router': nrm(ks[16], (N_EXPERTS,), 0.01),
        'w_exp_gate': nrm(ks[17], (DEPTH, N_EXPERTS, D_MODEL, D_FF_EXPERT), D_MODEL ** -0.5),
        'w_exp_up': nrm(ks[18], (DEPTH, N_EXPERTS, D_MODEL, D_FF_EXPERT), D_MODEL ** -0.5),
        'w_exp_down': nrm(ks[19], (DEPTH, N_EXPERTS, D_FF_EXPERT, D_MODEL), DN_BETA * D_FF_EXPERT ** -0.5),
        'ln2_g': 1.0 + nrm(ks[20], (DEPTH, D_MODEL), 0.02),
        'ln2_b': nrm(ks[21], (DEPTH, D_MODEL), 0.02),
    }

def reference(x, w_in, conv_a_w, w_branch_a, conv_r_w, conv_r_b, w_rg_a, b_rg_a, w_rg_x, b_rg_x,
              rg_lambda, w_branch_r, w_out, ln1_g, ln1_b, w_router, b_router,
              w_exp_gate, w_exp_up, w_exp_down, ln2_g, ln2_b):
    for l in range(DEPTH):
        z = x @ w_in[l]
        h_a, b_a, c_a, x_r, y_r, g_a, g_r = jnp.split(z, SPLITS, axis=-1)
        ya = (b_a * causal_dwconv(c_a * h_a, conv_a_w[l])) @ w_branch_a[l]
        xc = causal_dwconv(x_r, conv_r_w[l]) + conv_r_b[l]
        r_gate = jax.nn.sigmoid(block_diag(xc, w_rg_a[l], b_rg_a[l]))
        i_gate = jax.nn.sigmoid(block_diag(xc, w_rg_x[l], b_rg_x[l]))
        log_a = -RG_C * r_gate.astype(jnp.float32) * jax.nn.softplus(-rg_lambda[l].astype(jnp.float32))
        a_t = jnp.exp(log_a)
        b_t = jnp.sqrt(-jnp.expm1(2.0 * log_a)) * (i_gate * xc).astype(jnp.float32)
        h_r = linear_recurrence(a_t, b_t).astype(x.dtype)
        yr = (h_r * jax.nn.gelu(y_r)) @ w_branch_r[l]
        merged = jax.nn.sigmoid(g_a) * ya + jax.nn.sigmoid(g_r) * yr
        x = layer_norm(DN_ALPHA * x + merged @ w_out[l], ln1_g[l], ln1_b[l])
        moe = grouped_moe(x, w_router, b_router, w_exp_gate[l], w_exp_up[l], w_exp_down[l])
        x = layer_norm(DN_ALPHA * x + moe, ln2_g[l], ln2_b[l])
    return x


_drawn_inputs = setup_inputs


def setup_inputs(seed=0):
    import zlib

    import numpy as np

    out = dict(_drawn_inputs(seed))
    spreads = {}
    factors = {'b_rg_a': 84.043, 'b_rg_x': 32.393, 'ln2_g': 25.722, 'ln2_b': 23.947, 'conv_r_b': 2.717}
    for name, (base, spread) in spreads.items():
        noise = np.random.default_rng([zlib.crc32(name.encode()), seed]).standard_normal(out[name].shape)
        drawn = base * np.exp(spread * noise) if base else spread * noise
        out[name] = __import__('jax').numpy.asarray(drawn.astype(out[name].dtype))
    for name, factor in factors.items():
        out[name] = (out[name] * factor).astype(out[name].dtype)
    return out
```

```python
from contextlib import ExitStack

import concourse.bass as bass
from concourse import mybir

P = 128
F32 = mybir.dt.float32
F32R = mybir.dt.float32r
I32 = mybir.dt.int32
U32 = mybir.dt.uint32
ACT = mybir.ActivationFunctionType
ALU = mybir.AluOpType
AX = mybir.AxisListType.X
ds = bass.ds
KIB = 1024
LN_EPS = 1e-5
GELU_A = 0.044715
GELU_S = 2.0 * 0.7978845608028654


class Chain:

    def __init__(self, eng, sem):
        self.eng, self.sem, self.n = eng, sem, 0

    def link(self, ins):
        ins.then_inc(self.sem, 1)
        self.n = self.n + 1
        self.eng.wait_ge(self.sem, self.n)

    def loop(self, trips, body, per):
        start = self.n
        with self.eng.Fori(0, trips) as i:
            self.n = i * per + start
            body(i)
        self.n = start + trips * per


def trunk_moe(nc, x, w_in, conv_a_w, w_branch_a, conv_r_w, conv_r_b, w_rg_a, b_rg_a, w_rg_x, b_rg_x,
              rg_lambda, w_branch_r, w_out, ln1_g, ln1_b, w_router, b_router,
              w_exp_gate, w_exp_up, w_exp_down, ln2_g, ln2_b, out):
    _, S, D = x.shape
    DR = conv_r_b.shape[1]
    NE, DF = w_exp_gate.shape[1], w_exp_gate.shape[3]
    GRP = 4
    NG = NE // GRP
    KD, KR, KF = D // P, DR // P, DF // P
    TT = S // P
    ALPHA = 2.0 ** 0.25
    BLOCKS = NE + (2 * S - 1) // (P + 1)
    ZEROS = 16 * (2 * BLOCKS - NE)
    assert (S, D, DR, NE, DF) == (512, 1024, 1280, 16, 512)

    COL_H, COL_B, COL_C = 0, D, 2 * D
    COL_XR, COL_YR = 3 * D, 3 * D + DR
    COL_GA, COL_GR = 3 * D + 2 * DR, 4 * D + 2 * DR

    N_XR = 0
    N_A = N_XR + KR
    N_BA = N_A + 3 * KD
    N_YR = N_BA + KD
    N_GA = N_YR + KR
    N_GR = N_GA + KD
    N_BR = N_GR + KD
    N_O = N_BR + KD
    N_END = N_O + KD

    x2 = x.rearrange("a s d -> (a s) d")
    out2 = out.rearrange("a s d -> (a s) d")
    win_v = w_in[0].rearrange("(k p) n -> p k n", p=P)
    wba_v = w_branch_a[0].rearrange("(k p) n -> p k n", p=P)
    wbr_v = w_branch_r[0].rearrange("(k p) n -> p k n", p=P)
    wout_v = w_out[0].rearrange("(k p) n -> p k n", p=P)

    xs = nc.dram_tensor("xs", (BLOCKS * P, D), F32, kind="Internal").ap()
    ys = nc.dram_tensor("ys", (BLOCKS * P, D), F32, kind="Internal").ap()

    with ExitStack() as ctx:
        base = (nc.sbuf_base + 31) // 32 * 32

        def at(name, kib, shape, dt=F32):
            return nc.alloc_sbuf_tensor_at(name, shape, dt, offset=base + int(kib * KIB))

        def sem(name):
            return ctx.enter_context(nc.semaphore(name))

        zbuf = at("zbuf", 0, [P, KR, S])
        tbuf = at("tbuf", 20, [P, KR, S])
        ibuf = at("ibuf", 40, [P, KR, S])
        hg_hi = at("hg_hi", 20, [P, KR, S], F32R)
        hg_lo = at("hg_lo", 40, [P, KR, S], F32R)
        u_hi = at("u_hi", 60, [P, KD, S], F32R)
        u_lo = at("u_lo", 76, [P, KD, S], F32R)
        sgr = at("sgr", 60, [P, KD, S])
        ya = at("ya", 92, [P, KD, S])
        zero = at("zero", 92, [P, D])
        rg_st = [at(f"rg_st{p}", 96 + p, [P, 2, P]) for p in range(2)]
        rg_hi = [at(f"rg_hi{p}", 98 + p, [P, 2, P], F32R) for p in range(2)]
        rg_lo = [at(f"rg_lo{p}", 100 + p, [P, 2, P], F32R) for p in range(2)]
        rows = at("rows", 102, [P, P])
        wst = [at(f"wst{p}", 108 + 5 * p, [P, KR, P]) for p in range(2)]
        whi = [at(f"whi{p}", 118 + 5 * p, [P, KR, P], F32R) for p in range(2)]
        wlo = [at(f"wlo{p}", 128 + 5 * p, [P, KR, P], F32R) for p in range(2)]
        xT_hi = at("xT_hi", 138, [P, KD, S], F32R)
        xT_lo = at("xT_lo", 154, [P, KD, S], F32R)
        mg_hi = at("mg_hi", 138, [P, KD, S], F32R)
        mg_lo = at("mg_lo", 154, [P, KD, S], F32R)
        tmp = [at(f"tmp{i}", 170 + 2 * i, [P, S]) for i in range(8)]
        xc = [tmp[0], tmp[1]]
        xc_hi = at("xc_hi", 174, [P, S], F32R)
        xc_lo = at("xc_lo", 176, [P, S], F32R)
        ig = [tmp[4], tmp[5]]
        yT = at("yT", 170, [P, KD, S])
        x1 = at("x1", 186, [P, TT, D])
        ident = at("ident", 202, [P, P])
        before = at("before", 202.5, [P, P])
        ones = at("ones", 203, [P, P])
        chan = at("chan", 203.5, [P, P])
        wr = at("wr", 204, [P, KD, NE])
        decay = at("decay", 204.5, [P, 8, KR])
        brow = at("brow", 204.875, [P, NE])
        iota_e = at("iota_e", 204.9375, [P, NE])
        stat = at("stat", 205, [P, 32])
        gates = at("gates", 205.125, [P, 2, TT])
        dest = at("dest", 205.1875, [P, 2, TT], U32)
        plan = at("plan", 205.25, [P, 8], I32)
        r16 = [at(f"r16_{i}", 154 + 0.25 * i, [P, TT, NE]) for i in range(20)]
        r4 = [at(f"r4_{i}", 159.5 + 0.0625 * i, [P, TT, NG]) for i in range(8)]
        r1 = [at(f"r1_{i}", 160 + 0.015625 * 2 * i, [P, TT]) for i in range(16)]
        x1T = at("x1T", 138, [P, TT, KD, P])
        ln1_gb = at("ln1_gb", 40, [P, 2, D])
        est = [at(f"est{s}", 8 * s, [P, 4, DF]) for s in range(6)]
        ehi = [at(f"ehi{s}", o, [P, 4, DF], F32R) for s, o in enumerate([48, 56, 64, 72, 108, 170])]
        elo = [at(f"elo{s}", o, [P, 4, DF], F32R) for s, o in enumerate([80, 88, 96, 116, 124, 178])]
        xe = at("xe", 138, [P, D])
        xe_hi = at("xe_hi", 142, [P, KD, P], F32R)
        xe_lo = at("xe_lo", 146, [P, KD, P], F32R)
        sg = at("sg", 150, [P, DF])
        hb = at("hb", 152, [P, DF])
        hT_hi = at("hT_hi", 154, [P, KF, P], F32R)
        hT_lo = at("hT_lo", 156, [P, KF, P], F32R)
        yb = at("yb", 158, [P, D])
        ln2_gb = at("ln2_gb", 162, [P, 2, D])
        yg = at("yg", 0, [P, 2, TT, D])

        psA = [ctx.enter_context(nc.psum_tensor(f"psA{i}", [P, S], F32)) for i in range(2)]
        psB = [ctx.enter_context(nc.psum_tensor(f"psB{i}", [P, S], F32)) for i in range(2)]
        psC = [ctx.enter_context(nc.psum_tensor(f"psC{i}", [P, 2, S], F32)) for i in range(2)]
        ps6 = [psB[0][:], psB[1][:], psC[0][:, 0, :], psC[0][:, 1, :], psC[1][:, 0, :], psC[1][:, 1, :]]

        x_landed = sem("x_landed")
        sp_step = sem("sp_step")
        rows_landed = sem("rows_landed")
        small_landed = sem("small_landed")
        masks = sem("masks")
        pool_step = sem("pool_step")
        chan_t = sem("chan_t")
        chan_ready = sem("chan_ready")
        decay_act = sem("decay_act")
        decay_dve = sem("decay_dve")
        xt_t = sem("xt_t")
        xt_hi = sem("xt_hi")
        xt_lo = sem("xt_lo")
        w_landed = [sem(f"w_landed{p}") for p in range(2)]
        w_hi = sem("w_hi")
        w_lo = sem("w_lo")
        tile_done = sem("tile_done")
        rg_landed = [sem(f"rg_landed{p}") for p in range(2)]
        rgw_hi = sem("rgw_hi")
        rgw_lo = sem("rgw_lo")
        xc_start = sem("xc_start")
        xc_done = sem("xc_done")
        xc_h = sem("xc_h")
        xc_l = sem("xc_l")
        rg_done = sem("rg_done")
        gate_done = sem("gate_done")
        ix_done = sem("ix_done")
        c_read = sem("c_read")
        v_done = sem("v_done")
        t_start = sem("t_start")
        u_done = sem("u_done")
        u_h = sem("u_h")
        u_l = sem("u_l")
        a_done = sem("a_done")
        sq_done = sem("sq_done")
        bt_done = sem("bt_done")
        ya_done = sem("ya_done")
        y_sq = sem("y_sq")
        y_q = sem("y_q")
        y_sig = sem("y_sig")
        hg_done = sem("hg_done")
        hg_h = sem("hg_h")
        hg_l = sem("hg_l")
        ga_read = sem("ga_read")
        m_done = sem("m_done")
        gr_read = sem("gr_read")
        mf_done = sem("mf_done")
        mg_h = sem("mg_h")
        mg_l = sem("mg_l")
        yT_done = sem("yT_done")
        ln1_landed = sem("ln1_landed")
        y_t = sem("y_t")
        res_done = sem("res_done")
        var_done = sem("var_done")
        std_done = sem("std_done")
        x1_done = sem("x1_done")
        x1_t = sem("x1_t")
        x1T_done = sem("x1T_done")
        logit_done = sem("logit_done")
        lmax_done = sem("lmax_done")
        exp_done = sem("exp_done")
        sel_done = sem("sel_done")
        pos_done = sem("pos_done")
        dest_done = sem("dest_done")
        zero_done = sem("zero_done")
        scat = sem("scat")
        dve_step = sem("dve_step")
        e_landed = [sem(f"e_landed{s}") for s in range(6)]
        gu_hi = sem("gu_hi")
        gu_lo = sem("gu_lo")
        gu_used = sem("gu_used")
        d_hi = sem("d_hi")
        d_lo = sem("d_lo")
        d_used = sem("d_used")
        xe_landed = sem("xe_landed")
        xe_t = sem("xe_t")
        xe_h = sem("xe_h")
        xe_l = sem("xe_l")
        silu_done = sem("silu_done")
        h_done = sem("h_done")
        h_t = sem("h_t")
        h_h = sem("h_h")
        h_l = sem("h_l")
        y_evac = sem("y_evac")
        y_stored = sem("y_stored")
        all_stored = sem("all_stored")
        ln2_landed = sem("ln2_landed")
        got = [sem(f"got{t}") for t in range(TT)]
        out_ready = sem("out_ready")
        stored = sem("stored")

        C_CA = lambda k, j: k * KD + j
        C_CR = lambda k, j: 3 * KD + k * KR + j
        C_CB = 3 * KD + 4 * KR
        C_BA, C_BX, C_LAM = C_CB + KR, C_CB + 2 * KR, C_CB + 3 * KR
        NROW = C_LAM + KR

        block = ctx.enter_context(nc.Block())

        def load_expert(sp, b, s, expert=None, again=False):
            if again or b > 0:
                if s < 4:
                    sp.wait_ge(gu_lo, b * 4 + (s - 3))
                else:
                    sp.wait_ge(d_lo, b * 2 + (s - 5))
            if expert is not None:
                sp.wait_ge(gu_lo, 4 * NE)
            e = b if expert is None else expert
            w = (w_exp_gate, w_exp_up, w_exp_down)[s // 2]
            w = w[0, e] if isinstance(e, int) else w[0, ds(e, 1)].rearrange("a k n -> (a k) n")
            if s < 4:
                src = w.rearrange("(k p) n -> p k n", p=P)[:, 4 * (s % 2):4 * (s % 2) + 4, :]
            else:
                src = w.rearrange("(k p) n -> p k n", p=P)[:, :, (s - 4) * DF:(s - 3) * DF]
            sp.dma_start(est[s][:], src).then_inc(e_landed[s], 16)

        @block.sync
        def _(sp):
            for t in range(TT):
                sp.dma_start(x1[:, t, :], x2[t * P:(t + 1) * P, :]).then_inc(x_landed, 16)

            def load(N, p, src, K=KD):
                if not (isinstance(N, int) and N < 2):
                    sp.wait_ge(w_lo, N - 1)
                    sp.sem_inc(sp_step, 1)
                sp.dma_start(wst[p][:, 0:K, :], src).then_inc(w_landed[p], 16)

            def part(view, c0, j):
                if isinstance(j, int):
                    return view[:, :, c0 + j * P:c0 + (j + 1) * P]
                return view[:, :, ds(j * P + c0, P)]

            def load_rg(j, p):
                if not (isinstance(j, int) and j < 2):
                    sp.wait_ge(rgw_lo, j - 1)
                wa = w_rg_a[0, j] if isinstance(j, int) else w_rg_a[0, ds(j, 1)].rearrange("a i o -> (a i) o")
                wx = w_rg_x[0, j] if isinstance(j, int) else w_rg_x[0, ds(j, 1)].rearrange("a i o -> (a i) o")
                sp.dma_start(rg_st[p][:, 0, :], wa).then_inc(rg_landed[p], 16)
                sp.dma_start(rg_st[p][:, 1, :], wx).then_inc(rg_landed[p], 16)

            load(0, 0, part(win_v, COL_XR, 0))
            r = 0
            for src, n in ((conv_a_w[0].rearrange("k (j c) -> (k j) c", c=P), 3 * KD),
                           (conv_r_w[0].rearrange("k (j c) -> (k j) c", c=P), 4 * KR),
                           (conv_r_b[0].rearrange("(j c) -> j c", c=P), KR),
                           (b_rg_a[0], KR), (b_rg_x[0], KR),
                           (rg_lambda[0].rearrange("(j c) -> j c", c=P), KR)):
                sp.dma_start(rows[r:r + n, :], src).then_inc(rows_landed, 16)
                r += n
            load(1, 1, part(win_v, COL_XR, 1))
            load_rg(0, 0)
            load_rg(1, 1)
            sp.dma_start(wr[:], w_router.rearrange("(k p) e -> p k e", p=P)).then_inc(small_landed, 16)
            sp.dma_start(brow[:], b_router.rearrange("(a e) -> a e", a=1).to_broadcast([P, NE])
                         ).then_inc(small_landed, 16)
            with sp.Fori(1, KR // 2) as i:
                for p in range(2):
                    load(2 * i + p, p, part(win_v, COL_XR, 2 * i + p))
                    load_rg(2 * i + p, p)
            with sp.Fori(0, KD // 2) as i:
                for m in range(6):
                    c0 = (COL_C, COL_H, COL_B)[m % 3]
                    load(6 * i + (N_A + m), m % 2, part(win_v, c0, 2 * i + m // 3))
            for N0, view, c0, trips in ((N_BA, wba_v, 0, KD), (N_YR, win_v, COL_YR, KR),
                                        (N_GA, win_v, COL_GA, KD), (N_GR, win_v, COL_GR, KD),
                                        (N_BR, wbr_v, 0, KD), (N_O, wout_v, 0, KD)):
                with sp.Fori(0, trips // 2) as i:
                    for p in range(2):
                        load(2 * i + (N0 + p), p, part(view, c0, 2 * i + p), K=view.shape[1])
                if N0 == N_BR:
                    sp.wait_ge(tile_done, N_O)
                    for s in range(5):
                        load_expert(sp, 0, s)
                    for n, v in enumerate((ln1_g, ln1_b)):
                        sp.dma_start(ln1_gb[:, n, :], v.to_broadcast([P, D])).then_inc(ln1_landed, 16)
            sp.wait_ge(x1_done, TT)
            load_expert(sp, 0, 5)
            for s in range(4):
                load_expert(sp, 1, s)
            with sp.Fori(2, NE) as b:
                for s in (4, 5):
                    load_expert(sp, b - 1, s, again=True)
                for s in range(4):
                    load_expert(sp, b, s, again=True)
            for s in (4, 5):
                load_expert(sp, NE - 1, s)
            sp.wait_ge(dest_done, 1)
            more = sp.value_load(plan[0:1, 7:8], min_val=0, max_val=BLOCKS - NE)
            with sp.If(more > 0):
                with sp.Fori(0, more) as i:
                    e = sp.value_load(plan[0:1, ds(i, 1)], min_val=0, max_val=NE - 1)
                    for s in range(6):
                        load_expert(sp, i + NE, s, expert=e, again=True)
            for t in range(TT):
                sp.wait_ge(out_ready, t + 1)
                sp.dma_start(out2[t * P:(t + 1) * P, :], yg[:, 0, t, :]).then_inc(stored, 16)
            sp.wait_ge(stored, 16 * TT)

        @block.gpsimd
        def _(pool):
            nc.gpsimd.memset(ones[:], 1.0).then_inc(pool_step, 1)
            nc.gpsimd.memset(zero[:], 0.0).then_inc(pool_step, 1)
            nc.gpsimd.iota(iota_e[:], pattern=[[1, NE]], base=0, channel_multiplier=0,
                           allow_small_or_imprecise_dtypes=True).then_inc(pool_step, 1)
            pool.wait_ge(pool_step, 3)
            nc.gpsimd.affine_select(out=ident[:], in_=ones[:], compare_op=ALU.is_equal, fill=0.0,
                                    base=0, pattern=[[-1, P]], channel_multiplier=1).then_inc(masks, 1)
            nc.gpsimd.affine_select(out=before[:], in_=ones[:], compare_op=ALU.is_gt, fill=0.0,
                                    base=0, pattern=[[1, P]], channel_multiplier=-1).then_inc(masks, 1)
            with pool.Fori(0, BLOCKS) as b:
                pool.dma_start(xs[ds(b * P, P), :], zero[:]).then_inc(zero_done, 16)
            with pool.Fori(NE, BLOCKS) as b:
                pool.dma_start(ys[ds(b * P, P), :], zero[:]).then_inc(zero_done, 16)
            pool.wait_ge(zero_done, ZEROS)
            pool.wait_ge(dest_done, 1)
            for t in range(TT):
                for n in range(2):
                    pool.indirect_dma_start(
                        out=xs, out_offset=bass.IndirectOffsetOnAxis(ap=dest[:, n, t:t + 1], axis=0),
                        in_=x1[:, t, :], in_offset=None).then_inc(scat, 16)
            pool.wait_ge(scat, 16 * 2 * TT)

            def load_rows(b, first=False):
                if not first:
                    pool.wait_ge(xe_t, b)
                    pool.wait_ge(xe_t, 1)
                src = xs[b * P:(b + 1) * P, :] if isinstance(b, int) else xs[ds(b * P, P), :]
                pool.dma_start(xe[:], src).then_inc(xe_landed, 16)

            load_rows(0, first=True)
            for n, v in enumerate((ln2_g, ln2_b)):
                pool.dma_start(ln2_gb[:, n, :], v.to_broadcast([P, D])).then_inc(ln2_landed, 16)
            load_rows(1)
            with pool.Fori(1, NE - 1) as b:
                load_rows(b + 1)
            more = pool.value_load(plan[0:1, 7:8], min_val=0, max_val=BLOCKS - NE)
            with pool.If(more > 0):
                with pool.Fori(0, more) as i:
                    load_rows(i + NE)
            pool.wait_ge(all_stored, 1)
            for t in range(TT):
                for n in range(2):
                    pool.indirect_dma_start(
                        out=yg[:, n, t, :], out_offset=None, in_=ys,
                        in_offset=bass.IndirectOffsetOnAxis(ap=dest[:, n, t:t + 1], axis=0)
                    ).then_inc(got[t], 16)

        @block.tensor
        def _(pe):
            pe.wait_ge(masks, 2)
            pe.wait_ge(x_landed, 16 * TT)
            for t in range(TT):
                if t >= 2:
                    pe.wait_ge(xt_lo, t - 1)
                for k in range(KD):
                    mm = pe.transpose(psC[t % 2][:, k // 4, (k % 4) * P:(k % 4 + 1) * P],
                                      x1[:, t, k * P:(k + 1) * P], ident[:])
                mm.then_inc(xt_t, 1)
            pe.wait_ge(rows_landed, 16 * 6)
            pe.transpose(psB[0][:, 0:NROW], rows[0:NROW, :], ident[0:NROW, 0:NROW]).then_inc(chan_t, 1)
            pe.wait_ge(xt_lo, TT)

            def product(bank, stat, moving, K):
                (s_hi, s_lo), (m_hi, m_lo) = stat, moving
                for k in range(K):
                    pe.matmul(bank, s_hi[:, k, :], m_hi[:, k, :], start=(k == 0), stop=False)
                    pe.matmul(bank, s_hi[:, k, :], m_lo[:, k, :], start=False, stop=False)
                    mm = pe.matmul(bank, s_lo[:, k, :], m_hi[:, k, :], start=False, stop=(k == K - 1))
                return mm

            def tile(N, p, bank, moving, K=KD):
                pe.wait_ge(w_lo, N + 1)
                product(bank, (whi[p], wlo[p]), moving, K).then_inc(tile_done, 1)

            def xr(j, p, first=False):
                if not first:
                    pe.wait_ge(xc_done, j - 1)
                tile(j, p, psA[p][:], (xT_hi, xT_lo))

            def rg(j, p, first=False):
                pe.wait_ge(xc_l, j + 1)
                pe.wait_ge(rgw_lo, j + 1)
                if not first:
                    pe.wait_ge(gate_done, j)
                for n in range(2):
                    pe.matmul(psB[n][:], rg_hi[p][:, n, :], xc_hi[:], start=True, stop=False)
                    pe.matmul(psB[n][:], rg_hi[p][:, n, :], xc_lo[:], start=False, stop=False)
                    mm = pe.matmul(psB[n][:], rg_lo[p][:, n, :], xc_hi[:], start=False, stop=True)
                mm.then_inc(rg_done, 1)

            xr(0, 0, first=True)
            xr(1, 1, first=True)
            pe.wait_ge(chan_ready, 1)
            rg(0, 0, first=True)
            with pe.Fori(1, KR // 2) as i:
                xr(2 * i, 0)
                rg(2 * i - 1, 1)
                xr(2 * i + 1, 1)
                rg(2 * i, 0)
            rg(KR - 1, 1)
            pe.wait_ge(gate_done, KR)
            pe.wait_ge(xt_lo, TT)
            with pe.Fori(0, KD // 2) as i:
                for m in range(6):
                    if m % 3 == 0:
                        if m == 0:
                            pe.wait_ge(u_done, 2 * i)
                        elif m == 3:
                            pe.wait_ge(u_done, 2 * i)
                    tile(6 * i + (N_A + m), m % 2, ps6[m], (xT_hi, xT_lo))
            pe.wait_ge(xc_done, KR)
            pe.wait_ge(u_l, KD)
            for N0, bank, moving, read, K in (
                    (N_BA, psA, (u_hi, u_lo), ya_done, KD),
                    (N_YR, psB, (xT_hi, xT_lo), hg_done, KD),
                    (N_GA, psA, (xT_hi, xT_lo), ga_read, KD),
                    (N_GR, psB, (xT_hi, xT_lo), gr_read, KD),
                    (N_BR, psA, (hg_hi, hg_lo), mf_done, KR),
                    (N_O, psB, (mg_hi, mg_lo), yT_done, KD)):
                if N0 == N_GA:
                    pe.wait_ge(ya_done, KD)
                if N0 == N_GR:
                    pe.wait_ge(hg_done, KR)
                if N0 == N_BR:
                    pe.wait_ge(ga_read, KD)
                    pe.wait_ge(hg_l, KR)
                if N0 == N_O:
                    pe.wait_ge(gr_read, KD)
                    pe.wait_ge(mg_l, KD)
                n = KR if N0 == N_YR else KD
                for p in range(2):
                    tile(N0 + p, p, bank[p][:], moving, K)
                with pe.Fori(1, n // 2) as i:
                    for p in range(2):
                        pe.wait_ge(read, 2 * i + (p - 1))
                        tile(2 * i + (N0 + p), p, bank[p][:], moving, K)

            def back(t):
                if t >= 2:
                    pe.wait_ge(res_done, t - 1)
                for k in range(KD):
                    mm = pe.transpose(psC[t % 2][:, k // 4, (k % 4) * P:(k % 4 + 1) * P],
                                      yT[:, k, t * P:(t + 1) * P], ident[:])
                mm.then_inc(y_t, 1)

            def router(t):
                pe.wait_ge(x1_done, t + 1)
                if t >= 1:
                    pe.wait_ge(x1T_done, t)
                for k in range(KD):
                    mm = pe.transpose(psA[k // 4][:, (k % 4) * P:(k % 4 + 1) * P],
                                      x1[:, t, k * P:(k + 1) * P], ident[:])
                mm.then_inc(x1_t, 1)
                pe.wait_ge(x1T_done, t + 1)
                for k in range(KD):
                    mm = pe.matmul(psB[0][:, t * NE:(t + 1) * NE], x1T[:, t, k, :], wr[:, k, :],
                                   start=(k == 0), stop=(k == KD - 1))
                mm.then_inc(logit_done, 1)

            pe.wait_ge(yT_done, KD)
            pe.wait_ge(small_landed, 32)
            back(0)
            back(1)
            for t in range(TT):
                if t + 2 < TT:
                    back(t + 2)
                router(t)
            pe.wait_ge(sel_done, 1)
            sel = r16[8]
            for t in range(TT):
                for q in range(t):
                    pe.matmul(psB[1][:, t * NE:(t + 1) * NE], ones[:], sel[:, q, :],
                              start=(q == 0), stop=False)
                pe.matmul(psB[1][:, t * NE:(t + 1) * NE], before[:], sel[:, t, :], start=(t == 0), stop=True)
            for q in range(TT):
                mm = pe.matmul(psB[1][:, TT * NE:(TT + 1) * NE], ones[:], sel[:, q, :],
                               start=(q == 0), stop=(q == TT - 1))
            mm.then_inc(pos_done, 1)

            def rows_t(b, first=False):
                pe.wait_ge(xe_landed, b * 16 + 16)
                if not first:
                    pe.wait_ge(xe_l, b)
                for k in range(KD):
                    mm = pe.transpose(psC[0][:, k // 4, (k % 4) * P:(k % 4 + 1) * P],
                                      xe[:, k * P:(k + 1) * P], ident[:])
                mm.then_inc(xe_t, 1)

            def gate_up(b, first=False):
                pe.wait_ge(xe_l, b + 1)
                for s in range(4):
                    if s % 2 == 0 and not first:
                        pe.wait_ge((silu_done, h_done)[s // 2], b)
                    pe.wait_ge(gu_lo, b * 4 + (s + 1))
                    for k in range(4):
                        q = 4 * (s % 2) + k
                        pe.matmul(psA[s // 2][:], xe_hi[:, q, :], ehi[s][:, k, :], start=(q == 0), stop=False)
                        pe.matmul(psA[s // 2][:], xe_hi[:, q, :], elo[s][:, k, :], start=False, stop=False)
                        mm = pe.matmul(psA[s // 2][:], xe_lo[:, q, :], ehi[s][:, k, :], start=False,
                                       stop=(q == KD - 1))
                    mm.then_inc(gu_used, 1)

            def hidden_t(b, first=False):
                pe.wait_ge(h_done, b + 1)
                if not first:
                    pe.wait_ge(h_l, b)
                for k in range(KF):
                    mm = pe.transpose(psC[1][:, 0, k * P:(k + 1) * P], hb[:, k * P:(k + 1) * P], ident[:])
                mm.then_inc(h_t, 1)

            def down(b, first=False):
                pe.wait_ge(h_l, b + 1)
                for s in range(2):
                    if not first:
                        pe.wait_ge(y_evac, b * 2 + (s - 1))
                    pe.wait_ge(d_lo, b * 2 + (s + 1))
                    for k in range(KF):
                        pe.matmul(psB[s][:], hT_hi[:, k, :], ehi[4 + s][:, k, :], start=(k == 0), stop=False)
                        pe.matmul(psB[s][:], hT_hi[:, k, :], elo[4 + s][:, k, :], start=False, stop=False)
                        mm = pe.matmul(psB[s][:], hT_lo[:, k, :], ehi[4 + s][:, k, :], start=False,
                                       stop=(k == KF - 1))
                    mm.then_inc(d_used, 1)

            pe.wait_ge(dest_done, 1)
            rows_t(0, first=True)
            gate_up(0, first=True)
            rows_t(1)
            hidden_t(0, first=True)
            gate_up(1)
            rows_t(2)
            down(0, first=True)
            hidden_t(1)
            with pe.Fori(2, NE - 1) as b:
                gate_up(b)
                rows_t(b + 1)
                down(b - 1)
                hidden_t(b)
            gate_up(NE - 1)
            down(NE - 2)
            hidden_t(NE - 1)
            down(NE - 1)
            more = pe.value_load(plan[0:1, 7:8], min_val=0, max_val=BLOCKS - NE)
            with pe.If(more > 0):
                with pe.Fori(0, more) as i:
                    rows_t(i + NE)
                    gate_up(i + NE)
                    hidden_t(i + NE)
                    down(i + NE)

        @block.scalar
        def _(act):
            A = nc.scalar.activation

            def hi(N, p, K=KD, first=False):
                n, half = N
                act.wait_ge(w_landed[p], half * 16 + 16)
                if not first:
                    act.wait_ge(tile_done, n - 1)
                A(whi[p][:, 0:K, :], wst[p][:, 0:K, :], ACT.Copy).then_inc(w_hi, 1)

            for t in range(TT):
                act.wait_ge(xt_t, t + 1)
                A(xT_hi[:, :, t * P:(t + 1) * P], psC[t % 2][:].rearrange("p a (b c) -> p (a b) c", c=P),
                  ACT.Copy).then_inc(xt_hi, 1)
                if t == 1:
                    hi((0, 0), 0, first=True)
            act.wait_ge(chan_ready, 1)
            A(decay[:, 1, :], chan[:, C_LAM:C_LAM + KR], ACT.Abs).then_inc(decay_act, 1)
            act.wait_ge(decay_act, 1)
            A(decay[:, 2, :], decay[:, 1, :], ACT.Exp, scale=-1.0).then_inc(decay_act, 1)

            def conv_start(j, p, first=False):
                act.wait_ge(tile_done, j + 1)
                if not first:
                    act.wait_ge(ix_done, j - 1)
                A(xc[p][:], psA[p][:], ACT.Identity, bias=_col(chan, C_CB, j),
                  scale=_col(chan, C_CR(3, 0), j)).then_inc(xc_start, 1)

            def rg_round(j, p, first=False):
                j, half = j
                act.wait_ge(rg_landed[p], half * 32 + 32)
                if not first:
                    act.wait_ge(rg_done, j - 1)
                A(rg_hi[p][:], rg_st[p][:], ACT.Copy).then_inc(rgw_hi, 1)

            def xc_round(j, p, first=False):
                act.wait_ge(xc_done, j + 1)
                if not first:
                    act.wait_ge(rg_done, j)
                A(xc_hi[:], xc[p][:], ACT.Copy).then_inc(xc_h, 1)

            def sigmoids(j, p, first=False):
                act.wait_ge(rg_done, j + 1)
                if not first:
                    act.wait_ge(ix_done, j - 1)
                A(_tile(zbuf, j), psB[0][:], ACT.Sigmoid, bias=_col(chan, C_BA, j))
                A(ig[p][:], psB[1][:], ACT.Sigmoid, bias=_col(chan, C_BX, j)).then_inc(gate_done, 1)

            hi((1, 0), 1, first=True)
            rg_round((0, 0), 0, first=True)
            conv_start(0, 0, first=True)
            xc_round(0, 0, first=True)

            hi((2, 1), 0)
            rg_round((1, 0), 1, first=True)
            conv_start(1, 1, first=True)
            sigmoids(0, 0, first=True)
            xc_round(1, 1)
            with act.Fori(1, KR // 2) as i:
                for p in range(2):
                    hi((2 * i + (p + 1), i + p), 1 - p)
                    rg_round((2 * i + p, i), p)
                    conv_start(2 * i + p, p)
                    sigmoids(2 * i + (p - 1), 1 - p)
                    xc_round(2 * i + p, p)
            sigmoids(KR - 1, 1)

            QC = KR * S // 4
            zf = zbuf[:].rearrange("p j s -> p (j s)")
            tf = tbuf[:].rearrange("p j s -> p (j s)")
            act.wait_ge(ix_done, KR)
            act.wait_ge(zero_done, ZEROS)
            with act.Fori(0, KD // 2) as i:
                for q in range(2):
                    j, m = 2 * i + q, 3 * q
                    N = lambda n: (6 * i + (N_A + m + n), 3 * i + (N_A + m + n) // 2)
                    hi(N(1), (m + 1) % 2)
                    act.wait_ge(tile_done, 6 * i + (N_A + m + 1))
                    act.wait_ge(v_done, j)
                    A(tmp[0][:], ps6[m], ACT.Copy).then_inc(c_read, 1)
                    hi(N(2), m % 2)
                    act.wait_ge(v_done, j + 1)
                    act.wait_ge(u_done, j)
                    A(tmp[2][:], tmp[1][:], ACT.Identity, bias=0.0, scale=_col(chan, C_CA(2, 0), j)).then_inc(t_start, 1)
                    if q == 0:
                        A(tf[:, ds(i * QC, QC)], zf[:, ds(i * QC, QC)], ACT.Tanh, scale=-0.5)
                        A(zf[:, ds(i * QC, QC)], zf[:, ds(i * QC, QC)], ACT.Exp).then_inc(a_done, 1)
                    hi(N(3), (m + 1) % 2)
                    act.wait_ge(u_done, j + 1)
                    A(_tile(u_hi, j), tmp[3][:], ACT.Copy).then_inc(u_h, 1)
            with act.Fori(0, KD // 2) as i:
                for p in range(2):
                    hi((2 * i + (N_BA + p + 1), i + (N_BA + p + 1) // 2), 1 - p)
                    if p == 0:
                        act.wait_ge(a_done, i + 1)
                        A(tf[:, ds(i * QC, QC)], tf[:, ds(i * QC, QC)], ACT.Sqrt).then_inc(sq_done, 1)
                    act.wait_ge(tile_done, 2 * i + (N_BA + p + 1))
                    A(_tile(ya, 2 * i + p), psA[p][:], ACT.Copy).then_inc(ya_done, 1)
            act.wait_ge(bt_done, 4)
            with act.Fori(0, KR // 2) as i:
                for p in range(2):
                    j = 2 * i + p
                    hi((2 * i + (N_YR + p + 1), i + (N_YR + p + 1) // 2), 1 - p)
                    act.wait_ge(tile_done, 2 * i + (N_YR + p + 1))
                    act.wait_ge(y_q, j)
                    A(tmp[0][:], psB[p][:], ACT.Square).then_inc(y_sq, 1)
                    act.wait_ge(y_q, j + 1)
                    A(tmp[2][:], tmp[1][:], ACT.Sigmoid, scale=GELU_S * GELU_A).then_inc(y_sig, 1)
                    act.wait_ge(hg_done, j + 1)
                    A(_tile(hg_hi, j), tmp[4][:], ACT.Copy).then_inc(hg_h, 1)
            with act.Fori(0, KD // 2) as i:
                for p in range(2):
                    hi((2 * i + (N_GA + p + 1), i + (N_GA + p + 1) // 2), 1 - p)
                    act.wait_ge(tile_done, 2 * i + (N_GA + p + 1))
                    act.wait_ge(m_done, 2 * i + p)
                    A(tmp[6][:], psA[p][:], ACT.Sigmoid).then_inc(ga_read, 1)

            def gr(i, last):
                for p in range(2):
                    hi((2 * i + (N_GR + p + 1), i + (N_GR + p + 1) // 2), 1 - p, K=KR if last and p else KD)
                    act.wait_ge(tile_done, 2 * i + (N_GR + p + 1))
                    A(_tile(sgr, 2 * i + p), psB[p][:], ACT.Sigmoid).then_inc(gr_read, 1)

            with act.Fori(0, KD // 2 - 1) as i:
                gr(i, False)
            gr(KD // 2 - 1, True)

            def br(i, last):
                for p in range(2):
                    hi((2 * i + (N_BR + p + 1), i + (N_BR + p + 1) // 2), 1 - p, K=KD if last and p else KR)
                    act.wait_ge(mf_done, 2 * i + (p + 1))
                    A(_tile(mg_hi, 2 * i + p), tmp[1][:], ACT.Copy).then_inc(mg_h, 1)

            with act.Fori(0, KD // 2 - 1) as i:
                br(i, False)
            br(KD // 2 - 1, True)

            def e_round(b, s, first=False):
                act.wait_ge(e_landed[s], b * 16 + 16)
                if not first:
                    if s < 4:
                        act.wait_ge(gu_used, b * 4 + (s - 3))
                    else:
                        act.wait_ge(d_used, b * 2 + (s - 5))
                A(ehi[s][:], est[s][:], ACT.Copy).then_inc(gu_hi if s < 4 else d_hi, 1)

            for j in range(KD):
                N = N_O + j
                if j < KD - 1:
                    hi((N + 1, (N + 1) // 2), (N + 1) % 2)
                if j == 1:
                    act.wait_ge(mg_l, KD)
                if j % 2:
                    e_round(0, j // 2, first=True)
                act.wait_ge(tile_done, N + 1)
                A(yT[:, j, :], psB[j % 2][:], ACT.Copy).then_inc(yT_done, 1)

            for t in range(TT):
                _std(act, t, var_done, std_done, stat)
                act.wait_ge(x1_t, t + 1)
                if t == 0:
                    act.wait_ge(tile_done, N_END)
                A(x1T[:, t, 0:4, :], psA[0][:].rearrange("p (k c) -> p k c", c=P), ACT.Copy)
                A(x1T[:, t, 4:8, :], psA[1][:].rearrange("p (k c) -> p k c", c=P), ACT.Copy).then_inc(x1T_done, 1)
            act.wait_ge(lmax_done, 1)
            A(r16[1][:], r16[0][:], ACT.Exp).then_inc(exp_done, 1)
            e_round(0, 4, first=True)
            act.wait_ge(y_t, TT)
            e_round(0, 5, first=True)

            def rows_round(b, first=False):
                act.wait_ge(xe_t, b + 1)
                if not first:
                    act.wait_ge(gu_used, b * 4)
                A(xe_hi[:], psC[0][:].rearrange("p a (k c) -> p (a k) c", c=P), ACT.Copy).then_inc(xe_h, 1)

            def silu(b, first=False):
                act.wait_ge(gu_used, b * 4 + 2)
                if not first:
                    act.wait_ge(h_done, b)
                A(sg[:], psA[0][:], ACT.Silu).then_inc(silu_done, 1)

            def hidden_round(b, first=False):
                act.wait_ge(h_t, b + 1)
                if not first:
                    act.wait_ge(d_used, b * 2)
                A(hT_hi[:], psC[1][:, 0, :].rearrange("p (k c) -> p k c", c=P), ACT.Copy).then_inc(h_h, 1)

            def y_out(b, s, first=False):
                act.wait_ge(d_used, b * 2 + (s + 1))
                if not first:
                    act.wait_ge(y_stored, b * 16)
                A(yb[:, s * DF:(s + 1) * DF], psB[s][:], ACT.Copy).then_inc(y_evac, 1)
                if s == 1:
                    dst = ys[b * P:(b + 1) * P, :] if isinstance(b, int) else ys[ds(act.snap(b * P), P), :]
                    act.wait_ge(y_evac, b * 2 + 2)
                    act.dma_start(dst, yb[:]).then_inc(y_stored, 16)

            rows_round(0, first=True)

            def turn(b, nxt=True, prev=True, first=False, first_prev=False):
                if nxt:
                    e_round(b + 1, 0)
                    e_round(b + 1, 1)
                silu(b, first)
                if nxt:
                    e_round(b + 1, 2)
                    e_round(b + 1, 3)
                    rows_round(b + 1)
                for s in range(2):
                    if prev:
                        e_round(b, 4 + s)
                        y_out(b - 1, s, first_prev)
                hidden_round(b, first)

            turn(0, prev=False, first=True)
            turn(1, first_prev=True)
            with act.Fori(2, NE - 1) as b:
                turn(b)
            turn(NE - 1, nxt=False)
            for s in range(2):
                y_out(NE - 1, s)
            more = act.value_load(plan[0:1, 7:8], min_val=0, max_val=BLOCKS - NE)
            with act.If(more > 0):
                with act.Fori(0, more) as i:
                    b = i + NE
                    for s in range(4):
                        e_round(b, s)
                    rows_round(b)
                    silu(b)
                    for s in range(2):
                        e_round(b, 4 + s)
                    hidden_round(b)
                    for s in range(2):
                        y_out(b, s)
            act.wait_ge(y_stored, (more + NE) * 16)
            A(stat[:, 20:21], stat[:, 13:14], ACT.Copy).then_inc(all_stored, 1)
            for t in range(TT):
                _std(act, TT + t, var_done, std_done, stat)

        @block.vector
        def _(dve):
            V = nc.vector
            chain = Chain(dve, dve_step)

            def lo(N, p, K=KD):
                dve.wait_ge(w_hi, N + 1)
                V.tensor_tensor(wlo[p][:, 0:K, :], wst[p][:, 0:K, :], whi[p][:, 0:K, :],
                                ALU.subtract).then_inc(w_lo, 1)

            for t in range(TT):
                dve.wait_ge(xt_hi, t + 1)
                V.tensor_tensor(xT_lo[:, :, t * P:(t + 1) * P],
                                psC[t % 2][:].rearrange("p a (b c) -> p (a b) c", c=P),
                                xT_hi[:, :, t * P:(t + 1) * P], ALU.subtract).then_inc(xt_lo, 1)
                if t == 1:
                    lo(0, 0)
            dve.wait_ge(chan_t, 1)
            V.tensor_copy(chan[:, 0:NROW], psB[0][:, 0:NROW]).then_inc(chan_ready, 1)
            dve.wait_ge(decay_act, 2)
            e, s1, s2, acc = (decay[:, n, :] for n in (2, 3, 4, 5))
            chain.link(V.tensor_scalar(acc, e, 2.0, None, ALU.add))
            chain.link(V.reciprocal(s1, acc))
            chain.link(V.tensor_tensor(s1, s1, e, ALU.mult))
            chain.link(V.tensor_tensor(s2, s1, s1, ALU.mult))
            TERMS = 8
            chain.link(V.tensor_scalar(acc, s2, 1.0 / (2 * TERMS + 1), 1.0 / (2 * TERMS - 1), ALU.mult, ALU.add))
            for n in range(TERMS - 2, -1, -1):
                chain.link(V.tensor_tensor(acc, acc, s2, ALU.mult))
                chain.link(V.tensor_scalar(acc, acc, 1.0 / (2 * n + 1), None, ALU.add))
            chain.link(V.tensor_tensor(acc, acc, s1, ALU.mult))
            chain.link(V.tensor_scalar(s2, chan[:, C_LAM:C_LAM + KR], -1.0, 0.0, ALU.mult, ALU.max))
            chain.link(V.scalar_tensor_tensor(acc, acc, 2.0, s2, ALU.mult, ALU.add))
            chain.link(V.tensor_scalar(decay[:, 0, :], acc, -8.0, None, ALU.mult))

            def rg_rest(j, p):
                dve.wait_ge(rgw_hi, j + 1)
                V.tensor_tensor(rg_lo[p][:], rg_st[p][:], rg_hi[p][:], ALU.subtract).then_inc(rgw_lo, 1)

            def conv_rest(j, p):
                dve.wait_ge(xc_start, j + 1)
                for k in (2, 1, 0):
                    d = 3 - k
                    ins = V.scalar_tensor_tensor(xc[p][:, d:S], psA[p][:, 0:S - d], _col(chan, C_CR(k, 0), j),
                                                 xc[p][:, d:S], ALU.mult, ALU.add)
                    if k:
                        chain.link(ins)
                ins.then_inc(xc_done, 1)

            def xc_rest(j, p):
                dve.wait_ge(xc_h, j + 1)
                V.tensor_tensor(xc_lo[:], xc[p][:], xc_hi[:], ALU.subtract).then_inc(xc_l, 1)

            def gates_of(j, p):
                dve.wait_ge(gate_done, j + 1)
                V.tensor_scalar(_tile(zbuf, j), _tile(zbuf, j), _col(decay[:, 0, :], 0, j), None, ALU.mult)
                V.tensor_tensor(_tile(ibuf, j), ig[p][:], xc[p][:], ALU.mult).then_inc(ix_done, 1)

            lo(1, 1)
            rg_rest(0, 0)
            conv_rest(0, 0)
            xc_rest(0, 0)
            lo(2, 0)
            rg_rest(1, 1)
            conv_rest(1, 1)
            gates_of(0, 0)
            xc_rest(1, 1)

            start = chain.n
            with dve.Fori(1, KR // 2) as i:
                chain.n = i * 4 + (start - 4)
                for p in range(2):
                    lo(2 * i + (p + 1), 1 - p)
                    rg_rest(2 * i + p, p)
                    conv_rest(2 * i + p, p)
                    gates_of(2 * i + (p - 1), 1 - p)
                    xc_rest(2 * i + p, p)
            chain.n = start + 4 * (KR // 2 - 1)
            gates_of(KR - 1, 1)
            dve.wait_ge(zero_done, ZEROS)

            QC = KR * S // 4
            zf = zbuf[:].rearrange("p j s -> p (j s)")
            tf = tbuf[:].rearrange("p j s -> p (j s)")
            xf = ibuf[:].rearrange("p j s -> p (j s)")

            def gated_conv(i):
                for q in range(2):
                    j, m = 2 * i + q, 3 * q
                    N = 6 * i + (N_A + m)
                    lo(N + 1, (m + 1) % 2)
                    lo(N + 2, m % 2)
                    dve.wait_ge(c_read, j + 1)
                    dve.wait_ge(tile_done, N + 2)
                    dve.wait_ge(t_start, j)
                    V.tensor_tensor(tmp[1][:], tmp[0][:], ps6[m + 1], ALU.mult).then_inc(v_done, 1)
                    dve.wait_ge(t_start, j + 1)
                    for k in (1, 0):
                        d = 2 - k
                        chain.link(V.scalar_tensor_tensor(tmp[2][:, d:S], tmp[1][:, 0:S - d],
                                                          _col(chan, C_CA(k, 0), j), tmp[2][:, d:S],
                                                          ALU.mult, ALU.add))
                    lo(N + 3, (m + 1) % 2)
                    dve.wait_ge(tile_done, N + 3)
                    dve.wait_ge(u_h, j)
                    V.tensor_tensor(tmp[3][:], tmp[2][:], ps6[m + 2], ALU.mult).then_inc(u_done, 1)
                    dve.wait_ge(u_h, j + 1)
                    V.tensor_tensor(_tile(u_lo, j), tmp[3][:], _tile(u_hi, j), ALU.subtract).then_inc(u_l, 1)

            chain.loop(KD // 2, gated_conv, 4)

            def branch_a(i):
                for p in range(2):
                    lo(2 * i + (N_BA + p + 1), 1 - p)
                    if p == 0:
                        dve.wait_ge(sq_done, i + 1)
                        q = ds(i * QC, QC)
                        chain.link(V.scalar_tensor_tensor(tf[:, q], zf[:, q], 1.0, tf[:, q], ALU.add, ALU.mult))
                        V.tensor_tensor(xf[:, q], xf[:, q], tf[:, q], ALU.mult).then_inc(bt_done, 1)

            chain.loop(KD // 2, branch_a, 1)
            dve.wait_ge(bt_done, 4)

            def gelu_r(i):
                for p in range(2):
                    j = 2 * i + p
                    N = 2 * i + (N_YR + p)
                    lo(N + 1, 1 - p)
                    chain.link(V.tensor_tensor_scan(_tile(zbuf, j), _tile(zbuf, j), _tile(ibuf, j), 0.0,
                                                    ALU.mult, ALU.add))
                    dve.wait_ge(y_sq, j + 1)
                    dve.wait_ge(y_sig, j)
                    V.scalar_tensor_tensor(tmp[1][:], tmp[0][:], 1.0 / GELU_A, psB[p][:],
                                           ALU.add, ALU.mult).then_inc(y_q, 1)
                    chain.link(V.tensor_tensor(tmp[3][:], _tile(zbuf, j), psB[p][:], ALU.mult))
                    dve.wait_ge(y_sig, j + 1)
                    dve.wait_ge(hg_h, j)
                    V.tensor_tensor(tmp[4][:], tmp[3][:], tmp[2][:], ALU.mult).then_inc(hg_done, 1)
                    dve.wait_ge(hg_h, j + 1)
                    V.tensor_tensor(_tile(hg_lo, j), tmp[4][:], _tile(hg_hi, j), ALU.subtract).then_inc(hg_l, 1)

            chain.loop(KR // 2, gelu_r, 4)

            with dve.Fori(0, KD // 2) as i:
                for p in range(2):
                    j = 2 * i + p
                    lo(2 * i + (N_GA + p + 1), 1 - p)
                    dve.wait_ge(ga_read, j + 1)
                    V.tensor_tensor(_tile(ya, j), _tile(ya, j), tmp[6][:], ALU.mult).then_inc(m_done, 1)

            def gr(i, last):
                for p in range(2):
                    lo(2 * i + (N_GR + p + 1), 1 - p, K=KR if last and p else KD)

            with dve.Fori(0, KD // 2 - 1) as i:
                gr(i, False)
            gr(KD // 2 - 1, True)
            dve.wait_ge(gr_read, KD)
            dve.wait_ge(m_done, KD)

            def br(i, last):
                for p in range(2):
                    j = 2 * i + p
                    N = 2 * i + (N_BR + p)
                    lo(N + 1, 1 - p, K=KD if last and p else KR)
                    dve.wait_ge(tile_done, N + 1)
                    chain.link(V.tensor_tensor(tmp[0][:], _tile(sgr, j), psA[p][:], ALU.mult))
                    dve.wait_ge(mg_h, j)
                    V.tensor_tensor(tmp[1][:], tmp[0][:], _tile(ya, j), ALU.add).then_inc(mf_done, 1)
                    dve.wait_ge(mg_h, j + 1)
                    V.tensor_tensor(_tile(mg_lo, j), tmp[1][:], _tile(mg_hi, j), ALU.subtract).then_inc(mg_l, 1)

            chain.loop(KD // 2 - 1, lambda i: br(i, False), 2)
            br(KD // 2 - 1, True)

            def e_rest(b, s):
                if s < 4:
                    dve.wait_ge(gu_hi, b * 4 + (s + 1))
                else:
                    dve.wait_ge(d_hi, b * 2 + (s - 3))
                V.tensor_tensor(elo[s][:], est[s][:], ehi[s][:], ALU.subtract).then_inc(gu_lo if s < 4 else d_lo, 1)

            for j in range(KD):
                if j < KD - 1:
                    lo(N_O + j + 1, (N_O + j + 1) % 2)
                if j in (1, 3, 5):
                    e_rest(0, j // 2)
            dve.wait_ge(tile_done, N_END)

            def normalise(t, row, gb, done):
                b6 = stat[:, 0:12].rearrange("p (a c) -> p a c", c=6)
                for h in range(2):
                    ins = V.bn_stats(b6[:, h, :], row[:, h * S:(h + 1) * S])
                chain.link(ins)
                chain.link(V.bn_aggr(stat[:, 12:14], b6))
                V.tensor_scalar(stat[:, 14:15], stat[:, 13:14], LN_EPS, None, ALU.add).then_inc(var_done, 1)
                dve.wait_ge(std_done, t + 1)
                chain.link(V.reciprocal(stat[:, 16:17], stat[:, 15:16]))
                chain.link(V.scalar_tensor_tensor(stat[:, 17:18], stat[:, 14:15], stat[:, 16:17],
                                                  stat[:, 15:16], ALU.mult, ALU.add))
                chain.link(V.tensor_scalar(stat[:, 18:19], stat[:, 17:18], 0.5, None, ALU.mult))
                chain.link(V.reciprocal(stat[:, 19:20], stat[:, 18:19]))
                chain.link(V.tensor_scalar(row, row, stat[:, 12:13], stat[:, 19:20], ALU.subtract, ALU.mult))
                chain.link(V.tensor_tensor(row, row, gb[:, 0, :], ALU.mult))
                V.tensor_tensor(row, row, gb[:, 1, :], ALU.add).then_inc(done, 1)

            dve.wait_ge(ln1_landed, 32)
            for t in range(TT):
                dve.wait_ge(y_t, t + 1)
                for h in range(2):
                    ins = V.scalar_tensor_tensor(x1[:, t, h * S:(h + 1) * S], x1[:, t, h * S:(h + 1) * S],
                                                 ALPHA, psC[t % 2][:, h, :], ALU.mult, ALU.add)
                ins.then_inc(res_done, 1)
                dve.wait_ge(res_done, t + 1)
                normalise(t, x1[:, t, :], ln1_gb, x1_done)
            dve.wait_ge(small_landed, 32)

            def b16(v):
                return v[:].unsqueeze(2).to_broadcast([P, TT, NE])

            def tt(o, a, b, op):
                chain.link(V.tensor_tensor(o, a, b, op))

            def red(o, a, op):
                chain.link(V.tensor_reduce(o, a, AX, op))

            ex, iota3 = r16[1], iota_e[:].unsqueeze(1).to_broadcast([P, TT, NE])
            dve.wait_ge(logit_done, TT)
            tt(r16[0][:], psB[0][:, 0:TT * NE].rearrange("p (t e) -> p t e", e=NE),
               brow[:].unsqueeze(1).to_broadcast([P, TT, NE]), ALU.add)
            red(r1[0][:], r16[0][:], ALU.max)
            V.tensor_tensor(r16[0][:], r16[0][:], b16(r1[0]), ALU.subtract).then_inc(lmax_done, 1)
            e_rest(0, 3)
            dve.wait_ge(exp_done, 1)
            red(r1[1][:], ex[:], ALU.add)
            chain.link(V.reciprocal(r1[2][:], r1[1][:]))
            pr = r16[2]
            tt(pr[:], ex[:], b16(r1[2]), ALU.mult)
            g4 = pr[:].rearrange("p t (g e) -> p t g e", e=GRP)
            score, pair = r4[0], r4[1]
            first = True
            for a in range(GRP):
                for b in range(a + 1, GRP):
                    tt((score if first else pair)[:], g4[:, :, :, a], g4[:, :, :, b], ALU.add)
                    if not first:
                        tt(score[:], score[:], pair[:], ALU.max)
                    first = False

            def first_of(o, idx, vals, width, best, scratch):
                bb = best[:].unsqueeze(2).to_broadcast([P, TT, width])
                it = iota_e[:, 0:width].unsqueeze(1).to_broadcast([P, TT, width])
                tt(scratch, vals, bb, ALU.is_lt)
                chain.link(V.scalar_tensor_tensor(scratch, scratch, 99.0, it, ALU.mult, ALU.add))
                red(idx[:], scratch, ALU.min)
                tt(o, it, idx[:].unsqueeze(2).to_broadcast([P, TT, width]), ALU.is_equal)

            red(r1[3][:], score[:], ALU.max)
            first_of(r4[2][:], r1[4], score[:], NG, r1[3], r4[3][:])
            pm = r16[3]
            gm = r4[2][:].unsqueeze(3).to_broadcast([P, TT, NG, GRP])
            pm4 = pm[:].rearrange("p t (g e) -> p t g e", e=GRP)
            chain.link(V.tensor_scalar(pm[:], pr[:], 1.0, None, ALU.add))
            tt(pm4, pm4, gm, ALU.mult)
            chain.link(V.tensor_scalar(pm[:], pm[:], -1.0, None, ALU.add))
            pw = r16[4]
            tt(pw[:].rearrange("p t (g e) -> p t g e", e=GRP), g4, gm, ALU.mult)
            chain.link(V.tensor_scalar(r4[4][:], r4[2][:], -1.0, None, ALU.add))
            tt(pm4, pw[:].rearrange("p t (g e) -> p t g e", e=GRP),
               r4[4][:].unsqueeze(3).to_broadcast([P, TT, NG, GRP]), ALU.add)
            red(r1[5][:], pm[:], ALU.max)
            oh1, oh2, sel = r16[5], r16[6], r16[8]
            first_of(oh1[:], r1[6], pm[:], NE, r1[5], r16[7][:])
            chain.link(V.scalar_tensor_tensor(pm[:], oh1[:], -4.0, pm[:], ALU.mult, ALU.add))
            red(r1[7][:], pm[:], ALU.max)
            first_of(oh2[:], r1[8], pm[:], NE, r1[7], r16[7][:])
            V.tensor_tensor(sel[:], oh1[:], oh2[:], ALU.add).then_inc(sel_done, 1)
            tt(r1[9][:], r1[5][:], r1[7][:], ALU.add)
            chain.link(V.reciprocal(r1[10][:], r1[9][:]))
            tt(gates[:, 0, :], r1[5][:], r1[10][:], ALU.mult)
            tt(gates[:, 1, :], r1[7][:], r1[10][:], ALU.mult)
            dve.wait_ge(pos_done, 1)
            dve.wait_ge(sel_done, 1)
            cnt, ext, inc, bb = (r16[n][:, 0, :] for n in (9, 10, 11, 12))
            chain.link(V.tensor_copy(cnt, psB[1][:, TT * NE:(TT + 1) * NE]))
            chain.link(V.tensor_scalar(ext, cnt, float(P), None, ALU.is_gt))
            for n in range(2, TT):
                chain.link(V.scalar_tensor_tensor(ext, cnt, float(n * P), ext, ALU.is_gt, ALU.add))
            chain.link(V.tensor_tensor_scan(inc, ones[:, 0:NE], ext, 0.0, ALU.mult, ALU.add))
            tt(bb, inc, ext, ALU.subtract)
            tt(bb, bb, iota_e[:], ALU.subtract)
            chain.link(V.tensor_scalar(bb, bb, float(P), float((NE - 1) * P), ALU.mult, ALU.add))
            pos, row = r16[13], r16[14]
            chain.link(V.tensor_copy(pos[:], psB[1][:, 0:TT * NE].rearrange("p (t e) -> p t e", e=NE)))
            chain.link(V.tensor_scalar(row[:], pos[:], float(P), None, ALU.is_ge))
            tt(row[:], row[:], bb.unsqueeze(1).to_broadcast([P, TT, NE]), ALU.mult)
            tt(row[:], row[:], pos[:], ALU.add)
            chain.link(V.scalar_tensor_tensor(row[:], iota3, float(P), row[:], ALU.mult, ALU.add))
            for n, oh in enumerate((oh1, oh2)):
                tt(r16[7][:], oh[:], row[:], ALU.mult)
                red(r1[11 + n][:], r16[7][:], ALU.add)
                chain.link(V.tensor_copy(dest[:, n, :], r1[11 + n][:]))
            for n in range(BLOCKS - NE):
                chain.link(V.tensor_scalar(r16[15][:, 0, :], inc, float(n), None, ALU.is_le))
                red(r1[13][:, 0:1], r16[15][:, 0, :], ALU.add)
                chain.link(V.tensor_scalar(r1[14][:, 0:1], r1[13][:, 0:1], float(NE - 1), None, ALU.min))
                chain.link(V.tensor_copy(plan[:, n:n + 1], r1[14][:, 0:1]))
            V.tensor_copy(plan[:, 7:8], inc[:, NE - 1:NE]).then_inc(dest_done, 1)

            e_rest(0, 4)
            e_rest(0, 5)

            def rows_rest(b):
                dve.wait_ge(xe_h, b + 1)
                V.tensor_tensor(xe_lo[:], psC[0][:].rearrange("p a (k c) -> p (a k) c", c=P), xe_hi[:],
                                ALU.subtract).then_inc(xe_l, 1)

            def hidden(b, first=False):
                dve.wait_ge(silu_done, b + 1)
                dve.wait_ge(gu_used, b * 4 + 4)
                if not first:
                    dve.wait_ge(h_t, b)
                V.tensor_tensor(hb[:], sg[:], psA[1][:], ALU.mult).then_inc(h_done, 1)

            def hidden_rest(b):
                dve.wait_ge(h_h, b + 1)
                V.tensor_tensor(hT_lo[:], psC[1][:, 0, :].rearrange("p (k c) -> p k c", c=P), hT_hi[:],
                                ALU.subtract).then_inc(h_l, 1)

            rows_rest(0)

            def turn(b, nxt=True, prev=True, first=False):
                if nxt:
                    for s in range(3):
                        e_rest(b + 1, s)
                hidden(b, first)
                if nxt:
                    e_rest(b + 1, 3)
                    rows_rest(b + 1)
                if prev:
                    e_rest(b, 4)
                    e_rest(b, 5)
                hidden_rest(b)

            turn(0, prev=False, first=True)
            with dve.Fori(1, NE - 1) as b:
                turn(b)
            turn(NE - 1, nxt=False)
            more = dve.value_load(plan[0:1, 7:8], min_val=0, max_val=BLOCKS - NE)
            with dve.If(more > 0):
                with dve.Fori(0, more) as i:
                    b = i + NE
                    for s in range(4):
                        e_rest(b, s)
                    rows_rest(b)
                    hidden(b)
                    e_rest(b, 4)
                    e_rest(b, 5)
                    hidden_rest(b)

            dve.wait_ge(ln2_landed, 32)
            for t in range(TT):
                dve.wait_ge(got[t], 32)
                row = yg[:, 0, t, :]
                chain.link(V.tensor_scalar(row, row, gates[:, 0, t:t + 1], None, ALU.mult))
                chain.link(V.scalar_tensor_tensor(row, yg[:, 1, t, :], gates[:, 1, t:t + 1], row,
                                                  ALU.mult, ALU.add))
                chain.link(V.scalar_tensor_tensor(row, x1[:, t, :], ALPHA, row, ALU.mult, ALU.add))
                normalise(TT + t, row, ln2_gb, out_ready)


def _std(act, t, var_done, std_done, stat):
    act.wait_ge(var_done, t + 1)
    act.activation(stat[:, 15:16], stat[:, 14:15], ACT.Sqrt).then_inc(std_done, 1)


def _tile(buf, j):
    if isinstance(j, int):
        return buf[:, j, :]
    return buf[:, ds(j, 1), :].rearrange("p a s -> p (a s)")


def _col(buf, c0, j):
    if isinstance(j, int):
        return buf[:, c0 + j:c0 + j + 1]
    return buf[:, ds(j + c0, 1)]


_INS = ["x", "w_in", "conv_a_w", "w_branch_a", "conv_r_w", "conv_r_b", "w_rg_a", "b_rg_a", "w_rg_x",
        "b_rg_x", "rg_lambda", "w_branch_r", "w_out", "ln1_g", "ln1_b", "w_router", "b_router",
        "w_exp_gate", "w_exp_up", "w_exp_down", "ln2_g", "ln2_b"]


def kernel(**inputs):
    import numpy as _np
    import concourse.bacc as _bacc
    from concourse import mybir as _mybir
    from concourse.bass_utils import run_bass_kernel_spmd as _run

    nc = _bacc.Bacc("TRN2", target_bir_lowering=False, num_devices=1)
    arrays, args = {}, []
    for name in _INS:
        a = _np.ascontiguousarray(inputs[name])
        arrays[f"in_{name}_dram"] = a
        args.append(nc.dram_tensor(f"in_{name}_dram", a.shape, _mybir.dt.from_np(a.dtype), kind="ExternalInput").ap())
    shape = inputs["x"].shape
    args.append(nc.dram_tensor("out_dram", shape, _mybir.dt.float32, kind="ExternalOutput").ap())
    trunk_moe(nc, *args)
    r = _run(nc, [arrays], core_ids=[0])
    return r.results[0]["out_dram"]
```

```python
from contextlib import ExitStack

import concourse.bass as bass
from concourse import mybir

P = 128
F32 = mybir.dt.float32
F32R = mybir.dt.float32r
BF16 = mybir.dt.bfloat16
I32 = mybir.dt.int32
U32 = mybir.dt.uint32
ACT = mybir.ActivationFunctionType
ALU = mybir.AluOpType
AX = mybir.AxisListType.X
ds = bass.ds
KIB = 1024
LN_EPS = 1e-5
GELU_A = 0.044715
GELU_S = 2.0 * 0.7978845608028654


class Chain:

    def __init__(self, eng, sem):
        self.eng, self.sem, self.n = eng, sem, 0

    def link(self, ins):
        ins.then_inc(self.sem, 1)
        self.n = self.n + 1
        self.eng.wait_ge(self.sem, self.n)

    def loop(self, trips, body, per):
        start = self.n
        with self.eng.Fori(0, trips) as i:
            self.n = i * per + start
            body(i)
        self.n = start + trips * per


def trunk_moe(nc, x, w_in, conv_a_w, w_branch_a, conv_r_w, conv_r_b, w_rg_a, b_rg_a, w_rg_x, b_rg_x,
              rg_lambda, w_branch_r, w_out, ln1_g, ln1_b, w_router, b_router,
              w_exp_gate, w_exp_up, w_exp_down, ln2_g, ln2_b, out):
    _, S, D = x.shape
    DR = conv_r_b.shape[1]
    NE, DF = w_exp_gate.shape[1], w_exp_gate.shape[3]
    GRP = 4
    NG = NE // GRP
    KD, KR, KF = D // P, DR // P, DF // P
    TT = S // P
    ALPHA = 2.0 ** 0.25
    BLOCKS = NE + (2 * S - 1) // (P + 1)
    ZEROS = 16 * (2 * BLOCKS - NE)
    assert (S, D, DR, NE, DF) == (512, 1024, 1280, 16, 512)

    COL_H, COL_B, COL_C = 0, D, 2 * D
    COL_XR, COL_YR = 3 * D, 3 * D + DR
    COL_GA, COL_GR = 3 * D + 2 * DR, 4 * D + 2 * DR

    N_XR = 0
    N_A = N_XR + KR
    N_BA = N_A + 3 * KD
    N_YR = N_BA + KD
    N_GA = N_YR + KR
    N_GR = N_GA + KD
    N_BR = N_GR + KD
    N_O = N_BR + KD
    HALVES = 2
    N_END = N_O + HALVES * KD
    SH = S // HALVES

    x2 = x.rearrange("a s d -> (a s) d")
    out2 = out.rearrange("a s d -> (a s) d")
    win_v = w_in[0].rearrange("(k p) n -> p k n", p=P)
    wba_v = w_branch_a[0].rearrange("(k p) n -> p k n", p=P)
    wbr_v = w_branch_r[0].rearrange("(k p) n -> p k n", p=P)
    wout_v = w_out[0].rearrange("(k p) n -> p k n", p=P)

    xs = nc.dram_tensor("xs", (BLOCKS * P, D), F32, kind="Internal").ap()
    ys = nc.dram_tensor("ys", (BLOCKS * P, D), F32, kind="Internal").ap()

    with ExitStack() as ctx:
        base = (nc.sbuf_base + 31) // 32 * 32

        def at(name, kib, shape, dt=F32):
            return nc.alloc_sbuf_tensor_at(name, shape, dt, offset=base + int(kib * KIB))

        def sem(name):
            return ctx.enter_context(nc.semaphore(name))

        zbuf = at("zbuf", 0, [P, KR, S])
        tbuf = at("tbuf", 20, [P, KR, S])
        ibuf = at("ibuf", 40, [P, KR, S])
        hg_hi = at("hg_hi", 20, [P, KR, S], F32R)
        hg_lo = at("hg_lo", 40, [P, KR, S], F32R)
        u_hi = at("u_hi", 60, [P, KD, S], F32R)
        u_lo = at("u_lo", 76, [P, KD, S], F32R)
        sgr = at("sgr", 60, [P, KD, S])
        ya = at("ya", 92, [P, KD, S])
        zero = at("zero", 92, [P, D])
        rg_st = [at(f"rg_st{p}", 96 + p, [P, 2, P]) for p in range(2)]
        rg_hi = [at(f"rg_hi{p}", 98 + p, [P, 2, P], F32R) for p in range(2)]
        rg_lo = [at(f"rg_lo{p}", 100 + p, [P, 2, P], F32R) for p in range(2)]
        rows = at("rows", 102, [P, P])
        wst = [at(f"wst{p}", 108 + 5 * p, [P, KR, P]) for p in range(2)]
        whi = [at(f"whi{p}", 118 + 5 * p, [P, KR, P], F32R) for p in range(2)]
        wlo = [at(f"wlo{p}", 128 + 5 * p, [P, KR, P], F32R) for p in range(2)]
        xT_hi = at("xT_hi", 138, [P, KD, S], F32R)
        xT_lo = at("xT_lo", 154, [P, KD, S], F32R)
        mg_hi = at("mg_hi", 138, [P, KD, S], F32R)
        mg_lo = at("mg_lo", 154, [P, KD, S], F32R)
        tmp = [at(f"tmp{i}", 170 + 2 * i, [P, S]) for i in range(8)]
        xc = [tmp[0], tmp[1]]
        xc_hi = at("xc_hi", 174, [P, S], F32R)
        xc_lo = at("xc_lo", 176, [P, S], F32R)
        ig = [tmp[4], tmp[5]]
        yr = [tmp[0], tmp[6]]
        yT = at("yT", 170, [P, KD, S])
        x1 = at("x1", 186, [P, TT, D])
        ident = at("ident", 202, [P, P])
        before = at("before", 202.5, [P, P])
        ones = at("ones", 203, [P, P])
        chan = at("chan", 203.5, [P, P])
        wr = at("wr", 204, [P, KD, NE])
        decay = at("decay", 204.5, [P, 8, KR])
        brow = at("brow", 204.875, [P, NE])
        iota_e = at("iota_e", 204.9375, [P, NE])
        stat = at("stat", 206, [P, 48])
        gates = at("gates", 205.125, [P, 2, TT])
        dest = at("dest", 205.1875, [P, 2, TT], U32)
        ones_b = at("ones_b", 205.5, [P, P], BF16)
        before_b = at("before_b", 205.75, [P, P], BF16)
        plan = at("plan", 205.25, [P, 8], I32)
        r16 = [at(f"r16_{i}", 154 + 0.25 * i, [P, TT, NE]) for i in range(20)]
        r4 = [at(f"r4_{i}", 159.5 + 0.0625 * i, [P, TT, NG]) for i in range(8)]
        r1 = [at(f"r1_{i}", 160 + 0.015625 * 2 * i, [P, TT]) for i in range(16)]
        sel = at("sel", 161, [P, TT, NE], BF16)
        r6 = at("r6", 161.25, [P, TT, NG, 6])
        onehot = at("onehot", 155.25, [P, 2, TT, NE])
        chosen = at("chosen", 155.75, [P, 2, TT, NE])
        rowsum = at("rowsum", 161.75, [P, 2, TT])
        x1T = at("x1T", 138, [P, TT, KD, P])
        ln1_gb = at("ln1_gb", 40, [P, 2, D])
        est = [at(f"est{s}", 8 * s, [P, 4, DF]) for s in range(6)]
        ehi = [at(f"ehi{s}", o, [P, 4, DF], F32R) for s, o in enumerate([48, 56, 64, 72, 108, 170])]
        elo = [at(f"elo{s}", o, [P, 4, DF], F32R) for s, o in enumerate([80, 88, 96, 116, 124, 178])]
        xe = at("xe", 138, [P, D])
        xe_hi = at("xe_hi", 142, [P, KD, P], F32R)
        xe_lo = at("xe_lo", 146, [P, KD, P], F32R)
        sg = at("sg", 150, [P, DF])
        hb = at("hb", 152, [P, DF])
        hT_hi = at("hT_hi", 154, [P, KF, P], F32R)
        hT_lo = at("hT_lo", 156, [P, KF, P], F32R)
        yb = at("yb", 158, [P, D])
        ln2_gb = at("ln2_gb", 162, [P, 2, D])
        yg = at("yg", 0, [P, 2, TT, D])

        pairs = [ctx.enter_context(nc.psum_tensor(f"ps{n}", [P, 2, S], F32)) for n in "CDAB"]
        psC = pairs[0:2]
        psA, psB = ([pair[:, i, :] for i in range(2)] for pair in pairs[2:4])
        ps6 = [psB[0], psB[1], psC[0][:, 0, :], psC[0][:, 1, :], psC[1][:, 0, :], psC[1][:, 1, :]]

        x_landed = [sem(f"x_landed{t}") for t in range(TT)]
        sp_step = sem("sp_step")
        rows_landed = sem("rows_landed")
        small_landed = sem("small_landed")
        masks = sem("masks")
        pool_step = sem("pool_step")
        chan_t = sem("chan_t")
        chan_ready = sem("chan_ready")
        decay_act = sem("decay_act")
        decay_dve = sem("decay_dve")
        xt_t = sem("xt_t")
        xt_hi = sem("xt_hi")
        xt_lo = sem("xt_lo")
        w_landed = [sem(f"w_landed{p}") for p in range(2)]
        w_hi = sem("w_hi")
        w_lo = sem("w_lo")
        tile_done = sem("tile_done")
        rg_landed = [sem(f"rg_landed{p}") for p in range(2)]
        rgw_hi = sem("rgw_hi")
        rgw_lo = sem("rgw_lo")
        xc_start = sem("xc_start")
        xc_done = sem("xc_done")
        xc_h = sem("xc_h")
        xc_l = sem("xc_l")
        rg_done = sem("rg_done")
        gate_done = sem("gate_done")
        ix_done = sem("ix_done")
        c_read = sem("c_read")
        v_done = sem("v_done")
        t_start = sem("t_start")
        u_done = sem("u_done")
        u_h = sem("u_h")
        u_l = sem("u_l")
        a_done = sem("a_done")
        sq_done = sem("sq_done")
        bt_done = sem("bt_done")
        ya_done = sem("ya_done")
        y_sq = sem("y_sq")
        y_q = sem("y_q")
        y_sig = sem("y_sig")
        hg_done = sem("hg_done")
        hg_h = sem("hg_h")
        hg_l = sem("hg_l")
        ga_read = sem("ga_read")
        m_done = sem("m_done")
        gr_read = sem("gr_read")
        mf_done = sem("mf_done")
        mg_h = sem("mg_h")
        mg_l = sem("mg_l")
        yT_done = sem("yT_done")
        ln1_landed = sem("ln1_landed")
        y_t = sem("y_t")
        res_done = sem("res_done")
        stats_done = sem("stats_done")
        var_done = sem("var_done")
        std_done = sem("std_done")
        x1_done = sem("x1_done")
        x1_t = sem("x1_t")
        x1T_done = sem("x1T_done")
        logit_done = sem("logit_done")
        lmax_done = sem("lmax_done")
        exp_done = sem("exp_done")
        sel_done = sem("sel_done")
        pos_done = sem("pos_done")
        dest_done = sem("dest_done")
        plan_done = sem("plan_done")
        zero_done = sem("zero_done")
        scat = sem("scat")
        dve_step = sem("dve_step")
        e_landed = [sem(f"e_landed{s}") for s in range(6)]
        gu_hi = sem("gu_hi")
        gu_lo = sem("gu_lo")
        gu_used = sem("gu_used")
        d_hi = sem("d_hi")
        d_lo = sem("d_lo")
        d_used = sem("d_used")
        xe_landed = sem("xe_landed")
        xe_t = sem("xe_t")
        xe_h = sem("xe_h")
        xe_l = sem("xe_l")
        silu_done = sem("silu_done")
        h_done = sem("h_done")
        h_t = sem("h_t")
        h_h = sem("h_h")
        h_l = sem("h_l")
        y_evac = sem("y_evac")
        y_stored = sem("y_stored")
        all_stored = sem("all_stored")
        ln2_landed = sem("ln2_landed")
        got = [sem(f"got{t}") for t in range(TT)]
        x1_scaled = sem("x1_scaled")
        out_ready = sem("out_ready")
        stored = sem("stored")

        C_CA = lambda k, j: k * KD + j
        C_CR = lambda k, j: 3 * KD + k * KR + j
        C_CB = 3 * KD + 4 * KR
        C_BA, C_BX, C_LAM = C_CB + KR, C_CB + 2 * KR, C_CB + 3 * KR
        NROW = C_LAM + KR

        block = ctx.enter_context(nc.Block())

        def load_expert(sp, b, s, expert=None, again=False):
            if again or b > 0:
                if s < 4:
                    sp.wait_ge(gu_lo, b * 4 + (s - 3))
                else:
                    sp.wait_ge(d_lo, b * 2 + (s - 5))
            if expert is not None:
                sp.wait_ge(gu_lo, 4 * NE)
            e = b if expert is None else expert
            w = (w_exp_gate, w_exp_up, w_exp_down)[s // 2]
            w = w[0, e] if isinstance(e, int) else w[0, ds(e, 1)].rearrange("a k n -> (a k) n")
            if s < 4:
                src = w.rearrange("(k p) n -> p k n", p=P)[:, 4 * (s % 2):4 * (s % 2) + 4, :]
            else:
                src = w.rearrange("(k p) n -> p k n", p=P)[:, :, (s - 4) * DF:(s - 3) * DF]
            sp.dma_start(est[s][:], src).then_inc(e_landed[s], 16)

        @block.sync
        def _(sp):
            for t in range(TT):
                sp.dma_start(x1[:, t, :], x2[t * P:(t + 1) * P, :]).then_inc(x_landed[t], 16)

            def load(N, p, src, K=KD):
                if not (isinstance(N, int) and N < 2):
                    sp.wait_ge(w_lo, N - 1)
                    sp.sem_inc(sp_step, 1)
                sp.dma_start(wst[p][:, 0:K, :], src).then_inc(w_landed[p], 16)

            def part(view, c0, j):
                if isinstance(j, int):
                    return view[:, :, c0 + j * P:c0 + (j + 1) * P]
                return view[:, :, ds(j * P + c0, P)]

            def load_rg(j, p):
                if not (isinstance(j, int) and j < 2):
                    sp.wait_ge(rgw_lo, j - 1)
                wa = w_rg_a[0, j] if isinstance(j, int) else w_rg_a[0, ds(j, 1)].rearrange("a i o -> (a i) o")
                wx = w_rg_x[0, j] if isinstance(j, int) else w_rg_x[0, ds(j, 1)].rearrange("a i o -> (a i) o")
                sp.dma_start(rg_st[p][:, 0, :], wa).then_inc(rg_landed[p], 16)
                sp.dma_start(rg_st[p][:, 1, :], wx).then_inc(rg_landed[p], 16)

            load(0, 0, part(win_v, COL_XR, 0))
            r = 0
            for src, n in ((conv_a_w[0].rearrange("k (j c) -> (k j) c", c=P), 3 * KD),
                           (conv_r_w[0].rearrange("k (j c) -> (k j) c", c=P), 4 * KR),
                           (conv_r_b[0].rearrange("(j c) -> j c", c=P), KR),
                           (b_rg_a[0], KR), (b_rg_x[0], KR),
                           (rg_lambda[0].rearrange("(j c) -> j c", c=P), KR)):
                sp.dma_start(rows[r:r + n, :], src).then_inc(rows_landed, 16)
                r += n
            load(1, 1, part(win_v, COL_XR, 1))
            load_rg(0, 0)
            load_rg(1, 1)
            sp.dma_start(wr[:], w_router.rearrange("(k p) e -> p k e", p=P)).then_inc(small_landed, 16)
            sp.dma_start(brow[:], b_router.rearrange("(a e) -> a e", a=1).to_broadcast([P, NE])
                         ).then_inc(small_landed, 16)
            with sp.Fori(1, KR // 2) as i:
                for p in range(2):
                    load(2 * i + p, p, part(win_v, COL_XR, 2 * i + p))
                    load_rg(2 * i + p, p)
            with sp.Fori(0, KD // 2) as i:
                for m in range(6):
                    c0 = (COL_C, COL_H, COL_B)[m % 3]
                    load(6 * i + (N_A + m), m % 2, part(win_v, c0, 2 * i + m // 3))
            for N0, view, c0, trips in ((N_BA, wba_v, 0, KD), (N_YR, win_v, COL_YR, KR),
                                        (N_GA, win_v, COL_GA, KD), (N_GR, win_v, COL_GR, KD),
                                        (N_BR, wbr_v, 0, KD)):
                with sp.Fori(0, trips // 2) as i:
                    for p in range(2):
                        load(2 * i + (N0 + p), p, part(view, c0, 2 * i + p), K=view.shape[1])
                if N0 == N_GA:
                    sp.wait_ge(hg_done, KR)
                    load_expert(sp, 0, 0)
                    load_expert(sp, 0, 1)
            for n in range(HALVES * KD):
                load(N_O + n, n % 2, part(wout_v, 0, n % KD))
                if n == 2:
                    sp.wait_ge(tile_done, N_O)
                    for q, v in enumerate((ln1_g, ln1_b)):
                        sp.dma_start(ln1_gb[:, q, :], v.to_broadcast([P, D])).then_inc(ln1_landed, 16)
                if n in (4, 6, 8):
                    load_expert(sp, 0, n // 2)
            for s in range(3):
                load_expert(sp, 1, s)
            sp.wait_ge(x1_done, TT)
            load_expert(sp, 0, 5)
            load_expert(sp, 1, 3)
            with sp.Fori(2, NE) as b:
                for s in range(4):
                    load_expert(sp, b, s, again=True)
                for s in (4, 5):
                    load_expert(sp, b - 1, s, again=True)
            for s in (4, 5):
                load_expert(sp, NE - 1, s)
            sp.wait_ge(plan_done, 1)
            more = sp.value_load(plan[0:1, 7:8], min_val=0, max_val=BLOCKS - NE)
            with sp.If(more > 0):
                with sp.Fori(0, more) as i:
                    e = sp.value_load(plan[0:1, ds(i, 1)], min_val=0, max_val=NE - 1)
                    for s in range(6):
                        load_expert(sp, i + NE, s, expert=e, again=True)
            for t in range(TT):
                sp.wait_ge(out_ready, t + 1)
                sp.dma_start(out2[t * P:(t + 1) * P, :], yg[:, 0, t, :]).then_inc(stored, 16)
            sp.wait_ge(stored, 16 * TT)

        @block.gpsimd
        def _(pool):
            nc.gpsimd.memset(ones[:], 1.0).then_inc(pool_step, 1)
            nc.gpsimd.memset(zero[:], 0.0).then_inc(pool_step, 1)
            nc.gpsimd.iota(iota_e[:], pattern=[[1, NE]], base=0, channel_multiplier=0,
                           allow_small_or_imprecise_dtypes=True).then_inc(pool_step, 1)
            pool.wait_ge(pool_step, 3)
            nc.gpsimd.affine_select(out=ident[:], in_=ones[:], compare_op=ALU.is_equal, fill=0.0,
                                    base=0, pattern=[[-1, P]], channel_multiplier=1).then_inc(masks, 1)
            nc.gpsimd.affine_select(out=before[:], in_=ones[:], compare_op=ALU.is_gt, fill=0.0,
                                    base=0, pattern=[[1, P]], channel_multiplier=-1).then_inc(masks, 1)
            pool.wait_ge(masks, 2)
            nc.gpsimd.tensor_copy(before_b[:], before[:]).then_inc(masks, 1)
            nc.gpsimd.tensor_copy(ones_b[:], ones[:]).then_inc(masks, 1)
            with pool.Fori(0, BLOCKS) as b:
                pool.wait_ge(tile_done, b + 1)
                pool.dma_start(xs[ds(b * P, P), :], zero[:]).then_inc(zero_done, 16)
            with pool.Fori(NE, BLOCKS) as b:
                pool.wait_ge(tile_done, b + (BLOCKS - NE + 1))
                pool.dma_start(ys[ds(b * P, P), :], zero[:]).then_inc(zero_done, 16)
            pool.wait_ge(zero_done, ZEROS)
            pool.wait_ge(dest_done, 1)
            for t in range(TT):
                for n in range(2):
                    pool.indirect_dma_start(
                        out=xs, out_offset=bass.IndirectOffsetOnAxis(ap=dest[:, n, t:t + 1], axis=0),
                        in_=x1[:, t, :], in_offset=None).then_inc(scat, 16)
            pool.wait_ge(scat, 16 * 2 * TT)

            def load_rows(b, first=False):
                if not first:
                    pool.wait_ge(xe_t, b)
                    pool.wait_ge(xe_t, 1)
                src = xs[b * P:(b + 1) * P, :] if isinstance(b, int) else xs[ds(b * P, P), :]
                pool.dma_start(xe[:], src).then_inc(xe_landed, 16)

            load_rows(0, first=True)
            for n, v in enumerate((ln2_g, ln2_b)):
                pool.dma_start(ln2_gb[:, n, :], v.to_broadcast([P, D])).then_inc(ln2_landed, 16)
            load_rows(1)
            with pool.Fori(1, NE - 1) as b:
                load_rows(b + 1)
            pool.wait_ge(plan_done, 1)
            more = pool.value_load(plan[0:1, 7:8], min_val=0, max_val=BLOCKS - NE)
            with pool.If(more > 0):
                with pool.Fori(0, more) as i:
                    load_rows(i + NE)
            pool.wait_ge(all_stored, 1)
            for t in range(TT):
                for n in range(2):
                    pool.indirect_dma_start(
                        out=yg[:, n, t, :], out_offset=None, in_=ys,
                        in_offset=bass.IndirectOffsetOnAxis(ap=dest[:, n, t:t + 1], axis=0)
                    ).then_inc(got[t], 16)

        @block.tensor
        def _(pe):
            pe.wait_ge(masks, 2)
            for t in range(TT):
                pe.wait_ge(x_landed[t], 16)
                for k in range(KD):
                    mm = pe.transpose(pairs[t][:, k // 4, (k % 4) * P:(k % 4 + 1) * P],
                                      x1[:, t, k * P:(k + 1) * P], ident[:])
                mm.then_inc(xt_t, 1)
            pe.wait_ge(rows_landed, 16 * 6)
            pe.wait_ge(xt_lo, TT)
            pe.transpose(psB[0][:, 0:NROW], rows[0:NROW, :], ident[0:NROW, 0:NROW]).then_inc(chan_t, 1)

            def product(bank, stat, moving, K):
                (s_hi, s_lo), (m_hi, m_lo) = stat, moving
                for k in range(K):
                    pe.matmul(bank, s_hi[:, k, :], m_hi[:, k, :], start=(k == 0), stop=False)
                    pe.matmul(bank, s_hi[:, k, :], m_lo[:, k, :], start=False, stop=False)
                    mm = pe.matmul(bank, s_lo[:, k, :], m_hi[:, k, :], start=False, stop=(k == K - 1))
                return mm

            def tile(N, p, bank, moving, K=KD):
                pe.wait_ge(w_lo, N + 1)
                product(bank, (whi[p], wlo[p]), moving, K).then_inc(tile_done, 1)

            def xr(j, p, first=False):
                if not first:
                    pe.wait_ge(xc_done, j - 1)
                tile(j, p, psA[p], (xT_hi, xT_lo))

            def rg(j, p, first=False):
                pe.wait_ge(xc_l, j + 1)
                pe.wait_ge(rgw_lo, j + 1)
                if not first:
                    pe.wait_ge(gate_done, j)
                for n in range(2):
                    pe.matmul(psB[n], rg_hi[p][:, n, :], xc_hi[:], start=True, stop=False)
                    pe.matmul(psB[n], rg_hi[p][:, n, :], xc_lo[:], start=False, stop=False)
                    mm = pe.matmul(psB[n], rg_lo[p][:, n, :], xc_hi[:], start=False, stop=True)
                mm.then_inc(rg_done, 1)

            xr(0, 0, first=True)
            xr(1, 1, first=True)
            pe.wait_ge(chan_ready, 1)
            rg(0, 0, first=True)
            with pe.Fori(1, KR // 2) as i:
                xr(2 * i, 0)
                rg(2 * i - 1, 1)
                xr(2 * i + 1, 1)
                rg(2 * i, 0)
            rg(KR - 1, 1)
            pe.wait_ge(gate_done, KR)
            pe.wait_ge(xt_lo, TT)
            for m in range(6):
                tile(N_A + m, m % 2, ps6[m], (xT_hi, xT_lo))
            with pe.Fori(1, KD // 2) as i:
                for m in range(6):
                    if m % 3 == 0:
                        pe.wait_ge(u_done, 2 * i + (m // 3 - 1))
                    tile(6 * i + (N_A + m), m % 2, ps6[m], (xT_hi, xT_lo))
            pe.wait_ge(xc_done, KR)
            pe.wait_ge(u_l, KD)
            for N0, bank, moving, read, K in (
                    (N_BA, psA, (u_hi, u_lo), ya_done, KD),
                    (N_YR, psB, (xT_hi, xT_lo), y_sq, KD),
                    (N_GA, psA, (xT_hi, xT_lo), ga_read, KD),
                    (N_GR, psB, (xT_hi, xT_lo), gr_read, KD),
                    (N_BR, psA, (hg_hi, hg_lo), mf_done, KR)):
                if N0 == N_GA:
                    pe.wait_ge(ya_done, KD)
                if N0 == N_GR:
                    pe.wait_ge(hg_done, KR)
                if N0 == N_BR:
                    pe.wait_ge(ga_read, KD)
                    pe.wait_ge(hg_l, KR)
                n = KR if N0 == N_YR else KD
                for p in range(2):
                    tile(N0 + p, p, bank[p], moving, K)
                with pe.Fori(1, n // 2) as i:
                    for p in range(2):
                        pe.wait_ge(read, 2 * i + (p - 1))
                        tile(2 * i + (N0 + p), p, bank[p], moving, K)

            def back(t):
                if t >= 2:
                    pe.wait_ge(res_done, t - 1)
                for k in range(KD):
                    mm = pe.transpose(psC[t % 2][:, k // 4, (k % 4) * P:(k % 4 + 1) * P],
                                      yT[:, k, t * P:(t + 1) * P], ident[:])
                mm.then_inc(y_t, 1)

            def x1_back(t):
                pe.wait_ge(x1_done, t + 1)
                if t >= 1:
                    pe.wait_ge(x1T_done, t)
                for k in range(KD):
                    mm = pe.transpose(psA[k // 4][:, (k % 4) * P:(k % 4 + 1) * P],
                                      x1[:, t, k * P:(k + 1) * P], ident[:])
                mm.then_inc(x1_t, 1)

            def router(t):
                pe.wait_ge(x1T_done, t + 1)
                for k in range(KD):
                    mm = pe.matmul(psB[0][:, t * NE:(t + 1) * NE], x1T[:, t, k, :], wr[:, k, :],
                                   start=(k == 0), stop=(k == KD - 1))
                mm.then_inc(logit_done, 1)

            pe.wait_ge(gr_read, KD)
            pe.wait_ge(mg_l, KD)
            pe.wait_ge(small_landed, 32)
            for h in range(HALVES):
                half = [buf[:, :, h * SH:(h + 1) * SH] for buf in (mg_hi, mg_lo)]
                for j in range(KD):
                    n = h * KD + j
                    if n >= 2:
                        pe.wait_ge(yT_done, n - 1)
                    tile(N_O + n, n % 2, psB[n % 2][:, 0:SH], half)
                    if n == KD:
                        pe.wait_ge(yT_done, KD)
                        back(0)
                        back(1)
            pe.wait_ge(yT_done, HALVES * KD)
            back(2)
            back(3)
            for t in range(TT):
                x1_back(t)
                router(t)
            pe.wait_ge(sel_done, 1)
            pe.wait_ge(masks, 4)
            for t in range(TT):
                for q in range(t):
                    pe.matmul(psB[1][:, t * NE:(t + 1) * NE], ones_b[:], sel[:, q, :],
                              start=(q == 0), stop=False)
                pe.matmul(psB[1][:, t * NE:(t + 1) * NE], before_b[:], sel[:, t, :], start=(t == 0), stop=True)
            for q in range(TT):
                mm = pe.matmul(psB[1][:, TT * NE:(TT + 1) * NE], ones_b[:], sel[:, q, :],
                               start=(q == 0), stop=(q == TT - 1))
            mm.then_inc(pos_done, 1)

            def rows_t(b, first=False):
                pe.wait_ge(xe_landed, b * 16 + 16)
                if not first:
                    pe.wait_ge(xe_l, b)
                for k in range(KD):
                    mm = pe.transpose(psC[0][:, k // 4, (k % 4) * P:(k % 4 + 1) * P],
                                      xe[:, k * P:(k + 1) * P], ident[:])
                mm.then_inc(xe_t, 1)

            def gate_up(b, first=False):
                pe.wait_ge(xe_l, b + 1)
                for s in range(4):
                    if s % 2 == 0 and not first:
                        pe.wait_ge((silu_done, h_done)[s // 2], b)
                    pe.wait_ge(gu_lo, b * 4 + (s + 1))
                    for k in range(4):
                        q = 4 * (s % 2) + k
                        pe.matmul(psA[s // 2], xe_hi[:, q, :], ehi[s][:, k, :], start=(q == 0), stop=False)
                        pe.matmul(psA[s // 2], xe_hi[:, q, :], elo[s][:, k, :], start=False, stop=False)
                        mm = pe.matmul(psA[s // 2], xe_lo[:, q, :], ehi[s][:, k, :], start=False,
                                       stop=(q == KD - 1))
                    mm.then_inc(gu_used, 1)

            def hidden_t(b, first=False):
                pe.wait_ge(h_done, b + 1)
                if not first:
                    pe.wait_ge(h_l, b)
                for k in range(KF):
                    mm = pe.transpose(psC[1][:, 0, k * P:(k + 1) * P], hb[:, k * P:(k + 1) * P], ident[:])
                mm.then_inc(h_t, 1)

            def down(b, first=False):
                pe.wait_ge(h_l, b + 1)
                for s in range(2):
                    if not first:
                        pe.wait_ge(y_evac, b * 2 + (s - 1))
                    pe.wait_ge(d_lo, b * 2 + (s + 1))
                    for k in range(KF):
                        pe.matmul(psB[s], hT_hi[:, k, :], ehi[4 + s][:, k, :], start=(k == 0), stop=False)
                        pe.matmul(psB[s], hT_hi[:, k, :], elo[4 + s][:, k, :], start=False, stop=False)
                        mm = pe.matmul(psB[s], hT_lo[:, k, :], ehi[4 + s][:, k, :], start=False,
                                       stop=(k == KF - 1))
                    mm.then_inc(d_used, 1)

            pe.wait_ge(dest_done, 1)
            rows_t(0, first=True)
            gate_up(0, first=True)
            rows_t(1)
            hidden_t(0, first=True)
            gate_up(1)
            rows_t(2)
            down(0, first=True)
            hidden_t(1)
            with pe.Fori(2, NE - 1) as b:
                gate_up(b)
                rows_t(b + 1)
                down(b - 1)
                hidden_t(b)
            gate_up(NE - 1)
            down(NE - 2)
            hidden_t(NE - 1)
            down(NE - 1)
            pe.wait_ge(plan_done, 1)
            more = pe.value_load(plan[0:1, 7:8], min_val=0, max_val=BLOCKS - NE)
            with pe.If(more > 0):
                with pe.Fori(0, more) as i:
                    rows_t(i + NE)
                    gate_up(i + NE)
                    hidden_t(i + NE)
                    down(i + NE)

        @block.scalar
        def _(act):
            A = nc.scalar.activation

            def hi(N, p, K=KD, first=False):
                n, half = N
                act.wait_ge(w_landed[p], half * 16 + 16)
                if not first:
                    act.wait_ge(tile_done, n - 1)
                A(whi[p][:, 0:K, :], wst[p][:, 0:K, :], ACT.Copy).then_inc(w_hi, 1)

            for t in range(TT):
                act.wait_ge(xt_t, t + 1)
                A(xT_hi[:, :, t * P:(t + 1) * P], pairs[t][:].rearrange("p a (b c) -> p (a b) c", c=P),
                  ACT.Copy).then_inc(xt_hi, 1)
                if t == 2:
                    hi((0, 0), 0, first=True)
            hi((1, 0), 1, first=True)
            act.wait_ge(chan_ready, 1)
            A(decay[:, 1, :], chan[:, C_LAM:C_LAM + KR], ACT.Abs).then_inc(decay_act, 1)
            act.wait_ge(decay_act, 1)
            A(decay[:, 2, :], decay[:, 1, :], ACT.Exp, scale=-1.0).then_inc(decay_act, 1)

            def conv_start(j, p, first=False):
                act.wait_ge(tile_done, j + 1)
                if not first:
                    act.wait_ge(ix_done, j - 1)
                A(xc[p][:], psA[p], ACT.Identity, bias=_col(chan, C_CB, j),
                  scale=_col(chan, C_CR(3, 0), j)).then_inc(xc_start, 1)

            def rg_round(j, p, first=False):
                j, half = j
                act.wait_ge(rg_landed[p], half * 32 + 32)
                if not first:
                    act.wait_ge(rg_done, j - 1)
                A(rg_hi[p][:], rg_st[p][:], ACT.Copy).then_inc(rgw_hi, 1)

            def xc_round(j, p, first=False):
                act.wait_ge(xc_done, j + 1)
                if not first:
                    act.wait_ge(rg_done, j)
                A(xc_hi[:], xc[p][:], ACT.Copy).then_inc(xc_h, 1)

            def sigmoids(j, p, first=False):
                act.wait_ge(rg_done, j + 1)
                if not first:
                    act.wait_ge(ix_done, j - 1)
                A(_tile(zbuf, j), psB[0], ACT.Sigmoid, bias=_col(chan, C_BA, j))
                A(ig[p][:], psB[1], ACT.Sigmoid, bias=_col(chan, C_BX, j)).then_inc(gate_done, 1)

            rg_round((0, 0), 0, first=True)
            rg_round((1, 0), 1, first=True)
            conv_start(0, 0, first=True)
            hi((2, 1), 0)
            xc_round(0, 0, first=True)

            conv_start(1, 1, first=True)
            hi((3, 1), 1)
            sigmoids(0, 0, first=True)
            xc_round(1, 1)
            with act.Fori(1, KR // 2) as i:
                for p in range(2):
                    rg_round((2 * i + p, i), p)
                    conv_start(2 * i + p, p)
                    hi((2 * i + (p + 2), i + 1), p)
                    sigmoids(2 * i + (p - 1), 1 - p)
                    xc_round(2 * i + p, p)
            sigmoids(KR - 1, 1)

            QC = KR * S // 4
            zf = zbuf[:].rearrange("p j s -> p (j s)")
            tf = tbuf[:].rearrange("p j s -> p (j s)")
            act.wait_ge(ix_done, KR)
            with act.Fori(0, KD // 2) as i:
                for q in range(2):
                    j, m = 2 * i + q, 3 * q
                    N = lambda n: (6 * i + (N_A + m + n), 3 * i + (N_A + m + n) // 2)
                    act.wait_ge(tile_done, 6 * i + (N_A + m + 1))
                    act.wait_ge(v_done, j)
                    A(tmp[0][:], ps6[m], ACT.Copy).then_inc(c_read, 1)
                    hi(N(2), m % 2)
                    hi(N(3), (m + 1) % 2)
                    act.wait_ge(v_done, j + 1)
                    act.wait_ge(u_done, j)
                    A(tmp[2][:], tmp[1][:], ACT.Identity, bias=0.0, scale=_col(chan, C_CA(2, 0), j)).then_inc(t_start, 1)
                    if q == 0:
                        A(tf[:, ds(i * QC, QC)], zf[:, ds(i * QC, QC)], ACT.Tanh, scale=-0.5)
                        A(zf[:, ds(i * QC, QC)], zf[:, ds(i * QC, QC)], ACT.Exp).then_inc(a_done, 1)
                    hi(N(4), m % 2)
                    act.wait_ge(u_done, j + 1)
                    A(_tile(u_hi, j), tmp[3][:], ACT.Copy).then_inc(u_h, 1)
            act.wait_ge(zero_done, ZEROS)
            with act.Fori(0, KD // 2) as i:
                for p in range(2):
                    act.wait_ge(tile_done, 2 * i + (N_BA + p + 1))
                    A(_tile(ya, 2 * i + p), psA[p], ACT.Copy).then_inc(ya_done, 1)
                    hi((2 * i + (N_BA + p + 2), i + (N_BA + p + 2) // 2), p)
                    if p == 0:
                        act.wait_ge(a_done, i + 1)
                        A(tf[:, ds(i * QC, QC)], tf[:, ds(i * QC, QC)], ACT.Sqrt).then_inc(sq_done, 1)
            act.wait_ge(bt_done, 4)
            with act.Fori(0, KR // 2) as i:
                for p in range(2):
                    j = 2 * i + p
                    act.wait_ge(tile_done, 2 * i + (N_YR + p + 1))
                    act.wait_ge(hg_done, 2 * i)
                    A(yr[p][:], psB[p], ACT.Copy).then_inc(y_sq, 1)
                    hi((2 * i + (N_YR + p + 2), i + (N_YR + p + 2) // 2), p)
                    act.wait_ge(y_q, j + 1)
                    A(tmp[2][:], tmp[1][:], ACT.Sigmoid, scale=GELU_S * GELU_A).then_inc(y_sig, 1)
                    act.wait_ge(hg_done, j + 1)
                    A(_tile(hg_hi, j), tmp[4][:], ACT.Copy).then_inc(hg_h, 1)
            with act.Fori(0, KD // 2) as i:
                for p in range(2):
                    act.wait_ge(tile_done, 2 * i + (N_GA + p + 1))
                    act.wait_ge(m_done, 2 * i + p)
                    A(tmp[6][:], psA[p], ACT.Sigmoid).then_inc(ga_read, 1)
                    hi((2 * i + (N_GA + p + 2), i + (N_GA + p + 2) // 2), p)

            def gr(i, last):
                for p in range(2):
                    act.wait_ge(tile_done, 2 * i + (N_GR + p + 1))
                    A(_tile(sgr, 2 * i + p), psB[p], ACT.Sigmoid).then_inc(gr_read, 1)
                    hi((2 * i + (N_GR + p + 2), i + (N_GR + p + 2) // 2), p, K=KR if last else KD)

            with act.Fori(0, KD // 2 - 1) as i:
                gr(i, False)
            gr(KD // 2 - 1, True)

            def br(i, last):
                for p in range(2):
                    hi((2 * i + (N_BR + p + 2), i + (N_BR + p + 2) // 2), p, K=KD if last else KR)
                    act.wait_ge(mf_done, 2 * i + (p + 1))
                    A(_tile(mg_hi, 2 * i + p), tmp[1][:], ACT.Copy).then_inc(mg_h, 1)

            with act.Fori(0, KD // 2 - 1) as i:
                br(i, False)
            br(KD // 2 - 1, True)

            def e_round(b, s, first=False):
                act.wait_ge(e_landed[s], b * 16 + 16)
                if not first:
                    if s < 4:
                        act.wait_ge(gu_used, b * 4 + (s - 3))
                    else:
                        act.wait_ge(d_used, b * 2 + (s - 5))
                A(ehi[s][:], est[s][:], ACT.Copy).then_inc(gu_hi if s < 4 else d_hi, 1)

            act.wait_ge(mg_l, KD)

            def x1_copy(t):
                act.wait_ge(x1_t, t + 1)
                A(x1T[:, t, 0:4, :], psA[0].rearrange("p (k c) -> p k c", c=P), ACT.Copy)
                A(x1T[:, t, 4:8, :], psA[1].rearrange("p (k c) -> p k c", c=P), ACT.Copy).then_inc(x1T_done, 1)

            for n in range(HALVES * KD):
                N, h, j = N_O + n, n // KD, n % KD
                act.wait_ge(tile_done, N + 1)
                A(yT[:, j, h * SH:(h + 1) * SH], psB[n % 2][:, 0:SH], ACT.Copy).then_inc(yT_done, 1)
                if N + 2 < N_END:
                    hi((N + 2, (N + 2) // 2), n % 2)
                if n in (0, 1):
                    e_round(0, n, first=True)
                if n == 8:
                    e_round(0, 2, first=True)
                if n == 12:
                    e_round(0, 3, first=True)
                if n == 14:
                    _std(act, 0, var_done, std_done, stat, 0, 2)
            act.wait_ge(mg_l, KD)
            act.wait_ge(tile_done, N_END)
            x1_copy(0)
            x1_copy(1)
            _std(act, 1, var_done, std_done, stat, 0, 2)
            x1_copy(2)
            x1_copy(3)
            act.wait_ge(lmax_done, 1)
            A(r16[1][:], r16[0][:], ACT.Exp).then_inc(exp_done, 1)
            e_round(0, 4, first=True)
            act.wait_ge(y_t, TT)
            e_round(0, 5, first=True)

            def rows_round(b, first=False):
                act.wait_ge(xe_t, b + 1)
                if not first:
                    act.wait_ge(gu_used, b * 4)
                A(xe_hi[:], psC[0][:].rearrange("p a (k c) -> p (a k) c", c=P), ACT.Copy).then_inc(xe_h, 1)

            def silu(b, first=False):
                act.wait_ge(gu_used, b * 4 + 2)
                if not first:
                    act.wait_ge(h_done, b)
                A(sg[:], psA[0], ACT.Silu).then_inc(silu_done, 1)

            def hidden_round(b, first=False):
                act.wait_ge(h_t, b + 1)
                if not first:
                    act.wait_ge(d_used, b * 2)
                A(hT_hi[:], psC[1][:, 0, :].rearrange("p (k c) -> p k c", c=P), ACT.Copy).then_inc(h_h, 1)

            def y_out(b, s, first=False):
                act.wait_ge(d_used, b * 2 + (s + 1))
                if not first:
                    act.wait_ge(y_stored, b * 16)
                A(yb[:, s * DF:(s + 1) * DF], psB[s], ACT.Copy).then_inc(y_evac, 1)
                if s == 1:
                    dst = ys[b * P:(b + 1) * P, :] if isinstance(b, int) else ys[ds(act.snap(b * P), P), :]
                    act.wait_ge(y_evac, b * 2 + 2)
                    act.dma_start(dst, yb[:]).then_inc(y_stored, 16)

            rows_round(0, first=True)

            def turn(b, nxt=True, prev=True, first=False, first_prev=False):
                if nxt:
                    e_round(b + 1, 0)
                    e_round(b + 1, 1)
                silu(b, first)
                if nxt:
                    e_round(b + 1, 2)
                    rows_round(b + 1)
                    e_round(b + 1, 3)
                for s in range(2):
                    if prev:
                        e_round(b, 4 + s)
                        y_out(b - 1, s, first_prev)
                hidden_round(b, first)

            turn(0, prev=False, first=True)
            turn(1, first_prev=True)
            with act.Fori(2, NE - 1) as b:
                turn(b)
            turn(NE - 1, nxt=False)
            for s in range(2):
                y_out(NE - 1, s)
            act.wait_ge(plan_done, 1)
            more = act.value_load(plan[0:1, 7:8], min_val=0, max_val=BLOCKS - NE)
            with act.If(more > 0):
                with act.Fori(0, more) as i:
                    b = i + NE
                    for s in range(4):
                        e_round(b, s)
                    rows_round(b)
                    silu(b)
                    for s in range(2):
                        e_round(b, 4 + s)
                    hidden_round(b)
                    for s in range(2):
                        y_out(b, s)
            act.wait_ge(y_stored, (more + NE) * 16)
            A(stat[:, 40:41], stat[:, 30:31], ACT.Copy).then_inc(all_stored, 1)
            act.wait_ge(scat, 16 * 2 * TT)
            for t in range(TT):
                A(x1[:, t, :], x1[:, t, :], ACT.Copy, scale=ALPHA).then_inc(x1_scaled, 1)
            for t in range(TT):
                _std(act, 2 + t, var_done, std_done, stat, t % 2, 1)

        @block.vector
        def _(dve):
            V = nc.vector
            chain = Chain(dve, dve_step)

            def lo(N, p, K=KD):
                dve.wait_ge(w_hi, N + 1)
                V.tensor_tensor(wlo[p][:, 0:K, :], wst[p][:, 0:K, :], whi[p][:, 0:K, :],
                                ALU.subtract).then_inc(w_lo, 1)

            for t in range(TT):
                dve.wait_ge(xt_hi, t + 1)
                V.tensor_tensor(xT_lo[:, :, t * P:(t + 1) * P],
                                pairs[t][:].rearrange("p a (b c) -> p (a b) c", c=P),
                                xT_hi[:, :, t * P:(t + 1) * P], ALU.subtract).then_inc(xt_lo, 1)
                if t == 2:
                    lo(0, 0)
            dve.wait_ge(chan_t, 1)
            V.tensor_copy(chan[:, 0:NROW], psB[0][:, 0:NROW]).then_inc(chan_ready, 1)
            lo(1, 1)
            dve.wait_ge(decay_act, 2)
            e, s1, s2, acc = (decay[:, n, :] for n in (2, 3, 4, 5))
            chain.link(V.tensor_scalar(acc, e, 2.0, None, ALU.add))
            chain.link(V.reciprocal(s1, acc))
            chain.link(V.tensor_tensor(s1, s1, e, ALU.mult))
            chain.link(V.tensor_tensor(s2, s1, s1, ALU.mult))
            TERMS = 8
            chain.link(V.tensor_scalar(acc, s2, 1.0 / (2 * TERMS + 1), 1.0 / (2 * TERMS - 1), ALU.mult, ALU.add))
            for n in range(TERMS - 2, -1, -1):
                chain.link(V.tensor_tensor(acc, acc, s2, ALU.mult))
                chain.link(V.tensor_scalar(acc, acc, 1.0 / (2 * n + 1), None, ALU.add))
            chain.link(V.tensor_tensor(acc, acc, s1, ALU.mult))
            chain.link(V.tensor_scalar(s2, chan[:, C_LAM:C_LAM + KR], -1.0, 0.0, ALU.mult, ALU.max))
            chain.link(V.scalar_tensor_tensor(acc, acc, 2.0, s2, ALU.mult, ALU.add))
            chain.link(V.tensor_scalar(decay[:, 0, :], acc, -8.0, None, ALU.mult))

            def rg_rest(j, p):
                dve.wait_ge(rgw_hi, j + 1)
                V.tensor_tensor(rg_lo[p][:], rg_st[p][:], rg_hi[p][:], ALU.subtract).then_inc(rgw_lo, 1)

            def conv_rest(j, p):
                dve.wait_ge(xc_start, j + 1)
                for k in (2, 1, 0):
                    d = 3 - k
                    ins = V.scalar_tensor_tensor(xc[p][:, d:S], psA[p][:, 0:S - d], _col(chan, C_CR(k, 0), j),
                                                 xc[p][:, d:S], ALU.mult, ALU.add)
                    if k:
                        chain.link(ins)
                ins.then_inc(xc_done, 1)

            def xc_rest(j, p):
                dve.wait_ge(xc_h, j + 1)
                V.tensor_tensor(xc_lo[:], xc[p][:], xc_hi[:], ALU.subtract).then_inc(xc_l, 1)

            def gates_of(j, p):
                dve.wait_ge(gate_done, j + 1)
                V.tensor_scalar(_tile(zbuf, j), _tile(zbuf, j), _col(decay[:, 0, :], 0, j), None, ALU.mult)
                V.tensor_tensor(_tile(ibuf, j), ig[p][:], xc[p][:], ALU.mult).then_inc(ix_done, 1)

            rg_rest(0, 0)
            rg_rest(1, 1)
            conv_rest(0, 0)
            lo(2, 0)
            xc_rest(0, 0)
            conv_rest(1, 1)
            lo(3, 1)
            xc_rest(1, 1)
            gates_of(0, 0)

            start = chain.n
            with dve.Fori(1, KR // 2) as i:
                chain.n = i * 4 + (start - 4)
                for p in range(2):
                    rg_rest(2 * i + p, p)
                    conv_rest(2 * i + p, p)
                    lo(2 * i + (p + 2), p)
                    xc_rest(2 * i + p, p)
                    gates_of(2 * i + (p - 1), 1 - p)
            chain.n = start + 4 * (KR // 2 - 1)
            gates_of(KR - 1, 1)

            QC = KR * S // 4
            zf = zbuf[:].rearrange("p j s -> p (j s)")
            tf = tbuf[:].rearrange("p j s -> p (j s)")
            xf = ibuf[:].rearrange("p j s -> p (j s)")

            def gated_conv(i):
                for q in range(2):
                    j, m = 2 * i + q, 3 * q
                    N = 6 * i + (N_A + m)
                    lo(N + 2, m % 2)
                    dve.wait_ge(c_read, j + 1)
                    dve.wait_ge(tile_done, N + 2)
                    dve.wait_ge(t_start, j)
                    V.tensor_tensor(tmp[1][:], tmp[0][:], ps6[m + 1], ALU.mult).then_inc(v_done, 1)
                    lo(N + 3, (m + 1) % 2)
                    dve.wait_ge(t_start, j + 1)
                    for k in (1, 0):
                        d = 2 - k
                        chain.link(V.scalar_tensor_tensor(tmp[2][:, d:S], tmp[1][:, 0:S - d],
                                                          _col(chan, C_CA(k, 0), j), tmp[2][:, d:S],
                                                          ALU.mult, ALU.add))
                    dve.wait_ge(tile_done, N + 3)
                    dve.wait_ge(u_h, j)
                    V.tensor_tensor(tmp[3][:], tmp[2][:], ps6[m + 2], ALU.mult).then_inc(u_done, 1)
                    lo(N + 4, m % 2)
                    dve.wait_ge(u_h, j + 1)
                    V.tensor_tensor(_tile(u_lo, j), tmp[3][:], _tile(u_hi, j), ALU.subtract).then_inc(u_l, 1)

            chain.loop(KD // 2, gated_conv, 4)

            def branch_a(i):
                for p in range(2):
                    lo(2 * i + (N_BA + p + 2), p)
                    if p == 0:
                        dve.wait_ge(sq_done, i + 1)
                        q = ds(i * QC, QC)
                        chain.link(V.scalar_tensor_tensor(tf[:, q], zf[:, q], 1.0, tf[:, q], ALU.add, ALU.mult))
                        V.tensor_tensor(xf[:, q], xf[:, q], tf[:, q], ALU.mult).then_inc(bt_done, 1)

            chain.loop(KD // 2, branch_a, 1)
            dve.wait_ge(bt_done, 4)

            def gelu_r(i):
                for p in range(2):
                    j = 2 * i + p
                    chain.link(V.tensor_tensor_scan(_tile(zbuf, j), _tile(zbuf, j), _tile(ibuf, j), 0.0,
                                                    ALU.mult, ALU.add))
                    dve.wait_ge(y_sq, j + 1)
                    chain.link(V.tensor_tensor(tmp[5][:], yr[p][:], yr[p][:], ALU.mult))
                    dve.wait_ge(y_sig, j)
                    V.scalar_tensor_tensor(tmp[1][:], tmp[5][:], 1.0 / GELU_A, yr[p][:],
                                           ALU.add, ALU.mult).then_inc(y_q, 1)
                    lo(2 * i + (N_YR + p + 2), p)
                    chain.link(V.tensor_tensor(tmp[3][:], _tile(zbuf, j), yr[p][:], ALU.mult))
                    dve.wait_ge(y_sig, j + 1)
                    dve.wait_ge(hg_h, j)
                    V.tensor_tensor(tmp[4][:], tmp[3][:], tmp[2][:], ALU.mult).then_inc(hg_done, 1)
                    dve.wait_ge(hg_h, j + 1)
                    V.tensor_tensor(_tile(hg_lo, j), tmp[4][:], _tile(hg_hi, j), ALU.subtract).then_inc(hg_l, 1)

            chain.loop(KR // 2, gelu_r, 6)

            with dve.Fori(0, KD // 2) as i:
                for p in range(2):
                    j = 2 * i + p
                    dve.wait_ge(ga_read, j + 1)
                    V.tensor_tensor(_tile(ya, j), _tile(ya, j), tmp[6][:], ALU.mult).then_inc(m_done, 1)
                    lo(2 * i + (N_GA + p + 2), p)

            def gr(i, last):
                for p in range(2):
                    lo(2 * i + (N_GR + p + 2), p, K=KR if last else KD)

            with dve.Fori(0, KD // 2 - 1) as i:
                gr(i, False)
            gr(KD // 2 - 1, True)
            dve.wait_ge(gr_read, KD)
            dve.wait_ge(m_done, KD)

            def br(i, last):
                for p in range(2):
                    j = 2 * i + p
                    N = 2 * i + (N_BR + p)
                    dve.wait_ge(tile_done, N + 1)
                    chain.link(V.tensor_tensor(tmp[0][:], _tile(sgr, j), psA[p], ALU.mult))
                    dve.wait_ge(mg_h, j)
                    V.tensor_tensor(tmp[1][:], tmp[0][:], _tile(ya, j), ALU.add).then_inc(mf_done, 1)
                    lo(N + 2, p, K=KD if last else KR)
                    dve.wait_ge(mg_h, j + 1)
                    V.tensor_tensor(_tile(mg_lo, j), tmp[1][:], _tile(mg_hi, j), ALU.subtract).then_inc(mg_l, 1)

            chain.loop(KD // 2 - 1, lambda i: br(i, False), 2)
            br(KD // 2 - 1, True)

            def e_rest(b, s):
                if s < 4:
                    dve.wait_ge(gu_hi, b * 4 + (s + 1))
                else:
                    dve.wait_ge(d_hi, b * 2 + (s - 3))
                V.tensor_tensor(elo[s][:], est[s][:], ehi[s][:], ALU.subtract).then_inc(gu_lo if s < 4 else d_lo, 1)

            def residual(t):
                dve.wait_ge(y_t, t + 1)
                for h in range(2):
                    ins = V.scalar_tensor_tensor(x1[:, t, h * S:(h + 1) * S], x1[:, t, h * S:(h + 1) * S],
                                                 ALPHA, psC[t % 2][:, h, :], ALU.mult, ALU.add)
                ins.then_inc(res_done, 1)

            def moments(row, u):
                for h in range(2):
                    V.bn_stats(stat[:, 12 * u + 6 * h:12 * u + 6 * h + 6], row[:, h * S:(h + 1) * S]
                               ).then_inc(stats_done, 1)

            def variance(u, n, count):
                dve.wait_ge(stats_done, count)
                for v in range(u, u + n):
                    ins = V.bn_aggr(stat[:, 24 + 2 * v:26 + 2 * v],
                                    stat[:, 12 * v:12 * v + 12].rearrange("p (a c) -> p a c", c=6))
                chain.link(ins)
                for v in range(u, u + n):
                    ins = V.tensor_scalar(stat[:, 28 + v:29 + v], stat[:, 25 + 2 * v:26 + 2 * v], LN_EPS, None,
                                          ALU.add)
                ins.then_inc(var_done, 1)

            def rstd(u, n, count):
                v, s0, w0, s2, s3, r0 = (stat[:, c + u:c + u + n] for c in (28, 30, 32, 34, 36, 38))
                dve.wait_ge(std_done, count)
                chain.link(V.reciprocal(w0, s0))
                chain.link(V.tensor_tensor(s2, v, w0, ALU.mult))
                chain.link(V.tensor_tensor(s2, s2, s0, ALU.add))
                chain.link(V.tensor_scalar(s3, s2, 0.5, None, ALU.mult))
                chain.link(V.reciprocal(r0, s3))

            def scale_rows(row, u, gb, done):
                chain.link(V.scalar_tensor_tensor(row, row, stat[:, 24 + 2 * u:25 + 2 * u], gb[:, 0, :],
                                                  ALU.subtract, ALU.mult))
                V.scalar_tensor_tensor(row, row, stat[:, 38 + u:39 + u], gb[:, 1, :],
                                       ALU.mult, ALU.add).then_inc(done, 1)

            for n in range(HALVES * KD):
                if N_O + n + 2 < N_END:
                    lo(N_O + n + 2, n % 2)
                if n in (2, 3):
                    e_rest(0, n - 2)
                if n == 9:
                    residual(0)
                if n == 10:
                    residual(1)
                    dve.wait_ge(res_done, 1)
                    moments(x1[:, 0, :], 0)
                if n == 11:
                    e_rest(0, 2)
                if n == 12:
                    dve.wait_ge(res_done, 2)
                    moments(x1[:, 1, :], 1)
                    variance(0, 2, 4)
            dve.wait_ge(ln1_landed, 32)
            rstd(0, 2, 1)
            scale_rows(x1[:, 0, :], 0, ln1_gb, x1_done)
            scale_rows(x1[:, 1, :], 1, ln1_gb, x1_done)
            for u in range(2):
                residual(2 + u)
                dve.wait_ge(res_done, 3 + u)
                moments(x1[:, 2 + u, :], u)
            variance(0, 2, 8)
            rstd(0, 2, 2)
            for u in range(2):
                scale_rows(x1[:, 2 + u, :], u, ln1_gb, x1_done)
            dve.wait_ge(small_landed, 32)

            def b16(v):
                return v[:].unsqueeze(2).to_broadcast([P, TT, NE])

            def tt(o, a, b, op):
                chain.link(V.tensor_tensor(o, a, b, op))

            def red(o, a, op):
                chain.link(V.tensor_reduce(o, a, AX, op))

            ex, iota3 = r16[1], iota_e[:].unsqueeze(1).to_broadcast([P, TT, NE])
            dve.wait_ge(logit_done, TT)
            tt(r16[0][:], psB[0][:, 0:TT * NE].rearrange("p (t e) -> p t e", e=NE),
               brow[:].unsqueeze(1).to_broadcast([P, TT, NE]), ALU.add)
            red(r1[0][:], r16[0][:], ALU.max)
            V.tensor_tensor(r16[0][:], r16[0][:], b16(r1[0]), ALU.subtract).then_inc(lmax_done, 1)
            dve.wait_ge(exp_done, 1)
            red(r1[1][:], ex[:], ALU.add)
            chain.link(V.reciprocal(r1[2][:], r1[1][:]))
            pr = r16[2]
            tt(pr[:], ex[:], b16(r1[2]), ALU.mult)
            g4 = pr[:].rearrange("p t (g e) -> p t g e", e=GRP)
            score = r4[0]
            V.tensor_tensor(r6[:, :, :, 0:3], g4[:, :, :, 0:3], g4[:, :, :, 1:4], ALU.add)
            V.tensor_tensor(r6[:, :, :, 3:5], g4[:, :, :, 0:2], g4[:, :, :, 2:4], ALU.add)
            tt(r6[:, :, :, 5:6], g4[:, :, :, 0:1], g4[:, :, :, 3:4], ALU.add)
            red(score[:], r6[:], ALU.max)

            def first_of(o, idx, vals, width, best, scratch):
                bb = best[:].unsqueeze(2).to_broadcast([P, TT, width])
                it = iota_e[:, 0:width].unsqueeze(1).to_broadcast([P, TT, width])
                tt(scratch, vals, bb, ALU.is_lt)
                chain.link(V.scalar_tensor_tensor(scratch, scratch, 99.0, it, ALU.mult, ALU.add))
                red(idx[:], scratch, ALU.min)
                tt(o, it, idx[:].unsqueeze(2).to_broadcast([P, TT, width]), ALU.is_equal)

            red(r1[3][:], score[:], ALU.max)
            first_of(r4[2][:], r1[4], score[:], NG, r1[3], r4[3][:])
            pm, pw = r16[3], r16[4]
            gm = r4[2][:].unsqueeze(3).to_broadcast([P, TT, NG, GRP])
            V.tensor_scalar(r4[4][:], r4[2][:], -1.0, None, ALU.add)
            tt(pw[:].rearrange("p t (g e) -> p t g e", e=GRP), g4, gm, ALU.mult)
            tt(pm[:].rearrange("p t (g e) -> p t g e", e=GRP), pw[:].rearrange("p t (g e) -> p t g e", e=GRP),
               r4[4][:].unsqueeze(3).to_broadcast([P, TT, NG, GRP]), ALU.add)
            red(r1[5][:], pm[:], ALU.max)
            oh1, oh2 = (onehot[:, n] for n in range(2))
            first_of(oh1, r1[6], pm[:], NE, r1[5], chosen[:, 0])
            chain.link(V.scalar_tensor_tensor(pm[:], oh1, -4.0, pm[:], ALU.mult, ALU.add))
            red(r1[7][:], pm[:], ALU.max)
            first_of(oh2, r1[8], pm[:], NE, r1[7], chosen[:, 0])
            V.tensor_tensor(sel[:], oh1, oh2, ALU.add).then_inc(sel_done, 1)
            tt(r1[9][:], r1[5][:], r1[7][:], ALU.add)
            chain.link(V.reciprocal(r1[10][:], r1[9][:]))
            V.tensor_tensor(gates[:, 0, :], r1[5][:], r1[10][:], ALU.mult)
            tt(gates[:, 1, :], r1[7][:], r1[10][:], ALU.mult)
            dve.wait_ge(pos_done, 1)
            dve.wait_ge(sel_done, 1)
            cnt, ext, inc, bb = (r16[n][:, 0, :] for n in (9, 10, 11, 12))
            pos, row = r16[13], r16[14]
            V.tensor_copy(pos[:], psB[1][:, 0:TT * NE].rearrange("p (t e) -> p t e", e=NE))
            chain.link(V.tensor_copy(cnt, psB[1][:, TT * NE:(TT + 1) * NE]))
            chain.link(V.tensor_scalar(ext, cnt, float(P), None, ALU.is_gt))
            for n in range(2, TT):
                chain.link(V.scalar_tensor_tensor(ext, cnt, float(n * P), ext, ALU.is_gt, ALU.add))
            chain.link(V.tensor_tensor_scan(inc, ones[:, 0:NE], ext, 0.0, ALU.mult, ALU.add))
            tt(bb, inc, ext, ALU.subtract)
            tt(bb, bb, iota_e[:], ALU.subtract)
            V.tensor_scalar(row[:], pos[:], float(P), None, ALU.is_ge)
            chain.link(V.tensor_scalar(bb, bb, float(P), float((NE - 1) * P), ALU.mult, ALU.add))
            tt(row[:], row[:], bb.unsqueeze(1).to_broadcast([P, TT, NE]), ALU.mult)
            tt(row[:], row[:], pos[:], ALU.add)
            chain.link(V.scalar_tensor_tensor(row[:], iota3, float(P), row[:], ALU.mult, ALU.add))
            for n in range(2):
                ins = V.tensor_tensor(chosen[:, n], onehot[:, n], row[:], ALU.mult)
            chain.link(ins)
            red(rowsum[:], chosen[:], ALU.add)
            V.tensor_copy(dest[:], rowsum[:]).then_inc(dest_done, 1)
            for n in range(BLOCKS - NE):
                chain.link(V.tensor_scalar(r16[15][:, 0, :], inc, float(n), None, ALU.is_le))
                red(r1[13][:, 0:1], r16[15][:, 0, :], ALU.add)
                chain.link(V.tensor_scalar(r1[14][:, 0:1], r1[13][:, 0:1], float(NE - 1), None, ALU.min))
                chain.link(V.tensor_copy(plan[:, n:n + 1], r1[14][:, 0:1]))
            V.tensor_copy(plan[:, 7:8], inc[:, NE - 1:NE]).then_inc(plan_done, 1)

            e_rest(0, 3)
            e_rest(0, 4)
            e_rest(0, 5)

            def rows_rest(b):
                dve.wait_ge(xe_h, b + 1)
                V.tensor_tensor(xe_lo[:], psC[0][:].rearrange("p a (k c) -> p (a k) c", c=P), xe_hi[:],
                                ALU.subtract).then_inc(xe_l, 1)

            def hidden(b, first=False):
                dve.wait_ge(silu_done, b + 1)
                dve.wait_ge(gu_used, b * 4 + 4)
                if not first:
                    dve.wait_ge(h_t, b)
                V.tensor_tensor(hb[:], sg[:], psA[1], ALU.mult).then_inc(h_done, 1)

            def hidden_rest(b):
                dve.wait_ge(h_h, b + 1)
                V.tensor_tensor(hT_lo[:], psC[1][:, 0, :].rearrange("p (k c) -> p k c", c=P), hT_hi[:],
                                ALU.subtract).then_inc(h_l, 1)

            rows_rest(0)

            def turn(b, nxt=True, prev=True, first=False):
                if nxt:
                    for s in range(3):
                        e_rest(b + 1, s)
                hidden(b, first)
                if nxt:
                    rows_rest(b + 1)
                    e_rest(b + 1, 3)
                if prev:
                    e_rest(b, 4)
                    e_rest(b, 5)
                hidden_rest(b)

            turn(0, prev=False, first=True)
            with dve.Fori(1, NE - 1) as b:
                turn(b)
            turn(NE - 1, nxt=False)
            dve.wait_ge(plan_done, 1)
            more = dve.value_load(plan[0:1, 7:8], min_val=0, max_val=BLOCKS - NE)
            with dve.If(more > 0):
                with dve.Fori(0, more) as i:
                    b = i + NE
                    for s in range(4):
                        e_rest(b, s)
                    rows_rest(b)
                    hidden(b)
                    e_rest(b, 4)
                    e_rest(b, 5)
                    hidden_rest(b)

            dve.wait_ge(ln2_landed, 32)

            def gathered(t):
                dve.wait_ge(got[t], 32)
                dve.wait_ge(x1_scaled, t + 1)
                row = yg[:, 0, t, :]
                chain.link(V.scalar_tensor_tensor(row, row, gates[:, 0, t:t + 1], x1[:, t, :],
                                                  ALU.mult, ALU.add))
                chain.link(V.scalar_tensor_tensor(row, yg[:, 1, t, :], gates[:, 1, t:t + 1], row,
                                                  ALU.mult, ALU.add))
                moments(row, t % 2)
                variance(t % 2, 1, 2 * TT + 2 * t + 2)

            gathered(0)
            for t in range(TT):
                if t + 1 < TT:
                    gathered(t + 1)
                rstd(t % 2, 1, 3 + t)
                scale_rows(yg[:, 0, t, :], t % 2, ln2_gb, out_ready)


def _std(act, count, var_done, std_done, stat, u, n):
    act.wait_ge(var_done, count + 1)
    act.activation(stat[:, 30 + u:30 + u + n], stat[:, 28 + u:28 + u + n], ACT.Sqrt).then_inc(std_done, 1)


def _tile(buf, j):
    if isinstance(j, int):
        return buf[:, j, :]
    return buf[:, ds(j, 1), :].rearrange("p a s -> p (a s)")


def _col(buf, c0, j):
    if isinstance(j, int):
        return buf[:, c0 + j:c0 + j + 1]
    return buf[:, ds(j + c0, 1)]


_INS = ["x", "w_in", "conv_a_w", "w_branch_a", "conv_r_w", "conv_r_b", "w_rg_a", "b_rg_a", "w_rg_x",
        "b_rg_x", "rg_lambda", "w_branch_r", "w_out", "ln1_g", "ln1_b", "w_router", "b_router",
        "w_exp_gate", "w_exp_up", "w_exp_down", "ln2_g", "ln2_b"]


def kernel(**inputs):
    import numpy as _np
    import concourse.bacc as _bacc
    from concourse import mybir as _mybir
    from concourse.bass_utils import run_bass_kernel_spmd as _run

    nc = _bacc.Bacc("TRN2", target_bir_lowering=False, num_devices=1)
    arrays, args = {}, []
    for name in _INS:
        a = _np.ascontiguousarray(inputs[name])
        arrays[f"in_{name}_dram"] = a
        args.append(nc.dram_tensor(f"in_{name}_dram", a.shape, _mybir.dt.from_np(a.dtype), kind="ExternalInput").ap())
    shape = inputs["x"].shape
    args.append(nc.dram_tensor("out_dram", shape, _mybir.dt.float32, kind="ExternalOutput").ap())
    trunk_moe(nc, *args)
    r = _run(nc, [arrays], core_ids=[0])
    return r.results[0]["out_dram"]
```

```python
from contextlib import ExitStack

import concourse.bass as bass
from concourse import mybir

P = 128
F32 = mybir.dt.float32
F32R = mybir.dt.float32r
BF16 = mybir.dt.bfloat16
I32 = mybir.dt.int32
U32 = mybir.dt.uint32
ACT = mybir.ActivationFunctionType
ALU = mybir.AluOpType
AX = mybir.AxisListType.X
ds = bass.ds
KIB = 1024
LN_EPS = 1e-5
GELU_A = 0.044715
GELU_S = 2.0 * 0.7978845608028654


class Chain:

    def __init__(self, eng, sem):
        self.eng, self.sem, self.n = eng, sem, 0

    def link(self, ins):
        ins.then_inc(self.sem, 1)
        self.n = self.n + 1
        self.eng.wait_ge(self.sem, self.n)

    def loop(self, trips, body, per):
        start = self.n
        with self.eng.Fori(0, trips) as i:
            self.n = i * per + start
            body(i)
        self.n = start + trips * per


def trunk_moe(nc, x, w_in, conv_a_w, w_branch_a, conv_r_w, conv_r_b, w_rg_a, b_rg_a, w_rg_x, b_rg_x,
              rg_lambda, w_branch_r, w_out, ln1_g, ln1_b, w_router, b_router,
              w_exp_gate, w_exp_up, w_exp_down, ln2_g, ln2_b, out):
    _, S, D = x.shape
    DR = conv_r_b.shape[1]
    NE, DF = w_exp_gate.shape[1], w_exp_gate.shape[3]
    GRP = 4
    NG = NE // GRP
    KD, KR, KF = D // P, DR // P, DF // P
    TT = S // P
    ALPHA = 2.0 ** 0.25
    HEAD = P * 5 // 8
    BLOCKS = NE + (2 * S - 1) // (P + 1)
    ZEROS = 16 * 2 * BLOCKS
    assert (S, D, DR, NE, DF) == (512, 1024, 1280, 16, 512)

    COL_H, COL_B, COL_C = 0, D, 2 * D
    COL_XR, COL_YR = 3 * D, 3 * D + DR
    COL_GA, COL_GR = 3 * D + 2 * DR, 4 * D + 2 * DR

    N_XR = 0
    N_A = N_XR + KR
    N_BA = N_A + 3 * KD
    N_YR = N_BA + KD
    N_GA = N_YR + KR
    N_GR = N_GA + KD
    N_BR = N_GR + KD
    N_O = N_BR + KD
    HALVES = 2
    N_END = N_O + HALVES * KD
    SH = S // HALVES

    x2 = x.rearrange("a s d -> (a s) d")
    out2 = out.rearrange("a s d -> (a s) d")
    win_v = w_in[0].rearrange("(k p) n -> p k n", p=P)
    wba_v = w_branch_a[0].rearrange("(k p) n -> p k n", p=P)
    wbr_v = w_branch_r[0].rearrange("(k p) n -> p k n", p=P)
    wout_v = w_out[0].rearrange("(k p) n -> p k n", p=P)

    xs = nc.dram_tensor("xs", (BLOCKS * P, D), F32, kind="Internal").ap()
    ys = nc.dram_tensor("ys", (BLOCKS * P, D), F32, kind="Internal").ap()

    with ExitStack() as ctx:
        base = (nc.sbuf_base + 31) // 32 * 32

        def at(name, kib, shape, dt=F32):
            return nc.alloc_sbuf_tensor_at(name, shape, dt, offset=base + int(kib * KIB))

        def sem(name):
            return ctx.enter_context(nc.semaphore(name))

        zbuf = at("zbuf", 0, [P, KR, S])
        tbuf = at("tbuf", 20, [P, KR, S])
        ibuf = at("ibuf", 40, [P, KR, S])
        hg_hi = at("hg_hi", 20, [P, KR, S], F32R)
        hg_lo = at("hg_lo", 40, [P, KR, S], F32R)
        u_hi = at("u_hi", 60, [P, KD, S], F32R)
        u_lo = at("u_lo", 76, [P, KD, S], F32R)
        sgr = at("sgr", 60, [P, KD, S])
        ya = at("ya", 92, [P, KD, S])
        zero = at("zero", 92, [P, D])
        rg_st = [at(f"rg_st{p}", 96 + p, [P, 2, P]) for p in range(2)]
        rg_hi = [at(f"rg_hi{p}", 98 + p, [P, 2, P], F32R) for p in range(2)]
        rg_lo = [at(f"rg_lo{p}", 100 + p, [P, 2, P], F32R) for p in range(2)]
        rows = at("rows", 102, [P, P])
        wst = [at(f"wst{p}", 108 + 5 * p, [P, KR, P]) for p in range(2)]
        wst.append(at("wst2", 104, [P, KD, P]))
        whi = [at(f"whi{p}", 118 + 5 * p, [P, KR, P], F32R) for p in range(2)]
        wlo = [at(f"wlo{p}", 128 + 5 * p, [P, KR, P], F32R) for p in range(2)]
        xT_hi = at("xT_hi", 138, [P, KD, S], F32R)
        xT_lo = at("xT_lo", 154, [P, KD, S], F32R)
        mg_hi = at("mg_hi", 138, [P, KD, S], F32R)
        mg_lo = at("mg_lo", 154, [P, KD, S], F32R)
        tmp = [at(f"tmp{i}", 170 + 2 * i, [P, S]) for i in range(8)]
        xc = [tmp[0], tmp[1]]
        xc_hi = at("xc_hi", 174, [P, S], F32R)
        xc_lo = at("xc_lo", 176, [P, S], F32R)
        ig = [tmp[4], tmp[5]]
        yr = [tmp[0], tmp[6]]
        yT = at("yT", 170, [P, KD, S])
        x1 = at("x1", 186, [P, TT, D])
        ident = at("ident", 202, [P, P])
        before = at("before", 202.5, [P, P])
        ones = at("ones", 203, [P, P])
        chan = at("chan", 203.5, [P, P])
        wr = at("wr", 204, [P, KD, NE])
        decay = at("decay", 204.5, [P, 8, KR])
        brow = at("brow", 204.875, [P, NE])
        iota_e = at("iota_e", 204.9375, [P, NE])
        stat = at("stat", 206, [P, 48])
        gates = at("gates", 205.125, [P, 2, TT])
        dest = at("dest", 205.1875, [P, 2, TT], U32)
        ones_b = at("ones_b", 205.5, [P, P], BF16)
        before_b = at("before_b", 205.75, [P, P], BF16)
        slots = at("slots", 206.25, [P, P])
        alpha_i = at("alpha_i", 206.75, [P, P])
        plan = at("plan", 205.25, [P, 8], I32)
        full = at("full", 205.3125, [P, BLOCKS], I32)
        r16 = [at(f"r16_{i}", 154 + 0.25 * i, [P, TT, NE]) for i in range(20)]
        r4 = [at(f"r4_{i}", 159.5 + 0.0625 * i, [P, TT, NG]) for i in range(8)]
        r1 = [at(f"r1_{i}", 160 + 0.015625 * 2 * i, [P, TT]) for i in range(16)]
        sel = at("sel", 161, [P, TT, NE], BF16)
        r6 = at("r6", 161.25, [P, TT, NG, 6])
        onehot = at("onehot", 155.25, [P, 2, TT, NE])
        chosen = at("chosen", 155.75, [P, 2, TT, NE])
        rowsum = at("rowsum", 161.75, [P, 2, TT])
        x1T = at("x1T", 138, [P, TT, KD, P])
        ln1_gb = at("ln1_gb", 96, [P, 2, D])
        est = [at(f"est{s}", 8 * s, [P, 4, DF]) for s in range(6)]
        ehi = [at(f"ehi{s}", o, [P, 4, DF], F32R) for s, o in enumerate([48, 56, 64, 72, 108, 170])]
        elo = [at(f"elo{s}", o, [P, 4, DF], F32R) for s, o in enumerate([80, 88, 96, 116, 124, 178])]
        xe = at("xe", 138, [P, D])
        xe_hi = at("xe_hi", 142, [P, KD, P], F32R)
        xe_lo = at("xe_lo", 146, [P, KD, P], F32R)
        sg = at("sg", 150, [P, DF])
        hb = at("hb", 152, [P, DF])
        hT_hi = at("hT_hi", 154, [P, KF, P], F32R)
        hT_lo = at("hT_lo", 156, [P, KF, P], F32R)
        yb = at("yb", 158, [P, D])
        ln2_gb = at("ln2_gb", 162, [P, 2, D])
        block0 = at("block0", 152, [P, TT, P])
        diag = at("diag", 104, [P, 2, TT, P])
        yg = at("yg", 0, [P, 2, TT, D])

        pairs = [ctx.enter_context(nc.psum_tensor(f"ps{n}", [P, 2, S], F32)) for n in "CDAB"]
        psC = pairs[0:2]
        psA, psB = ([pair[:, i, :] for i in range(2)] for pair in pairs[2:4])
        ps6 = [psC[0][:, 0, :], psC[0][:, 1, :], psC[1][:, 0, :], psC[1][:, 1, :], psB[0], psB[1]]
        back_ps = [pairs[2], pairs[2], pairs[0], pairs[1]]

        x_landed = [sem(f"x_landed{t}") for t in range(TT)]
        sp_step = sem("sp_step")
        rows_landed = sem("rows_landed")
        small_landed = sem("small_landed")
        masks = sem("masks")
        pool_step = sem("pool_step")
        chan_t = sem("chan_t")
        chan_ready = sem("chan_ready")
        decay_act = sem("decay_act")
        xt_t = sem("xt_t")
        xt_hi = sem("xt_hi")
        xt_lo = sem("xt_lo")
        w_landed = [sem(f"w_landed{p}") for p in range(3)]
        w_hi = sem("w_hi")
        w_lo = sem("w_lo")
        tile_done = sem("tile_done")
        rg_landed = [sem(f"rg_landed{p}") for p in range(2)]
        rgw_hi = sem("rgw_hi")
        rgw_lo = sem("rgw_lo")
        xc_start = sem("xc_start")
        xc_done = sem("xc_done")
        xc_h = sem("xc_h")
        xc_l = sem("xc_l")
        rg_done = sem("rg_done")
        gate_done = sem("gate_done")
        ix_done = sem("ix_done")
        c_read = sem("c_read")
        v_done = sem("v_done")
        t_start = sem("t_start")
        u_done = sem("u_done")
        u_h = sem("u_h")
        u_l = sem("u_l")
        a_done = sem("a_done")
        sq_done = sem("sq_done")
        bt_done = sem("bt_done")
        ya_done = sem("ya_done")
        y_sq = sem("y_sq")
        y_q = sem("y_q")
        y_sig = sem("y_sig")
        hg_done = sem("hg_done")
        hg_h = sem("hg_h")
        hg_l = sem("hg_l")
        ga_read = sem("ga_read")
        m_done = sem("m_done")
        gr_read = sem("gr_read")
        mf_done = sem("mf_done")
        mg_h = sem("mg_h")
        mg_l = sem("mg_l")
        yT_done = sem("yT_done")
        ln1_landed = sem("ln1_landed")
        y_t = sem("y_t")
        res_done = sem("res_done")
        stats_done = sem("stats_done")
        var_done = sem("var_done")
        std_done = sem("std_done")
        x1_done = sem("x1_done")
        x1_t = sem("x1_t")
        x1T_done = sem("x1T_done")
        logit_done = sem("logit_done")
        lmax_done = sem("lmax_done")
        exp_done = sem("exp_done")
        sel_done = sem("sel_done")
        pos_done = sem("pos_done")
        dest_done = sem("dest_done")
        plan_done = sem("plan_done")
        zero_done = sem("zero_done")
        scat = sem("scat")
        dve_step = sem("dve_step")
        e_landed = [sem(f"e_landed{s}") for s in range(6)]
        gu_hi = sem("gu_hi")
        gu_lo = sem("gu_lo")
        gu_used = sem("gu_used")
        d_hi = sem("d_hi")
        d_lo = sem("d_lo")
        d_used = sem("d_used")
        xe_landed = sem("xe_landed")
        xe_t = sem("xe_t")
        xe_h = sem("xe_h")
        xe_l = sem("xe_l")
        silu_done = sem("silu_done")
        h_done = sem("h_done")
        h_t = sem("h_t")
        h_h = sem("h_h")
        h_l = sem("h_l")
        y_evac = sem("y_evac")
        y_stored = sem("y_stored")
        y_rest_stored = sem("y_rest_stored")
        all_stored = sem("all_stored")
        ln2_landed = sem("ln2_landed")
        got = [sem(f"got{t}") for t in range(TT)]
        diag_done = sem("diag_done")
        picked0 = sem("picked0")
        block0_done = sem("block0_done")
        sum_done = sem("sum_done")
        out_ready = sem("out_ready")
        stored = sem("stored")

        C_CA = lambda k, j: k * KD + j
        C_CR = lambda k, j: 3 * KD + k * KR + j
        C_CB = 3 * KD + 4 * KR
        C_BA, C_BX, C_LAM = C_CB + KR, C_CB + 2 * KR, C_CB + 3 * KR
        NROW = C_LAM + KR

        block = ctx.enter_context(nc.Block())

        def load_expert(sp, b, s, expert=None, again=False):
            if again or b > 0:
                if s < 4:
                    sp.wait_ge(gu_lo, b * 4 + (s - 3))
                else:
                    sp.wait_ge(d_lo, b * 2 + (s - 5))
            if expert is not None:
                sp.wait_ge(gu_lo, 4 * NE)
            e = b if expert is None else expert
            w = (w_exp_gate, w_exp_up, w_exp_down)[s // 2]
            w = w[0, e] if isinstance(e, int) else w[0, ds(e, 1)].rearrange("a k n -> (a k) n")
            if s < 4:
                src = w.rearrange("(k p) n -> p k n", p=P)[:, 4 * (s % 2):4 * (s % 2) + 4, :]
            else:
                src = w.rearrange("(k p) n -> p k n", p=P)[:, :, (s - 4) * DF:(s - 3) * DF]
            sp.dma_start(est[s][:], src).then_inc(e_landed[s], 16)

        @block.sync
        def _(sp):
            for t in range(TT):
                sp.dma_start(x1[:, t, :], x2[t * P:(t + 1) * P, :]).then_inc(x_landed[t], 16)

            def load(N, p, src, K=KD):
                if not (isinstance(N, int) and N < 2):
                    sp.wait_ge(w_lo, N - 1)
                    sp.sem_inc(sp_step, 1)
                sp.dma_start(wst[p][:, 0:K, :], src).then_inc(w_landed[p], 16)

            def part(view, c0, j):
                if isinstance(j, int):
                    return view[:, :, c0 + j * P:c0 + (j + 1) * P]
                return view[:, :, ds(j * P + c0, P)]

            def load_rg(j, p):
                if not (isinstance(j, int) and j < 2):
                    sp.wait_ge(rgw_lo, j - 1)
                wa = w_rg_a[0, j] if isinstance(j, int) else w_rg_a[0, ds(j, 1)].rearrange("a i o -> (a i) o")
                wx = w_rg_x[0, j] if isinstance(j, int) else w_rg_x[0, ds(j, 1)].rearrange("a i o -> (a i) o")
                sp.dma_start(rg_st[p][:, 0, :], wa).then_inc(rg_landed[p], 16)
                sp.dma_start(rg_st[p][:, 1, :], wx).then_inc(rg_landed[p], 16)

            load(0, 0, part(win_v, COL_XR, 0))
            r = 0
            for src, n in ((conv_a_w[0].rearrange("k (j c) -> (k j) c", c=P), 3 * KD),
                           (conv_r_w[0].rearrange("k (j c) -> (k j) c", c=P), 4 * KR),
                           (conv_r_b[0].rearrange("(j c) -> j c", c=P), KR),
                           (b_rg_a[0], KR), (b_rg_x[0], KR),
                           (rg_lambda[0].rearrange("(j c) -> j c", c=P), KR)):
                sp.dma_start(rows[r:r + n, :], src).then_inc(rows_landed, 16)
                r += n
            load(1, 1, part(win_v, COL_XR, 1))
            load_rg(0, 0)
            load_rg(1, 1)
            sp.dma_start(wr[:], w_router.rearrange("(k p) e -> p k e", p=P)).then_inc(small_landed, 16)
            sp.dma_start(brow[:], b_router.rearrange("(a e) -> a e", a=1).to_broadcast([P, NE])
                         ).then_inc(small_landed, 16)
            with sp.Fori(1, KR // 2) as i:
                for p in range(2):
                    load(2 * i + p, p, part(win_v, COL_XR, 2 * i + p))
                    load_rg(2 * i + p, p)
            with sp.Fori(0, KD // 2) as i:
                for m in range(6):
                    c0 = (COL_C, COL_H, COL_B)[m % 3]
                    load(6 * i + (N_A + m), m % 2, part(win_v, c0, 2 * i + m // 3))
            for N0, view, c0, trips in ((N_BA, wba_v, 0, KD), (N_YR, win_v, COL_YR, KR),
                                        (N_GA, win_v, COL_GA, KD), (N_GR, win_v, COL_GR, KD),
                                        (N_BR, wbr_v, 0, KD)):
                with sp.Fori(0, trips // 2) as i:
                    for p in range(2):
                        load(2 * i + (N0 + p), p, part(view, c0, 2 * i + p), K=view.shape[1])
                if N0 == N_GA:
                    sp.wait_ge(hg_done, KR)
                    load_expert(sp, 0, 0)
                    load_expert(sp, 0, 1)
            for n in range(HALVES * KD):
                if n < 2:
                    load(N_O + n, n, part(wout_v, 0, n))
                else:
                    if n == 2:
                        sp.wait_ge(mf_done, KD)
                    else:
                        sp.wait_ge(w_lo, N_O + n - 2)
                    sp.dma_start(wst[n % 3][:, 0:KD, :], part(wout_v, 0, n % KD)).then_inc(w_landed[n % 3], 16)
                if n == 4:
                    load_expert(sp, 0, 2)
                if n == 6:
                    for q, v in enumerate((ln1_g, ln1_b)):
                        sp.dma_start(ln1_gb[:, q, :], v.to_broadcast([P, D])).then_inc(ln1_landed, 16)
                if n in (7, 9, 11):
                    load_expert(sp, 0, (n - 1) // 2)
            for s in range(6):
                if s == 5:
                    sp.wait_ge(xe_landed, 32)
                load_expert(sp, 1, s)
            for s in range(4):
                load_expert(sp, 2, s)
            with sp.Fori(3, NE) as b:
                for s in range(4):
                    load_expert(sp, b, s, again=True)
                for s in (4, 5):
                    load_expert(sp, b - 1, s, again=True)
            for s in (4, 5):
                load_expert(sp, NE - 1, s)
            sp.wait_ge(plan_done, 2)
            more = sp.value_load(plan[0:1, 7:8], min_val=0, max_val=BLOCKS - NE)
            with sp.If(more > 0):
                with sp.Fori(0, more) as i:
                    e = sp.value_load(plan[0:1, ds(i, 1)], min_val=0, max_val=NE - 1)
                    for s in range(6):
                        load_expert(sp, i + NE, s, expert=e, again=True)
            for n, v in enumerate((ln2_g, ln2_b)):
                sp.dma_start(ln2_gb[:, n, :], v.to_broadcast([P, D])).then_inc(ln2_landed, 16)
            for t in range(TT):
                sp.wait_ge(out_ready, t + 1)
                sp.dma_start(out2[t * P:(t + 1) * P, :], yg[:, 0, t, :]).then_inc(stored, 16)
            sp.wait_ge(stored, 16 * TT)

        @block.gpsimd
        def _(pool):
            nc.gpsimd.memset(ones[:], 1.0).then_inc(pool_step, 1)
            nc.gpsimd.memset(zero[:], 0.0).then_inc(pool_step, 1)
            nc.gpsimd.iota(iota_e[:], pattern=[[1, NE]], base=0, channel_multiplier=0,
                           allow_small_or_imprecise_dtypes=True).then_inc(pool_step, 1)
            nc.gpsimd.iota(slots[:], pattern=[[1, P]], base=0, channel_multiplier=0,
                           allow_small_or_imprecise_dtypes=True).then_inc(pool_step, 1)
            pool.wait_ge(pool_step, 4)
            nc.gpsimd.affine_select(out=ident[:], in_=ones[:], compare_op=ALU.is_equal, fill=0.0,
                                    base=0, pattern=[[-1, P]], channel_multiplier=1).then_inc(masks, 1)
            nc.gpsimd.affine_select(out=before[:], in_=ones[:], compare_op=ALU.is_gt, fill=0.0,
                                    base=0, pattern=[[1, P]], channel_multiplier=-1).then_inc(masks, 1)
            pool.wait_ge(masks, 2)
            nc.gpsimd.tensor_copy(before_b[:], before[:]).then_inc(masks, 1)
            nc.gpsimd.tensor_copy(ones_b[:], ones[:]).then_inc(masks, 1)
            with pool.Fori(0, BLOCKS) as b:
                pool.wait_ge(tile_done, b + 1)
                pool.dma_start(xs[ds(b * P, P), :], zero[:]).then_inc(zero_done, 16)
            with pool.Fori(0, NE) as b:
                pool.wait_ge(tile_done, b + (BLOCKS + 1 - NE))
                pool.dma_start(ys[ds(b * P + HEAD, P - HEAD), :], zero[HEAD:P, :]).then_inc(zero_done, 16)
            with pool.Fori(NE, BLOCKS) as b:
                pool.dma_start(ys[ds(b * P, P), :], zero[:]).then_inc(zero_done, 16)
            pool.wait_ge(zero_done, ZEROS)
            pool.wait_ge(dest_done, 1)
            for t in range(TT):
                for n in range(2):
                    pool.indirect_dma_start(
                        out=xs, out_offset=bass.IndirectOffsetOnAxis(ap=dest[:, n, t:t + 1], axis=0),
                        in_=x1[:, t, :], in_offset=None).then_inc(scat, 16)
            pool.wait_ge(scat, 16 * 2 * TT)

            def part_of(dram, b, r0, n):
                if isinstance(b, int):
                    return dram[b * P + r0:b * P + r0 + n, :]
                return dram[ds(b * P + r0, n), :]

            def load_rows(b, first=False):
                if not first:
                    pool.wait_ge(xe_t, b)
                    pool.wait_ge(xe_t, 2)
                pool.dma_start(xe[0:HEAD, :], part_of(xs, b, 0, HEAD)).then_inc(xe_landed, 16)
                if first:
                    pool.dma_start(xe[HEAD:P, :], part_of(xs, b, HEAD, P - HEAD)).then_inc(xe_landed, 16)
                    return
                flag = pool.value_load(full[0:1, ds(b, 1)], min_val=0, max_val=1)
                with pool.If(flag > 0):
                    pool.dma_start(xe[HEAD:P, :], part_of(xs, b, HEAD, P - HEAD)).then_inc(xe_landed, 16)
                with pool.If(flag < 1):
                    pool.dma_start(xe[HEAD:HEAD + 1, :], part_of(xs, b, HEAD, 1)).then_inc(xe_landed, 16)

            def store_rest(b):
                pool.wait_ge(y_evac, b * 2 + 2)
                pool.wait_ge(y_evac, 2)
                pool.dma_start(part_of(ys, b, HEAD, 1), yb[HEAD:HEAD + 1, :]).then_inc(y_rest_stored, 16)
                flag = pool.value_load(full[0:1, ds(b, 1)], min_val=0, max_val=1)
                with pool.If(flag > 0):
                    pool.dma_start(part_of(ys, b, HEAD + 1, P - HEAD - 1), yb[HEAD + 1:P, :]
                                   ).then_inc(y_rest_stored, 16)
                with pool.If(flag < 1):
                    pool.dma_start(part_of(ys, b, P - 1, 1), yb[P - 1:P, :]).then_inc(y_rest_stored, 16)

            load_rows(1, first=True)
            pool.wait_ge(plan_done, 2)
            load_rows(2)
            with pool.Fori(3, NE) as b:
                load_rows(b)
                store_rest(b - 3)
            for b in range(NE - 3, NE):
                store_rest(b)
            more = pool.value_load(plan[0:1, 7:8], min_val=0, max_val=BLOCKS - NE)
            with pool.If(more > 0):
                with pool.Fori(0, more) as i:
                    load_rows(i + NE)
                    store_rest(i + NE)
            pool.wait_ge(all_stored, 1)
            for t in range(TT):
                for n in range(2):
                    pool.indirect_dma_start(
                        out=yg[:, n, t, :], out_offset=None, in_=ys,
                        in_offset=bass.IndirectOffsetOnAxis(ap=dest[:, n, t:t + 1], axis=0)
                    ).then_inc(got[t], 16)

        @block.tensor
        def _(pe):
            pe.wait_ge(masks, 2)
            for t in range(TT):
                pe.wait_ge(x_landed[t], 16)
                for k in range(KD):
                    mm = pe.transpose(pairs[t][:, k // 4, (k % 4) * P:(k % 4 + 1) * P],
                                      x1[:, t, k * P:(k + 1) * P], ident[:])
                mm.then_inc(xt_t, 1)
            pe.wait_ge(rows_landed, 16 * 6)
            pe.wait_ge(xt_lo, TT)
            pe.transpose(psB[0][:, 0:NROW], rows[0:NROW, :], ident[0:NROW, 0:NROW]).then_inc(chan_t, 1)

            def product(bank, stat, moving, K, ready=None):
                (s_hi, s_lo), (m_hi, m_lo) = stat, moving
                for k in range(K):
                    if ready is not None:
                        pe.wait_ge(ready, k + 1)
                    pe.matmul(bank, s_hi[:, k, :], m_hi[:, k, :], start=(k == 0), stop=False)
                    pe.matmul(bank, s_hi[:, k, :], m_lo[:, k, :], start=False, stop=False)
                    mm = pe.matmul(bank, s_lo[:, k, :], m_hi[:, k, :], start=False, stop=(k == K - 1))
                return mm

            def tile(N, p, bank, moving, K=KD, ready=None):
                pe.wait_ge(w_lo, N + 1)
                product(bank, (whi[p], wlo[p]), moving, K, ready).then_inc(tile_done, 1)

            def xr(j, p, first=False):
                if not first:
                    pe.wait_ge(xc_done, j - 1)
                tile(j, p, psA[p], (xT_hi, xT_lo))

            def rg(j, p, first=False):
                pe.wait_ge(xc_l, j + 1)
                pe.wait_ge(rgw_lo, j + 1)
                if not first:
                    pe.wait_ge(gate_done, j)
                for n in range(2):
                    pe.matmul(psB[n], rg_hi[p][:, n, :], xc_hi[:], start=True, stop=False)
                    pe.matmul(psB[n], rg_hi[p][:, n, :], xc_lo[:], start=False, stop=False)
                    mm = pe.matmul(psB[n], rg_lo[p][:, n, :], xc_hi[:], start=False, stop=True)
                mm.then_inc(rg_done, 1)

            xr(0, 0, first=True)
            xr(1, 1, first=True)
            pe.wait_ge(chan_ready, 1)
            rg(0, 0, first=True)
            with pe.Fori(1, KR // 2) as i:
                xr(2 * i, 0)
                rg(2 * i - 1, 1)
                xr(2 * i + 1, 1)
                rg(2 * i, 0)
            for m in range(6):
                if m == 1:
                    rg(KR - 1, 1)
                if m == 4:
                    pe.wait_ge(gate_done, KR)
                tile(N_A + m, m % 2, ps6[m], (xT_hi, xT_lo))
            with pe.Fori(1, KD // 2) as i:
                for m in range(6):
                    if m % 3 == 0:
                        pe.wait_ge(u_done, 2 * i + (m // 3 - 1))
                    tile(6 * i + (N_A + m), m % 2, ps6[m], (xT_hi, xT_lo))
            pe.wait_ge(xc_done, KR)
            for N0, bank, moving, read, K in (
                    (N_BA, psA, (u_hi, u_lo), ya_done, KD),
                    (N_YR, psB, (xT_hi, xT_lo), y_sq, KD),
                    (N_GA, psA, (xT_hi, xT_lo), ga_read, KD),
                    (N_GR, psB, (xT_hi, xT_lo), gr_read, KD),
                    (N_BR, psA, (hg_hi, hg_lo), mf_done, KR)):
                if N0 == N_GA:
                    pe.wait_ge(ya_done, KD)
                if N0 == N_GR:
                    pe.wait_ge(hg_done, KR)
                if N0 == N_BR:
                    pe.wait_ge(ga_read, KD)
                    pe.wait_ge(hg_l, KR)
                n = KR if N0 == N_YR else KD
                for p in range(2):
                    tile(N0 + p, p, bank[p], moving, K, ready=u_l if N0 + p == N_BA else None)
                    if N0 + p == N_BA:
                        pe.wait_ge(u_done, KD)
                with pe.Fori(1, n // 2) as i:
                    for p in range(2):
                        pe.wait_ge(read, 2 * i + (p - 1))
                        tile(2 * i + (N0 + p), p, bank[p], moving, K)

            def back(t):
                if t >= 2:
                    pe.wait_ge(res_done, t - 1)
                for k in range(KD):
                    mm = pe.transpose(psC[t % 2][:, k // 4, (k % 4) * P:(k % 4 + 1) * P],
                                      yT[:, k, t * P:(t + 1) * P], ident[:])
                mm.then_inc(y_t, 1)

            def x1_back(t):
                pe.wait_ge(x1_done, t + 1)
                if t == 1:
                    pe.wait_ge(x1T_done, 1)
                for k in range(KD):
                    mm = pe.transpose(back_ps[t][:, k // 4, (k % 4) * P:(k % 4 + 1) * P],
                                      x1[:, t, k * P:(k + 1) * P], ident[:])
                mm.then_inc(x1_t, 1)

            def warm(n, bank=psB[1]):
                for _ in range(n):
                    pe.matmul(bank, ehi[0][:, 0, 0:P], ehi[0][:, 0, :], start=True, stop=True)

            def router(t):
                pe.wait_ge(x1T_done, t + 1)
                for k in range(KD):
                    mm = pe.matmul(psB[0][:, t * NE:(t + 1) * NE], x1T[:, t, k, :], wr[:, k, :],
                                   start=(k == 0), stop=(k == KD - 1))
                mm.then_inc(logit_done, 1)

            pe.wait_ge(gr_read, KD)
            pe.wait_ge(small_landed, 32)
            for h in range(HALVES):
                half = [buf[:, :, h * SH:(h + 1) * SH] for buf in (mg_hi, mg_lo)]
                for j in range(KD):
                    n = h * KD + j
                    if n >= 2:
                        pe.wait_ge(yT_done, n - 1)
                    tile(N_O + n, n % 2, psB[n % 2][:, 0:SH], half, ready=mg_l if n == 0 else None)
                    if n == KD:
                        pe.wait_ge(yT_done, KD)
                        back(0)
                        back(1)
            pe.wait_ge(yT_done, HALVES * KD)
            back(2)
            back(3)
            pe.wait_ge(gu_hi, 1)
            x1_back(0)
            warm(5)
            router(0)
            warm(3)
            x1_back(1)
            warm(5)
            router(1)
            warm(12)
            x1_back(2)
            warm(3)
            x1_back(3)
            router(2)
            warm(2)
            router(3)
            warm(30)
            pe.wait_ge(sel_done, 1)
            pe.wait_ge(masks, 4)
            for t in range(TT):
                for q in range(t):
                    pe.matmul(psB[1][:, t * NE:(t + 1) * NE], ones_b[:], sel[:, q, :],
                              start=(q == 0), stop=False)
                pe.matmul(psB[1][:, t * NE:(t + 1) * NE], before_b[:], sel[:, t, :], start=(t == 0), stop=True)
            for q in range(TT):
                mm = pe.matmul(psB[1][:, TT * NE:(TT + 1) * NE], ones_b[:], sel[:, q, :],
                               start=(q == 0), stop=(q == TT - 1))
            mm.then_inc(pos_done, 1)

            def rows_t(b):
                pe.wait_ge(xe_landed, b * 32)
                pe.wait_ge(xe_l, b)
                for k in range(KD):
                    mm = pe.transpose(psC[0][:, k // 4, (k % 4) * P:(k % 4 + 1) * P],
                                      xe[:, k * P:(k + 1) * P], ident[:])
                mm.then_inc(xe_t, 1)

            def gate_up(b, first=False):
                pe.wait_ge(xe_l, b + 1)
                for s in range(4):
                    if s % 2 == 0 and not first:
                        pe.wait_ge((silu_done, h_done)[s // 2], b)
                    pe.wait_ge(gu_lo, b * 4 + (s + 1))
                    for k in range(4):
                        q = 4 * (s % 2) + k
                        pe.matmul(psA[s // 2], xe_hi[:, q, :], ehi[s][:, k, :], start=(q == 0), stop=False)
                        pe.matmul(psA[s // 2], xe_hi[:, q, :], elo[s][:, k, :], start=False, stop=False)
                        mm = pe.matmul(psA[s // 2], xe_lo[:, q, :], ehi[s][:, k, :], start=False,
                                       stop=(q == KD - 1))
                    mm.then_inc(gu_used, 1)

            def hidden_t(b, first=False):
                pe.wait_ge(h_done, b + 1)
                if not first:
                    pe.wait_ge(h_l, b)
                for k in range(KF):
                    mm = pe.transpose(psC[1][:, 0, k * P:(k + 1) * P], hb[:, k * P:(k + 1) * P], ident[:])
                mm.then_inc(h_t, 1)

            def down(b, first=False):
                pe.wait_ge(h_l, b + 1)
                for s in range(2):
                    if not first:
                        pe.wait_ge(y_evac, b * 2 + (s - 1))
                    pe.wait_ge(d_lo, b * 2 + (s + 1))
                    for k in range(KF):
                        pe.matmul(psB[s], hT_hi[:, k, :], ehi[4 + s][:, k, :], start=(k == 0), stop=False)
                        pe.matmul(psB[s], hT_hi[:, k, :], elo[4 + s][:, k, :], start=False, stop=False)
                        mm = pe.matmul(psB[s], hT_lo[:, k, :], ehi[4 + s][:, k, :], start=False,
                                       stop=(k == KF - 1))
                    mm.then_inc(d_used, 1)

            warm(8, psB[0])
            pe.wait_ge(block0_done, 1)
            for k in range(KD):
                for t in range(TT):
                    mm = pe.matmul(psC[0][:, k // 4, (k % 4) * P:(k % 4 + 1) * P],
                                   x1[:, t, k * P:(k + 1) * P], block0[:, t, :],
                                   start=(t == 0), stop=(t == TT - 1))
            mm.then_inc(xe_t, 1)
            warm(11, psB[0])
            gate_up(0, first=True)
            rows_t(1)
            hidden_t(0, first=True)
            gate_up(1)
            rows_t(2)
            down(0, first=True)
            hidden_t(1)
            with pe.Fori(2, NE - 1) as b:
                gate_up(b)
                rows_t(b + 1)
                down(b - 1)
                hidden_t(b)
            gate_up(NE - 1)
            down(NE - 2)
            hidden_t(NE - 1)
            down(NE - 1)
            pe.wait_ge(plan_done, 2)
            more = pe.value_load(plan[0:1, 7:8], min_val=0, max_val=BLOCKS - NE)
            with pe.If(more > 0):
                with pe.Fori(0, more) as i:
                    rows_t(i + NE)
                    gate_up(i + NE)
                    hidden_t(i + NE)
                    down(i + NE)

            pe.wait_ge(diag_done, 1)
            for t in range(TT):
                if t == TT - 1:
                    pe.wait_ge(y_evac, (more + NE) * 2)
                    warm(18, psB[0])
                for h in range(2):
                    pe.matmul(pairs[t][:, h, :], alpha_i[:], x1[:, t, h * S:(h + 1) * S], start=True, stop=False)
            for t in range(TT):
                pe.wait_ge(got[t], 32)
                for n in range(2):
                    for h in range(2):
                        mm = pe.matmul(pairs[t][:, h, :], diag[:, n, t, :], yg[:, n, t, h * S:(h + 1) * S],
                                       start=False, stop=(n == 1))
                mm.then_inc(sum_done, 1)

        @block.scalar
        def _(act):
            A = nc.scalar.activation

            def hi(N, p, K=KD, first=False):
                n, half = N
                act.wait_ge(w_landed[p], half * 16 + 16)
                if not first:
                    act.wait_ge(tile_done, n - 1)
                A(whi[p][:, 0:K, :], wst[p][:, 0:K, :], ACT.Copy).then_inc(w_hi, 1)

            for t in range(TT):
                act.wait_ge(xt_t, t + 1)
                A(xT_hi[:, :, t * P:(t + 1) * P], pairs[t][:].rearrange("p a (b c) -> p (a b) c", c=P),
                  ACT.Copy).then_inc(xt_hi, 1)
                if t == 2:
                    hi((0, 0), 0, first=True)
            hi((1, 0), 1, first=True)
            act.wait_ge(chan_ready, 1)
            A(decay[:, 1, :], chan[:, C_LAM:C_LAM + KR], ACT.Abs).then_inc(decay_act, 1)
            act.wait_ge(decay_act, 1)
            A(decay[:, 2, :], decay[:, 1, :], ACT.Exp, scale=-1.0).then_inc(decay_act, 1)

            def conv_start(j, p, first=False):
                act.wait_ge(tile_done, j + 1)
                if not first:
                    act.wait_ge(ix_done, j - 1)
                A(xc[p][:], psA[p], ACT.Identity, bias=_col(chan, C_CB, j),
                  scale=_col(chan, C_CR(3, 0), j)).then_inc(xc_start, 1)

            def rg_round(j, p, first=False):
                j, half = j
                act.wait_ge(rg_landed[p], half * 32 + 32)
                if not first:
                    act.wait_ge(rg_done, j - 1)
                A(rg_hi[p][:], rg_st[p][:], ACT.Copy).then_inc(rgw_hi, 1)

            def xc_round(j, p, first=False):
                act.wait_ge(xc_done, j + 1)
                if not first:
                    act.wait_ge(rg_done, j)
                A(xc_hi[:], xc[p][:], ACT.Copy).then_inc(xc_h, 1)

            def sigmoids(j, p, first=False):
                act.wait_ge(rg_done, j + 1)
                if not first:
                    act.wait_ge(ix_done, j - 1)
                A(_tile(zbuf, j), psB[0], ACT.Sigmoid, bias=_col(chan, C_BA, j))
                A(ig[p][:], psB[1], ACT.Sigmoid, bias=_col(chan, C_BX, j)).then_inc(gate_done, 1)

            rg_round((0, 0), 0, first=True)
            rg_round((1, 0), 1, first=True)
            conv_start(0, 0, first=True)
            hi((2, 1), 0)
            xc_round(0, 0, first=True)

            conv_start(1, 1, first=True)
            hi((3, 1), 1)
            sigmoids(0, 0, first=True)
            xc_round(1, 1)
            with act.Fori(1, KR // 2) as i:
                for p in range(2):
                    rg_round((2 * i + p, i), p)
                    conv_start(2 * i + p, p)
                    hi((2 * i + (p + 2), i + 1), p)
                    sigmoids(2 * i + (p - 1), 1 - p)
                    xc_round(2 * i + p, p)
            sigmoids(KR - 1, 1)

            QC = KR * S // 4
            zf = zbuf[:].rearrange("p j s -> p (j s)")
            tf = tbuf[:].rearrange("p j s -> p (j s)")
            act.wait_ge(ix_done, KR)
            with act.Fori(0, KD // 2) as i:
                for q in range(2):
                    j, m = 2 * i + q, 3 * q
                    N = lambda n: (6 * i + (N_A + m + n), 3 * i + (N_A + m + n) // 2)
                    act.wait_ge(tile_done, 6 * i + (N_A + m + 1))
                    act.wait_ge(v_done, j)
                    A(tmp[0][:], ps6[m], ACT.Copy).then_inc(c_read, 1)
                    hi(N(2), m % 2)
                    hi(N(3), (m + 1) % 2)
                    act.wait_ge(v_done, j + 1)
                    act.wait_ge(u_done, j)
                    A(tmp[2][:], tmp[1][:], ACT.Identity, bias=0.0, scale=_col(chan, C_CA(2, 0), j)).then_inc(t_start, 1)
                    if q == 0:
                        A(tf[:, ds(i * QC, QC)], zf[:, ds(i * QC, QC)], ACT.Tanh, scale=-0.5)
                        A(zf[:, ds(i * QC, QC)], zf[:, ds(i * QC, QC)], ACT.Exp).then_inc(a_done, 1)
                    hi(N(4), m % 2)
                    act.wait_ge(u_done, j + 1)
                    A(_tile(u_hi, j), tmp[3][:], ACT.Copy).then_inc(u_h, 1)
            act.wait_ge(zero_done, ZEROS)
            with act.Fori(0, KD // 2) as i:
                for p in range(2):
                    act.wait_ge(tile_done, 2 * i + (N_BA + p + 1))
                    A(_tile(ya, 2 * i + p), psA[p], ACT.Copy).then_inc(ya_done, 1)
                    hi((2 * i + (N_BA + p + 2), i + (N_BA + p + 2) // 2), p)
                    if p == 0:
                        act.wait_ge(a_done, i + 1)
                        A(tf[:, ds(i * QC, QC)], tf[:, ds(i * QC, QC)], ACT.Sqrt).then_inc(sq_done, 1)
            act.wait_ge(bt_done, 4)
            with act.Fori(0, KR // 2) as i:
                for p in range(2):
                    j = 2 * i + p
                    act.wait_ge(tile_done, 2 * i + (N_YR + p + 1))
                    act.wait_ge(hg_done, 2 * i)
                    A(yr[p][:], psB[p], ACT.Copy).then_inc(y_sq, 1)
                    hi((2 * i + (N_YR + p + 2), i + (N_YR + p + 2) // 2), p)
                    act.wait_ge(y_q, j + 1)
                    A(tmp[2][:], tmp[1][:], ACT.Sigmoid, scale=GELU_S * GELU_A).then_inc(y_sig, 1)
            def hg_round(j):
                act.wait_ge(hg_done, j + 1)
                A(_tile(hg_hi, j), _tile(ibuf, j), ACT.Copy).then_inc(hg_h, 1)

            act.wait_ge(hg_done, KR)
            with act.Fori(0, KD // 2) as i:
                for p in range(2):
                    act.wait_ge(tile_done, 2 * i + (N_GA + p + 1))
                    act.wait_ge(m_done, 2 * i + p)
                    A(tmp[6][:], psA[p], ACT.Sigmoid).then_inc(ga_read, 1)
                    hi((2 * i + (N_GA + p + 2), i + (N_GA + p + 2) // 2), p)
                    hg_round(2 * i + p)
            for j in range(KD, KR):
                hg_round(j)

            def gr(i, last):
                for p in range(2):
                    act.wait_ge(tile_done, 2 * i + (N_GR + p + 1))
                    A(_tile(sgr, 2 * i + p), psB[p], ACT.Sigmoid).then_inc(gr_read, 1)
                    hi((2 * i + (N_GR + p + 2), i + (N_GR + p + 2) // 2), p, K=KR if last else KD)

            with act.Fori(0, KD // 2 - 1) as i:
                gr(i, False)
            gr(KD // 2 - 1, True)

            def br(i, last):
                for p in range(2):
                    hi((2 * i + (N_BR + p + 2), i + (N_BR + p + 2) // 2), p, K=KD if last else KR)
                    act.wait_ge(mf_done, 2 * i + (p + 1))
                    A(_tile(mg_hi, 2 * i + p), tmp[1][:], ACT.Copy).then_inc(mg_h, 1)

            with act.Fori(0, KD // 2 - 1) as i:
                br(i, False)
            br(KD // 2 - 1, True)

            def e_round(b, s, first=False):
                act.wait_ge(e_landed[s], b * 16 + 16)
                if not first:
                    if s < 4:
                        act.wait_ge(gu_used, b * 4 + (s - 3))
                    else:
                        act.wait_ge(d_used, b * 2 + (s - 5))
                A(ehi[s][:], est[s][:], ACT.Copy).then_inc(gu_hi if s < 4 else d_hi, 1)

            def e_round_part(s, part):
                act.wait_ge(e_landed[s], 16)
                h = slice(2 * part, 2 * part + 2)
                ins = A(ehi[s][:, h, :], est[s][:, h, :], ACT.Copy)
                if part == 1:
                    ins.then_inc(gu_hi, 1)

            act.wait_ge(mg_l, KD)

            def x1_copy(t):
                act.wait_ge(x1_t, t + 1)
                A(x1T[:, t], back_ps[t][:].rearrange("p a (k c) -> p (a k) c", c=P), ACT.Copy).then_inc(x1T_done, 1)

            for n in range(HALVES * KD):
                N, h, j = N_O + n, n // KD, n % KD
                act.wait_ge(tile_done, N + 1)
                if N + 2 < N_END:
                    q = (n + 2) % 3
                    act.wait_ge(w_landed[q], ((N_O // 2 if q < 2 else 0) + (n + 2) // 3 + 1) * 16)
                    A(whi[n % 2][:, 0:KD, :], wst[q][:, 0:KD, :], ACT.Copy).then_inc(w_hi, 1)
                A(yT[:, j, h * SH:(h + 1) * SH], psB[n % 2][:, 0:SH], ACT.Copy).then_inc(yT_done, 1)
                for s, at_n in enumerate((0, 2, 7, 10)):
                    if n in (at_n, at_n + 1):
                        e_round_part(s, n - at_n)
                if n == 13:
                    _std(act, 0, var_done, std_done, stat, 0, 2)
            act.wait_ge(mg_l, KD)
            act.wait_ge(tile_done, N_END)
            x1_copy(0)
            x1_copy(1)
            _std(act, 1, var_done, std_done, stat, 0, 2)
            e_round(0, 4, first=True)
            act.wait_ge(y_t, TT)
            e_round(0, 5, first=True)
            x1_copy(2)
            x1_copy(3)
            act.wait_ge(lmax_done, 1)
            A(r16[1][:], r16[0][:], ACT.Exp).then_inc(exp_done, 1)

            def rows_round(b, first=False):
                act.wait_ge(xe_t, b + 1)
                if not first:
                    act.wait_ge(gu_used, b * 4)
                A(xe_hi[:], psC[0][:].rearrange("p a (k c) -> p (a k) c", c=P), ACT.Copy).then_inc(xe_h, 1)

            def silu(b, first=False):
                act.wait_ge(gu_used, b * 4 + 2)
                if not first:
                    act.wait_ge(h_done, b)
                A(sg[:], psA[0], ACT.Silu).then_inc(silu_done, 1)

            def hidden_round(b, first=False):
                act.wait_ge(h_t, b + 1)
                if not first:
                    act.wait_ge(d_used, b * 2)
                A(hT_hi[:], psC[1][:, 0, :].rearrange("p (k c) -> p k c", c=P), ACT.Copy).then_inc(h_h, 1)

            def y_out(b, s, first=False):
                act.wait_ge(d_used, b * 2 + (s + 1))
                if not first:
                    act.wait_ge(y_stored, b * 32)
                    act.wait_ge(y_rest_stored, b * 32)
                A(yb[:, s * DF:(s + 1) * DF], psB[s], ACT.Copy).then_inc(y_evac, 1)
                dst = ys[b * P:(b + 1) * P, :] if isinstance(b, int) else ys[ds(act.snap(b * P), P), :]
                act.wait_ge(y_evac, b * 2 + (s + 1))
                act.dma_start(dst[0:HEAD, s * DF:(s + 1) * DF], yb[0:HEAD, s * DF:(s + 1) * DF]
                              ).then_inc(y_stored, 16)

            rows_round(0, first=True)

            def turn(b, prev=True, first=False, first_prev=False):
                e_round(b + 1, 0)
                e_round(b + 1, 1)
                silu(b, first)
                rows_round(b + 1)
                e_round(b + 1, 2)
                e_round(b + 1, 3)
                for s in range(2):
                    if prev:
                        e_round(b, 4 + s)
                        y_out(b - 1, s, first_prev)
                hidden_round(b, first)

            turn(0, prev=False, first=True)
            turn(1, first_prev=True)
            with act.Fori(2, NE - 1) as b:
                turn(b)
            silu(NE - 1)
            e_round(NE - 1, 4)
            y_out(NE - 2, 0)
            hidden_round(NE - 1)
            e_round(NE - 1, 5)
            y_out(NE - 2, 1)
            for s in range(2):
                y_out(NE - 1, s)
            act.wait_ge(plan_done, 2)
            more = act.value_load(plan[0:1, 7:8], min_val=0, max_val=BLOCKS - NE)
            with act.If(more > 0):
                with act.Fori(0, more) as i:
                    b = i + NE
                    for s in range(4):
                        e_round(b, s)
                    rows_round(b)
                    silu(b)
                    for s in range(2):
                        e_round(b, 4 + s)
                    hidden_round(b)
                    for s in range(2):
                        y_out(b, s)
            act.wait_ge(y_stored, (more + NE) * 32)
            act.wait_ge(y_rest_stored, (more + NE) * 32)
            A(stat[:, 40:41], stat[:, 30:31], ACT.Copy).then_inc(all_stored, 1)
            for t in range(TT):
                _std(act, 2 + t, var_done, std_done, stat, t % 2, 1)

        @block.vector
        def _(dve):
            V = nc.vector
            chain = Chain(dve, dve_step)

            def lo(N, p, K=KD):
                dve.wait_ge(w_hi, N + 1)
                V.tensor_tensor(wlo[p][:, 0:K, :], wst[p][:, 0:K, :], whi[p][:, 0:K, :],
                                ALU.subtract).then_inc(w_lo, 1)

            for t in range(TT):
                dve.wait_ge(xt_hi, t + 1)
                V.tensor_tensor(xT_lo[:, :, t * P:(t + 1) * P],
                                pairs[t][:].rearrange("p a (b c) -> p (a b) c", c=P),
                                xT_hi[:, :, t * P:(t + 1) * P], ALU.subtract).then_inc(xt_lo, 1)
                if t == 2:
                    lo(0, 0)
            dve.wait_ge(chan_t, 1)
            V.tensor_copy(chan[:, 0:NROW], psB[0][:, 0:NROW]).then_inc(chan_ready, 1)
            lo(1, 1)
            dve.wait_ge(decay_act, 2)
            e, s1, s2, acc = (decay[:, n, :] for n in (2, 3, 4, 5))
            chain.link(V.tensor_scalar(acc, e, 2.0, None, ALU.add))
            chain.link(V.reciprocal(s1, acc))
            chain.link(V.tensor_tensor(s1, s1, e, ALU.mult))
            chain.link(V.tensor_tensor(s2, s1, s1, ALU.mult))
            TERMS = 8
            chain.link(V.tensor_scalar(acc, s2, 1.0 / (2 * TERMS + 1), 1.0 / (2 * TERMS - 1), ALU.mult, ALU.add))
            for n in range(TERMS - 2, -1, -1):
                chain.link(V.tensor_tensor(acc, acc, s2, ALU.mult))
                chain.link(V.tensor_scalar(acc, acc, 1.0 / (2 * n + 1), None, ALU.add))
            chain.link(V.tensor_tensor(acc, acc, s1, ALU.mult))
            chain.link(V.tensor_scalar(s2, chan[:, C_LAM:C_LAM + KR], -1.0, 0.0, ALU.mult, ALU.max))
            chain.link(V.scalar_tensor_tensor(acc, acc, 2.0, s2, ALU.mult, ALU.add))
            chain.link(V.tensor_scalar(decay[:, 0, :], acc, -8.0, None, ALU.mult))

            def rg_rest(j, p):
                dve.wait_ge(rgw_hi, j + 1)
                V.tensor_tensor(rg_lo[p][:], rg_st[p][:], rg_hi[p][:], ALU.subtract).then_inc(rgw_lo, 1)

            def conv_rest(j, p):
                dve.wait_ge(xc_start, j + 1)
                for k in (2, 1, 0):
                    d = 3 - k
                    ins = V.scalar_tensor_tensor(xc[p][:, d:S], psA[p][:, 0:S - d], _col(chan, C_CR(k, 0), j),
                                                 xc[p][:, d:S], ALU.mult, ALU.add)
                    if k:
                        chain.link(ins)
                ins.then_inc(xc_done, 1)

            def xc_rest(j, p):
                dve.wait_ge(xc_h, j + 1)
                V.tensor_tensor(xc_lo[:], xc[p][:], xc_hi[:], ALU.subtract).then_inc(xc_l, 1)

            def gates_of(j, p):
                dve.wait_ge(gate_done, j + 1)
                V.tensor_scalar(_tile(zbuf, j), _tile(zbuf, j), _col(decay[:, 0, :], 0, j), None, ALU.mult)
                V.tensor_tensor(_tile(ibuf, j), ig[p][:], xc[p][:], ALU.mult).then_inc(ix_done, 1)

            rg_rest(0, 0)
            rg_rest(1, 1)
            conv_rest(0, 0)
            lo(2, 0)
            xc_rest(0, 0)
            conv_rest(1, 1)
            lo(3, 1)
            xc_rest(1, 1)
            gates_of(0, 0)

            start = chain.n
            with dve.Fori(1, KR // 2) as i:
                chain.n = i * 4 + (start - 4)
                for p in range(2):
                    rg_rest(2 * i + p, p)
                    conv_rest(2 * i + p, p)
                    lo(2 * i + (p + 2), p)
                    xc_rest(2 * i + p, p)
                    gates_of(2 * i + (p - 1), 1 - p)
            chain.n = start + 4 * (KR // 2 - 1)
            gates_of(KR - 1, 1)

            QC = KR * S // 4
            zf = zbuf[:].rearrange("p j s -> p (j s)")
            tf = tbuf[:].rearrange("p j s -> p (j s)")
            xf = ibuf[:].rearrange("p j s -> p (j s)")

            def gated_conv(i):
                for q in range(2):
                    j, m = 2 * i + q, 3 * q
                    N = 6 * i + (N_A + m)
                    lo(N + 2, m % 2)
                    dve.wait_ge(c_read, j + 1)
                    dve.wait_ge(tile_done, N + 2)
                    dve.wait_ge(t_start, j)
                    V.tensor_tensor(tmp[1][:], tmp[0][:], ps6[m + 1], ALU.mult).then_inc(v_done, 1)
                    lo(N + 3, (m + 1) % 2)
                    dve.wait_ge(t_start, j + 1)
                    for k in (1, 0):
                        d = 2 - k
                        chain.link(V.scalar_tensor_tensor(tmp[2][:, d:S], tmp[1][:, 0:S - d],
                                                          _col(chan, C_CA(k, 0), j), tmp[2][:, d:S],
                                                          ALU.mult, ALU.add))
                    dve.wait_ge(tile_done, N + 3)
                    dve.wait_ge(u_h, j)
                    V.tensor_tensor(tmp[3][:], tmp[2][:], ps6[m + 2], ALU.mult).then_inc(u_done, 1)
                    lo(N + 4, m % 2)
                    dve.wait_ge(u_h, j + 1)
                    V.tensor_tensor(_tile(u_lo, j), tmp[3][:], _tile(u_hi, j), ALU.subtract).then_inc(u_l, 1)

            chain.loop(KD // 2, gated_conv, 4)

            def branch_a(i):
                for p in range(2):
                    lo(2 * i + (N_BA + p + 2), p)
                    if p == 0:
                        dve.wait_ge(sq_done, i + 1)
                        q = ds(i * QC, QC)
                        chain.link(V.scalar_tensor_tensor(tf[:, q], zf[:, q], 1.0, tf[:, q], ALU.add, ALU.mult))
                        V.tensor_tensor(xf[:, q], xf[:, q], tf[:, q], ALU.mult).then_inc(bt_done, 1)

            chain.loop(KD // 2, branch_a, 1)
            dve.wait_ge(bt_done, 4)

            def gelu_r(i):
                for p in range(2):
                    j = 2 * i + p
                    chain.link(V.tensor_tensor_scan(_tile(zbuf, j), _tile(zbuf, j), _tile(ibuf, j), 0.0,
                                                    ALU.mult, ALU.add))
                    dve.wait_ge(y_sq, j + 1)
                    chain.link(V.tensor_tensor(tmp[5][:], yr[p][:], yr[p][:], ALU.mult))
                    dve.wait_ge(y_sig, j)
                    V.scalar_tensor_tensor(tmp[1][:], tmp[5][:], 1.0 / GELU_A, yr[p][:],
                                           ALU.add, ALU.mult).then_inc(y_q, 1)
                    lo(2 * i + (N_YR + p + 2), p)
                    chain.link(V.tensor_tensor(tmp[3][:], _tile(zbuf, j), yr[p][:], ALU.mult))
                    dve.wait_ge(y_sig, j + 1)
                    V.tensor_tensor(_tile(ibuf, j), tmp[3][:], tmp[2][:], ALU.mult).then_inc(hg_done, 1)

            chain.loop(KR // 2, gelu_r, 6)

            def hg_rest(j):
                dve.wait_ge(hg_h, j + 1)
                V.tensor_tensor(_tile(hg_lo, j), _tile(ibuf, j), _tile(hg_hi, j), ALU.subtract).then_inc(hg_l, 1)

            with dve.Fori(0, KD // 2) as i:
                for p in range(2):
                    j = 2 * i + p
                    dve.wait_ge(ga_read, j + 1)
                    V.tensor_tensor(_tile(ya, j), _tile(ya, j), tmp[6][:], ALU.mult).then_inc(m_done, 1)
                    lo(2 * i + (N_GA + p + 2), p)
                    hg_rest(2 * i + p)
            for j in range(KD, KR):
                hg_rest(j)

            def gr(i, last):
                for p in range(2):
                    lo(2 * i + (N_GR + p + 2), p, K=KR if last else KD)

            with dve.Fori(0, KD // 2 - 1) as i:
                gr(i, False)
            gr(KD // 2 - 1, True)
            dve.wait_ge(gr_read, KD)
            dve.wait_ge(m_done, KD)

            def br(i, last):
                for p in range(2):
                    j = 2 * i + p
                    N = 2 * i + (N_BR + p)
                    dve.wait_ge(tile_done, N + 1)
                    chain.link(V.tensor_tensor(tmp[0][:], _tile(sgr, j), psA[p], ALU.mult))
                    dve.wait_ge(mg_h, j)
                    V.tensor_tensor(tmp[1][:], tmp[0][:], _tile(ya, j), ALU.add).then_inc(mf_done, 1)
                    if not (last and p):
                        lo(N + 2, p, K=KD if last else KR)
                    dve.wait_ge(mg_h, j + 1)
                    V.tensor_tensor(_tile(mg_lo, j), tmp[1][:], _tile(mg_hi, j), ALU.subtract).then_inc(mg_l, 1)
            
            chain.loop(KD // 2 - 1, lambda i: br(i, False), 2)
            br(KD // 2 - 1, True)
            lo(N_O + 1, 1)

            def e_rest(b, s):
                if s < 4:
                    dve.wait_ge(gu_hi, b * 4 + (s + 1))
                else:
                    dve.wait_ge(d_hi, b * 2 + (s - 3))
                V.tensor_tensor(elo[s][:], est[s][:], ehi[s][:], ALU.subtract).then_inc(gu_lo if s < 4 else d_lo, 1)

            def e_rest_part(s, part):
                dve.wait_ge(gu_hi, s + 1)
                h = slice(2 * part, 2 * part + 2)
                ins = V.tensor_tensor(elo[s][:, h, :], est[s][:, h, :], ehi[s][:, h, :], ALU.subtract)
                if part == 1:
                    ins.then_inc(gu_lo, 1)

            def residual(t):
                dve.wait_ge(y_t, t + 1)
                for h in range(2):
                    ins = V.scalar_tensor_tensor(x1[:, t, h * S:(h + 1) * S], x1[:, t, h * S:(h + 1) * S],
                                                 ALPHA, psC[t % 2][:, h, :], ALU.mult, ALU.add)
                ins.then_inc(res_done, 1)

            def moments(halves, u):
                for h, half in enumerate(halves):
                    V.bn_stats(stat[:, 12 * u + 6 * h:12 * u + 6 * h + 6], half).then_inc(stats_done, 1)

            def variance(u, n, count):
                dve.wait_ge(stats_done, count)
                for v in range(u, u + n):
                    ins = V.bn_aggr(stat[:, 24 + 2 * v:26 + 2 * v],
                                    stat[:, 12 * v:12 * v + 12].rearrange("p (a c) -> p a c", c=6))
                chain.link(ins)
                for v in range(u, u + n):
                    ins = V.tensor_scalar(stat[:, 28 + v:29 + v], stat[:, 25 + 2 * v:26 + 2 * v], LN_EPS, 0.25,
                                          ALU.add, ALU.mult)
                ins.then_inc(var_done, 1)

            def rstd(u, n, count):
                dve.wait_ge(std_done, count)
                chain.link(V.reciprocal(stat[:, 32 + u:32 + u + n], stat[:, 30 + u:30 + u + n]))
                for v in range(u, u + n):
                    ins = V.scalar_tensor_tensor(stat[:, 34 + v:35 + v], stat[:, 32 + v:33 + v],
                                                 stat[:, 28 + v:29 + v], stat[:, 30 + v:31 + v],
                                                 ALU.mult, ALU.add)
                chain.link(ins)
                chain.link(V.reciprocal(stat[:, 38 + u:38 + u + n], stat[:, 34 + u:34 + u + n]))

            def scale_rows(row, src, u, gb, done):
                chain.link(V.scalar_tensor_tensor(row, src, stat[:, 24 + 2 * u:25 + 2 * u], gb[:, 0, :],
                                                  ALU.subtract, ALU.mult))
                V.scalar_tensor_tensor(row, row, stat[:, 38 + u:39 + u], gb[:, 1, :],
                                       ALU.mult, ALU.add).then_inc(done, 1)

            for n in range(HALVES * KD):
                if N_O + n + 2 < N_END:
                    dve.wait_ge(w_hi, N_O + n + 3)
                    V.tensor_tensor(wlo[n % 2][:, 0:KD, :], wst[(n + 2) % 3][:, 0:KD, :],
                                    whi[n % 2][:, 0:KD, :], ALU.subtract).then_inc(w_lo, 1)
                if n in (3, 4, 5, 6):
                    e_rest_part((n - 3) // 2, (n - 3) % 2)
                if n in (9, 10):
                    residual(n - 9)
                if n in (11, 12):
                    dve.wait_ge(res_done, n - 10)
                    moments(_halves(x1[:, n - 11, :], S), n - 11)
                if n == 12:
                    variance(0, 2, 4)
            dve.wait_ge(ln1_landed, 32)
            rstd(0, 2, 1)
            for u in range(2):
                scale_rows(x1[:, u, :], x1[:, u, :], u, ln1_gb, x1_done)
            for u in range(2):
                residual(2 + u)
                dve.wait_ge(res_done, 3 + u)
                moments(_halves(x1[:, 2 + u, :], S), u)
            variance(0, 2, 8)
            rstd(0, 2, 2)
            for u in range(2):
                scale_rows(x1[:, 2 + u, :], x1[:, 2 + u, :], u, ln1_gb, x1_done)
            dve.wait_ge(x1_done, TT)
            for s in (2, 3, 4):
                e_rest(0, s)
            dve.wait_ge(small_landed, 32)

            def b16(v):
                return v[:].unsqueeze(2).to_broadcast([P, TT, NE])

            def tt(o, a, b, op):
                chain.link(V.tensor_tensor(o, a, b, op))

            def red(o, a, op):
                chain.link(V.tensor_reduce(o, a, AX, op))

            k0, key = r1[3], r1[4]
            ex, iota3 = r16[1], iota_e[:].unsqueeze(1).to_broadcast([P, TT, NE])
            dve.wait_ge(logit_done, TT)
            tt(r16[0][:], psB[0][:, 0:TT * NE].rearrange("p (t e) -> p t e", e=NE),
               brow[:].unsqueeze(1).to_broadcast([P, TT, NE]), ALU.add)
            red(r1[0][:], r16[0][:], ALU.max)
            V.tensor_tensor(r16[0][:], r16[0][:], b16(r1[0]), ALU.subtract).then_inc(lmax_done, 1)
            dve.wait_ge(exp_done, 1)
            red(r1[1][:], ex[:], ALU.add)
            chain.link(V.reciprocal(r1[2][:], r1[1][:]))
            pr = r16[2]
            tt(pr[:], ex[:], b16(r1[2]), ALU.mult)
            g4 = pr[:].rearrange("p t (g e) -> p t g e", e=GRP)
            score = r4[0]
            V.tensor_tensor(r6[:, :, :, 0:3], g4[:, :, :, 0:3], g4[:, :, :, 1:4], ALU.add)
            V.tensor_tensor(r6[:, :, :, 3:5], g4[:, :, :, 0:2], g4[:, :, :, 2:4], ALU.add)
            tt(r6[:, :, :, 5:6], g4[:, :, :, 0:1], g4[:, :, :, 3:4], ALU.add)
            red(score[:], r6[:], ALU.max)

            def first_of(o, idx, vals, width, best, scratch):
                bb = best[:].unsqueeze(2).to_broadcast([P, TT, width])
                it = iota_e[:, 0:width].unsqueeze(1).to_broadcast([P, TT, width])
                tt(scratch, vals, bb, ALU.is_lt)
                chain.link(V.scalar_tensor_tensor(scratch, scratch, 99.0, it, ALU.mult, ALU.add))
                red(idx[:], scratch, ALU.min)
                tt(o, it, idx[:].unsqueeze(2).to_broadcast([P, TT, width]), ALU.is_equal)

            red(r1[3][:], score[:], ALU.max)
            first_of(r4[2][:], r1[4], score[:], NG, r1[3], r4[3][:])
            pm, pw = r16[3], r16[4]
            gm = r4[2][:].unsqueeze(3).to_broadcast([P, TT, NG, GRP])
            V.tensor_scalar(r4[4][:], r4[2][:], -1.0, None, ALU.add)
            tt(pw[:].rearrange("p t (g e) -> p t g e", e=GRP), g4, gm, ALU.mult)
            tt(pm[:].rearrange("p t (g e) -> p t g e", e=GRP), pw[:].rearrange("p t (g e) -> p t g e", e=GRP),
               r4[4][:].unsqueeze(3).to_broadcast([P, TT, NG, GRP]), ALU.add)
            red(r1[5][:], pm[:], ALU.max)
            oh1, oh2 = (onehot[:, n] for n in range(2))
            first_of(oh1, r1[6], pm[:], NE, r1[5], chosen[:, 0])
            chain.link(V.scalar_tensor_tensor(pm[:], oh1, -4.0, pm[:], ALU.mult, ALU.add))
            red(r1[7][:], pm[:], ALU.max)
            first_of(oh2, r1[8], pm[:], NE, r1[7], chosen[:, 0])
            V.tensor_tensor(sel[:], oh1, oh2, ALU.add).then_inc(sel_done, 1)
            tt(r1[9][:], r1[5][:], r1[7][:], ALU.add)
            chain.link(V.reciprocal(r1[10][:], r1[9][:]))
            V.tensor_tensor(gates[:, 0, :], r1[5][:], r1[10][:], ALU.mult)
            tt(gates[:, 1, :], r1[7][:], r1[10][:], ALU.mult)
            V.tensor_tensor(k0[:], oh1[:, :, 0], oh2[:, :, 0], ALU.add).then_inc(picked0, 1)
            dve.wait_ge(pos_done, 1)
            dve.wait_ge(sel_done, 1)
            cnt, ext, inc, bb = (r16[n][:, 0, :] for n in (9, 10, 11, 12))
            pos, row = r16[13], r16[14]
            V.tensor_copy(pos[:], psB[1][:, 0:TT * NE].rearrange("p (t e) -> p t e", e=NE))
            dve.wait_ge(picked0, 1)
            V.tensor_scalar(key[:], k0[:], -1000.0, 1000.0, ALU.mult, ALU.add)
            chain.link(V.tensor_copy(cnt, psB[1][:, TT * NE:(TT + 1) * NE]))
            tt(key[:], key[:], pos[:, :, 0], ALU.add)
            for t in range(TT):
                ins = V.tensor_scalar(block0[:, t, :], slots[:], key[:, t:t + 1], None, ALU.is_equal)
            ins.then_inc(block0_done, 1)
            chain.link(V.tensor_scalar(ext, cnt, float(P), None, ALU.is_gt))
            for n in range(2, TT):
                chain.link(V.scalar_tensor_tensor(ext, cnt, float(n * P), ext, ALU.is_gt, ALU.add))
            chain.link(V.tensor_tensor_scan(inc, ones[:, 0:NE], ext, 0.0, ALU.mult, ALU.add))
            tt(bb, inc, ext, ALU.subtract)
            tt(bb, bb, iota_e[:], ALU.subtract)
            V.tensor_scalar(row[:], pos[:], float(P), None, ALU.is_ge)
            chain.link(V.tensor_scalar(bb, bb, float(P), float((NE - 1) * P), ALU.mult, ALU.add))
            tt(row[:], row[:], bb.unsqueeze(1).to_broadcast([P, TT, NE]), ALU.mult)
            tt(row[:], row[:], pos[:], ALU.add)
            chain.link(V.scalar_tensor_tensor(row[:], iota3, float(P), row[:], ALU.mult, ALU.add))
            for n in range(2):
                ins = V.tensor_tensor(chosen[:, n], onehot[:, n], row[:], ALU.mult)
            chain.link(ins)
            red(rowsum[:], chosen[:], ALU.add)
            V.tensor_copy(dest[:], rowsum[:]).then_inc(dest_done, 1)
            more_n = BLOCKS - NE
            below, owner = chosen[:].rearrange("p a t e -> p (a t) e")[:, 0:more_n], rowsum[:].rearrange("p a t -> p (a t)")[:, 0:more_n]
            dve.wait_ge(dest_done, 1)
            tt(below, inc.unsqueeze(1).to_broadcast([P, more_n, NE]),
               iota_e[:, 0:more_n].unsqueeze(2).to_broadcast([P, more_n, NE]), ALU.is_le)
            red(owner, below, ALU.add)
            chain.link(V.tensor_scalar(owner, owner, float(NE - 1), None, ALU.min))
            chain.link(V.tensor_copy(plan[:, 0:more_n], owner))
            chain.link(V.memset(full[:], 1))
            V.tensor_scalar(full[:, 0:NE], cnt, float(HEAD), None, ALU.is_gt).then_inc(plan_done, 1)
            V.tensor_copy(plan[:, 7:8], inc[:, NE - 1:NE]).then_inc(plan_done, 1)

            e_rest(0, 5)

            def rows_rest(b):
                dve.wait_ge(xe_h, b + 1)
                V.tensor_tensor(xe_lo[:], psC[0][:].rearrange("p a (k c) -> p (a k) c", c=P), xe_hi[:],
                                ALU.subtract).then_inc(xe_l, 1)

            def hidden(b, first=False):
                dve.wait_ge(silu_done, b + 1)
                dve.wait_ge(gu_used, b * 4 + 4)
                if not first:
                    dve.wait_ge(h_t, b)
                V.tensor_tensor(hb[:], sg[:], psA[1], ALU.mult).then_inc(h_done, 1)

            def hidden_rest(b):
                dve.wait_ge(h_h, b + 1)
                V.tensor_tensor(hT_lo[:], psC[1][:, 0, :].rearrange("p (k c) -> p k c", c=P), hT_hi[:],
                                ALU.subtract).then_inc(h_l, 1)

            rows_rest(0)

            def turn(b, prev=True, first=False):
                e_rest(b + 1, 0)
                e_rest(b + 1, 1)
                hidden(b, first)
                rows_rest(b + 1)
                e_rest(b + 1, 2)
                e_rest(b + 1, 3)
                if prev:
                    e_rest(b, 4)
                    e_rest(b, 5)
                hidden_rest(b)

            turn(0, prev=False, first=True)
            with dve.Fori(1, NE - 1) as b:
                turn(b)
            hidden(NE - 1)
            e_rest(NE - 1, 4)
            hidden_rest(NE - 1)
            e_rest(NE - 1, 5)
            dve.wait_ge(plan_done, 2)
            more = dve.value_load(plan[0:1, 7:8], min_val=0, max_val=BLOCKS - NE)
            with dve.If(more > 0):
                with dve.Fori(0, more) as i:
                    b = i + NE
                    for s in range(4):
                        e_rest(b, s)
                    rows_rest(b)
                    hidden(b)
                    e_rest(b, 4)
                    e_rest(b, 5)
                    hidden_rest(b)

            for t in range(TT):
                for n in range(2):
                    V.tensor_scalar(diag[:, n, t, :], ident[:], gates[:, n, t:t + 1], None, ALU.mult)
            V.tensor_scalar(alpha_i[:], ident[:], ALPHA, None, ALU.mult).then_inc(diag_done, 1)
            dve.wait_ge(ln2_landed, 32)

            def summed(t):
                dve.wait_ge(sum_done, t + 1)
                moments([pairs[t][:, h, :] for h in range(2)], t % 2)
                variance(t % 2, 1, 2 * TT + 2 * t + 2)

            summed(0)
            for t in range(TT):
                if t + 1 < TT:
                    summed(t + 1)
                rstd(t % 2, 1, 3 + t)
                scale_rows(yg[:, 0, t, :], pairs[t][:].rearrange("p a s -> p (a s)"), t % 2, ln2_gb, out_ready)


def _halves(row, S):
    return [row[:, h * S:(h + 1) * S] for h in range(2)]


def _std(act, count, var_done, std_done, stat, u, n):
    act.wait_ge(var_done, count + 1)
    act.activation(stat[:, 30 + u:30 + u + n], stat[:, 28 + u:28 + u + n], ACT.Sqrt).then_inc(std_done, 1)


def _tile(buf, j):
    if isinstance(j, int):
        return buf[:, j, :]
    return buf[:, ds(j, 1), :].rearrange("p a s -> p (a s)")


def _col(buf, c0, j):
    if isinstance(j, int):
        return buf[:, c0 + j:c0 + j + 1]
    return buf[:, ds(j + c0, 1)]


_INS = ["x", "w_in", "conv_a_w", "w_branch_a", "conv_r_w", "conv_r_b", "w_rg_a", "b_rg_a", "w_rg_x",
        "b_rg_x", "rg_lambda", "w_branch_r", "w_out", "ln1_g", "ln1_b", "w_router", "b_router",
        "w_exp_gate", "w_exp_up", "w_exp_down", "ln2_g", "ln2_b"]


def kernel(**inputs):
    import numpy as _np
    import concourse.bacc as _bacc
    from concourse import mybir as _mybir
    from concourse.bass_utils import run_bass_kernel_spmd as _run

    nc = _bacc.Bacc("TRN2", target_bir_lowering=False, num_devices=1)
    arrays, args = {}, []
    for name in _INS:
        a = _np.ascontiguousarray(inputs[name])
        arrays[f"in_{name}_dram"] = a
        args.append(nc.dram_tensor(f"in_{name}_dram", a.shape, _mybir.dt.from_np(a.dtype), kind="ExternalInput").ap())
    shape = inputs["x"].shape
    args.append(nc.dram_tensor("out_dram", shape, _mybir.dt.float32, kind="ExternalOutput").ap())
    trunk_moe(nc, *args)
    r = _run(nc, [arrays], core_ids=[0])
    return r.results[0]["out_dram"]
```
